# Optimizing a Trainium2 kernel written in Bass

```python
import math
import jax, jax.numpy as jnp
from jax import lax
import numpy as np

D_MODEL = 1024
BATCH = 1
SEQ = 256
DEPTH = 1

D_MIX = D_MODEL
N_GROUPS = 4
GROUP_W = D_MIX // N_GROUPS

A_HEADS = 4
A_QK_DIM = GROUP_W // A_HEADS // 2
A_V_DIM = 2 * A_QK_DIM

B_HEADS = 4
B_HEAD_DIM = GROUP_W // B_HEADS
MOBA_BLOCK = 256
MOBA_TOPK = 3

C_HEADS = 4
C_V_DIM = GROUP_W // C_HEADS
C_K_DIM = C_V_DIM // 2
GLA_RANK = 16
GLA_TAU = 16.0
GLA_CHUNK = 64

D_WIDTH = GROUP_W
D_BLOCKS = 4
D_BLOCK_DIM = D_WIDTH // D_BLOCKS
CONV_W = 4
LRU_C = 8.0

N_EXPERTS = 32
TOP_K = 4
D_FF = D_MODEL
SWIGLU_ALPHA = 1.702
SWIGLU_LIMIT = 7.0
MOE_BLOCK = 128

Q_BLOCK = 128
EPS = 1e-6

A_Q = A_HEADS * 2 * A_QK_DIM
A_K = A_HEADS * 2 * A_QK_DIM
A_V = A_HEADS * A_V_DIM
B_Q = GROUP_W
B_K = GROUP_W
B_V = GROUP_W
C_Q = C_HEADS * C_K_DIM
C_K = C_HEADS * C_K_DIM
C_V = C_HEADS * C_V_DIM
C_G = GLA_RANK
C_R = C_HEADS * C_V_DIM
D_X = D_WIDTH
D_G = D_WIDTH
D_IN = A_Q + A_K + A_V + B_Q + B_K + B_V + C_Q + C_K + C_V + C_G + C_R + D_X + D_G


def rms_norm(x, gain):
    xf = x.astype(jnp.float32)
    y = xf * lax.rsqrt(jnp.mean(xf * xf, axis=-1, keepdims=True) + EPS)
    return (y * gain.astype(jnp.float32)).astype(x.dtype)

def to_heads(t, n):
    b, s, f = t.shape
    return t.reshape(b, s, n, f // n).transpose(0, 2, 1, 3)

def merge_heads(t):
    b, h, s, d = t.shape
    return t.transpose(0, 2, 1, 3).reshape(b, s, h * d)

def split_columns(proj):
    sizes = (A_Q, A_K, A_V, B_Q, B_K, B_V, C_Q, C_K, C_V, C_G, C_R, D_X, D_G)
    out, off = [], 0
    for sz in sizes:
        out.append(proj[..., off:off + sz])
        off += sz
    return out

def diff_attention(q, k, v, q_gain, k_gain, lam_q1, lam_k1, lam_q2, lam_k2, out_gain, layer_idx):
    bsz, s, _ = q.shape
    q = rms_norm(q.reshape(bsz, s, A_HEADS, 2, A_QK_DIM), q_gain).transpose(0, 2, 3, 1, 4)
    k = rms_norm(k.reshape(bsz, s, A_HEADS, 2, A_QK_DIM), k_gain).transpose(0, 2, 3, 1, 4)
    v = to_heads(v, A_HEADS)
    lam_init = 0.8 - 0.6 * math.exp(-0.3 * layer_idx)
    lam = (jnp.exp(jnp.sum(lam_q1.astype(jnp.float32) * lam_k1.astype(jnp.float32)))
           - jnp.exp(jnp.sum(lam_q2.astype(jnp.float32) * lam_k2.astype(jnp.float32))) + lam_init)
    scale = A_QK_DIM ** -0.5
    nq = s // Q_BLOCK
    qb = q.reshape(bsz, A_HEADS, 2, nq, Q_BLOCK, A_QK_DIM).transpose(3, 0, 1, 2, 4, 5)
    kpos = jnp.arange(s)

    def block(args):
        j, qj = args
        qpos = j * Q_BLOCK + jnp.arange(Q_BLOCK)
        sc = jnp.einsum('bhiqd,bhikd->bhiqk', qj, k).astype(jnp.float32) * scale
        sc = jnp.where(kpos[None, :] <= qpos[:, None], sc, -jnp.inf)
        p = jax.nn.softmax(sc, axis=-1)
        w = p[:, :, 0] - lam * p[:, :, 1]
        return jnp.einsum('bhqk,bhkd->bhqd', w.astype(v.dtype), v)

    o = lax.map(block, (jnp.arange(nq), qb))
    o = o.transpose(1, 2, 0, 3, 4).reshape(bsz, A_HEADS, s, A_V_DIM)
    o = rms_norm(o, out_gain) * (1.0 - lam_init)
    return merge_heads(o)

def moba_attention(q, k, v, q_gain, k_gain):
    bsz, s, _ = q.shape
    q = rms_norm(to_heads(q, B_HEADS), q_gain)
    k = rms_norm(to_heads(k, B_HEADS), k_gain)
    v = to_heads(v, B_HEADS)
    nb = -(-s // MOBA_BLOCK)
    pad = nb * MOBA_BLOCK - s
    k_p = jnp.pad(k, ((0, 0), (0, 0), (0, pad), (0, 0)))
    v_p = jnp.pad(v, ((0, 0), (0, 0), (0, pad), (0, 0)))
    kb = k_p.reshape(bsz, B_HEADS, nb, MOBA_BLOCK, B_HEAD_DIM)
    vb = v_p.reshape(bsz, B_HEADS, nb, MOBA_BLOCK, B_HEAD_DIM)
    k_mean = jnp.mean(kb.astype(jnp.float32), axis=3)
    topk = min(MOBA_TOPK, nb)
    scale = B_HEAD_DIM ** -0.5
    nq = s // Q_BLOCK
    qb = q.reshape(bsz, B_HEADS, nq, Q_BLOCK, B_HEAD_DIM).transpose(2, 0, 1, 3, 4)
    b_idx = jnp.arange(bsz)[:, None, None, None]
    h_idx = jnp.arange(B_HEADS)[None, :, None, None]
    blk_ids = jnp.arange(nb)

    def block(args):
        j, qj = args
        qpos = j * Q_BLOCK + jnp.arange(Q_BLOCK)
        own = (j * Q_BLOCK) // MOBA_BLOCK
        gate = jnp.einsum('bhqd,bhnd->bhqn', qj.astype(jnp.float32), k_mean)
        gate = jnp.where(blk_ids < own, gate, -jnp.inf)
        _, sel = lax.top_k(gate, topk)
        valid = sel < own
        k_sel = kb[b_idx, h_idx, sel]
        v_sel = vb[b_idx, h_idx, sel]
        s_sel = jnp.einsum('bhqd,bhqnkd->bhqnk', qj, k_sel).astype(jnp.float32) * scale
        s_sel = jnp.where(valid[..., None], s_sel, -jnp.inf).reshape(bsz, B_HEADS, Q_BLOCK, topk * MOBA_BLOCK)
        k_own = lax.dynamic_slice_in_dim(k_p, own * MOBA_BLOCK, MOBA_BLOCK, axis=2)
        v_own = lax.dynamic_slice_in_dim(v_p, own * MOBA_BLOCK, MOBA_BLOCK, axis=2)
        kpos = own * MOBA_BLOCK + jnp.arange(MOBA_BLOCK)
        s_own = jnp.einsum('bhqd,bhkd->bhqk', qj, k_own).astype(jnp.float32) * scale
        s_own = jnp.where(kpos[None, :] <= qpos[:, None], s_own, -jnp.inf)
        p = jax.nn.softmax(jnp.concatenate([s_sel, s_own], axis=-1), axis=-1).astype(v.dtype)
        p_sel = p[..., :topk * MOBA_BLOCK].reshape(bsz, B_HEADS, Q_BLOCK, topk, MOBA_BLOCK)
        p_own = p[..., topk * MOBA_BLOCK:]
        return (jnp.einsum('bhqnk,bhqnkd->bhqd', p_sel, v_sel)
                + jnp.einsum('bhqk,bhkd->bhqd', p_own, v_own))

    o = lax.map(block, (jnp.arange(nq), qb))
    o = o.transpose(1, 2, 0, 3, 4).reshape(bsz, B_HEADS, s, B_HEAD_DIM)
    return merge_heads(o)

def gla(q, k, v, g_low, r, w_g2, b_g, out_gain):
    bsz, s, _ = q.shape
    dt = q.dtype
    f32 = jnp.float32
    q = to_heads(q, C_HEADS).astype(f32) * (C_K_DIM ** -0.5)
    k = to_heads(k, C_HEADS).astype(f32)
    v = to_heads(v, C_HEADS).astype(f32)
    g = jax.nn.log_sigmoid((g_low @ w_g2 + b_g).astype(f32)) / GLA_TAU
    g = to_heads(g, C_HEADS)
    nc = s // GLA_CHUNK

    def chunks(t):
        return t.reshape(bsz, C_HEADS, nc, GLA_CHUNK, t.shape[-1]).transpose(2, 0, 1, 3, 4)

    causal = jnp.tril(jnp.ones((GLA_CHUNK, GLA_CHUNK), bool))

    def step(state, inp):
        qc, kc, vc, gc = inp
        bcum = jnp.cumsum(gc, axis=2)
        o_inter = jnp.einsum('bhcd,bhde->bhce', qc * jnp.exp(bcum), state)
        diff = bcum[:, :, :, None, :] - bcum[:, :, None, :, :]
        decay = jnp.exp(jnp.where(causal[:, :, None], diff, -jnp.inf))
        att = jnp.einsum('bhid,bhjd,bhijd->bhij', qc, kc, decay)
        o_intra = jnp.einsum('bhij,bhje->bhie', att, vc)
        b_last = bcum[:, :, -1:, :]
        state = (jnp.exp(b_last[:, :, 0, :])[..., None] * state
                 + jnp.einsum('bhcd,bhce->bhde', kc * jnp.exp(b_last - bcum), vc))
        return state, o_inter + o_intra

    state0 = jnp.zeros((bsz, C_HEADS, C_K_DIM, C_V_DIM), f32)
    _, o = lax.scan(step, state0, (chunks(q), chunks(k), chunks(v), chunks(g)))
    o = o.transpose(1, 2, 0, 3, 4).reshape(bsz, C_HEADS, s, C_V_DIM)
    o = merge_heads(rms_norm(o, out_gain)) * jax.nn.silu(r.astype(f32))
    return o.astype(dt)

def rg_lru(xb, gate_in, conv_w, conv_b, w_a, b_a, w_x, b_x, lam):
    bsz, s, cw = xb.shape
    f32 = jnp.float32
    xc = lax.conv_general_dilated(xb, conv_w[:, None, :], window_strides=(1,),
                                  padding=[(CONV_W - 1, 0)],
                                  dimension_numbers=('NWC', 'WIO', 'NWC'),
                                  feature_group_count=cw) + conv_b
    xs = xc.reshape(bsz, s, D_BLOCKS, D_BLOCK_DIM)
    r_gate = jax.nn.sigmoid((jnp.einsum('bsnd,nde->bsne', xs, w_a).reshape(bsz, s, cw) + b_a).astype(f32))
    i_gate = jax.nn.sigmoid((jnp.einsum('bsnd,nde->bsne', xs, w_x).reshape(bsz, s, cw) + b_x).astype(f32))
    log_a = LRU_C * r_gate * jax.nn.log_sigmoid(lam.astype(f32))
    a = jnp.exp(log_a)
    bt = jnp.sqrt(-jnp.expm1(2.0 * log_a)) * (i_gate * xc.astype(f32))

    def combine(c1, c2):
        a1, b1 = c1
        a2, b2 = c2
        return a1 * a2, a2 * b1 + b2

    _, h = lax.associative_scan(combine, (a, bt), axis=1)
    return (h * jax.nn.gelu(gate_in.astype(f32))).astype(xb.dtype)

def hybrid_mixer(h, w_in, w_out, a_q_gain, a_k_gain, a_lam_q1, a_lam_k1, a_lam_q2, a_lam_k2,
                 a_out_gain, b_q_gain, b_k_gain, c_w_g2, c_b_g, c_out_gain, d_conv_w, d_conv_b,
                 d_w_a, d_b_a, d_w_x, d_b_x, d_lambda, layer_idx):
    proj = h @ w_in
    aq, ak, av, bq, bk, bv, cq, ck, cv, cg, cr, dx, dg = split_columns(proj)
    o_a = diff_attention(aq, ak, av, a_q_gain, a_k_gain, a_lam_q1, a_lam_k1, a_lam_q2, a_lam_k2,
                         a_out_gain, layer_idx)
    o_b = moba_attention(bq, bk, bv, b_q_gain, b_k_gain)
    o_c = gla(cq, ck, cv, cg, cr, c_w_g2, c_b_g, c_out_gain)
    o_d = rg_lru(dx, dg, d_conv_w, d_conv_b, d_w_a, d_b_a, d_w_x, d_b_x, d_lambda)
    y = jnp.concatenate([o_a.astype(h.dtype), o_b.astype(h.dtype), o_c, o_d], axis=-1)
    return y @ w_out

def moe(h, router_w, router_b, w_up, b_up, w_down, b_down):
    bsz, s, d = h.shape
    t = bsz * s
    xt = h.reshape(t, d)
    logits = (xt @ router_w + router_b).astype(jnp.float32)
    top_vals, top_idx = lax.top_k(logits, TOP_K)
    gates = jax.nn.softmax(top_vals, axis=-1)
    n = t * TOP_K
    e_flat = top_idx.reshape(n)
    tok_flat = jnp.arange(n, dtype=jnp.int32) // TOP_K
    g_flat = gates.reshape(n)
    order = jnp.argsort(e_flat)
    e_sorted = e_flat[order]
    tok_sorted = tok_flat[order]
    g_sorted = g_flat[order]
    counts = jax.ops.segment_sum(jnp.ones((n,), jnp.int32), e_flat, num_segments=N_EXPERTS)
    starts = jnp.cumsum(counts) - counts
    padded = (counts + MOE_BLOCK - 1) // MOE_BLOCK * MOE_BLOCK
    pad_ends = jnp.cumsum(padded)
    pad_starts = pad_ends - padded
    dest = pad_starts[e_sorted] + (jnp.arange(n, dtype=jnp.int32) - starts[e_sorted])
    n_rows = -(-n // MOE_BLOCK) * MOE_BLOCK + N_EXPERTS * MOE_BLOCK
    n_blocks = n_rows // MOE_BLOCK
    row_tok = jnp.full((n_rows,), t, jnp.int32).at[dest].set(tok_sorted)
    row_gate = jnp.zeros((n_rows,), jnp.float32).at[dest].set(g_sorted)
    blk_expert = jnp.minimum(jnp.searchsorted(pad_ends, jnp.arange(n_blocks) * MOE_BLOCK, side='right'),
                             N_EXPERTS - 1)
    x_pad = jnp.concatenate([xt, jnp.zeros((1, d), xt.dtype)], axis=0)
    x_rows = x_pad[row_tok].reshape(n_blocks, MOE_BLOCK, d)

    def expert_block(args):
        e, xb = args
        hu = xb @ w_up[e] + b_up[e]
        g = jnp.minimum(hu[:, :D_FF], SWIGLU_LIMIT)
        lin = jnp.clip(hu[:, D_FF:], -SWIGLU_LIMIT, SWIGLU_LIMIT)
        glu = g * jax.nn.sigmoid(SWIGLU_ALPHA * g)
        return ((lin + 1.0) * glu) @ w_down[e] + b_down[e]

    y_rows = lax.map(expert_block, (blk_expert, x_rows)).reshape(n_rows, d)
    y = jax.ops.segment_sum(y_rows * row_gate[:, None].astype(y_rows.dtype), row_tok, num_segments=t + 1)[:t]
    return y.reshape(bsz, s, d)

def first_inputs(seed: int = 0) -> dict:
    key = jax.random.key(seed)
    ks = iter(jax.random.split(key, 40))
    L = DEPTH
    f32 = jnp.float32

    def nrm(shape, scale):
        return jax.random.normal(next(ks), shape, f32) * scale

    def gain(shape):
        return 1.0 + nrm(shape, 0.05)

    x = nrm((BATCH, SEQ, D_MODEL), 1.0)
    c = nrm((BATCH, D_MODEL), 1.0)
    ada_w = nrm((L, D_MODEL, 6 * D_MODEL), 0.5 * D_MODEL ** -0.5)
    ada_b = nrm((L, 6 * D_MODEL), 0.02)
    norm1_g = gain((L, D_MODEL))
    norm2_g = gain((L, D_MODEL))
    w_in = nrm((L, D_MODEL, D_IN), D_MODEL ** -0.5)
    w_out = nrm((L, D_MIX, D_MODEL), D_MIX ** -0.5)
    a_q_gain = gain((L, A_QK_DIM))
    a_k_gain = gain((L, A_QK_DIM))
    a_lam_q1 = nrm((L, A_QK_DIM), 0.1)
    a_lam_k1 = nrm((L, A_QK_DIM), 0.1)
    a_lam_q2 = nrm((L, A_QK_DIM), 0.1)
    a_lam_k2 = nrm((L, A_QK_DIM), 0.1)
    a_out_gain = gain((L, A_V_DIM))
    b_q_gain = gain((L, B_HEAD_DIM))
    b_k_gain = gain((L, B_HEAD_DIM))
    c_w_g2 = nrm((L, GLA_RANK, C_HEADS * C_K_DIM), GLA_RANK ** -0.5)
    c_b_g = nrm((L, C_HEADS * C_K_DIM), 0.1)
    c_out_gain = gain((L, C_V_DIM))
    d_conv_w = nrm((L, CONV_W, D_WIDTH), CONV_W ** -0.5)
    d_conv_b = nrm((L, D_WIDTH), 0.02)
    d_w_a = nrm((L, D_BLOCKS, D_BLOCK_DIM, D_BLOCK_DIM), D_BLOCK_DIM ** -0.5)
    d_b_a = nrm((L, D_WIDTH), 0.02)
    d_w_x = nrm((L, D_BLOCKS, D_BLOCK_DIM, D_BLOCK_DIM), D_BLOCK_DIM ** -0.5)
    d_b_x = nrm((L, D_WIDTH), 0.02)
    u = jax.random.uniform(next(ks), (L, D_WIDTH), f32, 0.9, 0.999)
    p = u ** (1.0 / LRU_C)
    d_lambda = jnp.log(p) - jnp.log1p(-p)
    router_w = nrm((L, D_MODEL, N_EXPERTS), D_MODEL ** -0.5)
    router_b = nrm((L, N_EXPERTS), 0.01)
    exp_w_up = nrm((L, N_EXPERTS, D_MODEL, 2 * D_FF), D_MODEL ** -0.5)
    exp_b_up = nrm((L, N_EXPERTS, 2 * D_FF), 0.01)
    exp_w_down = nrm((L, N_EXPERTS, D_FF, D_MODEL), D_FF ** -0.5)
    exp_b_down = nrm((L, N_EXPERTS, D_MODEL), 0.01)
    return {"x": x, "c": c, "ada_w": ada_w, "ada_b": ada_b, "norm1_g": norm1_g, "norm2_g": norm2_g,
            "w_in": w_in, "w_out": w_out, "a_q_gain": a_q_gain, "a_k_gain": a_k_gain,
            "a_lam_q1": a_lam_q1, "a_lam_k1": a_lam_k1, "a_lam_q2": a_lam_q2, "a_lam_k2": a_lam_k2,
            "a_out_gain": a_out_gain, "b_q_gain": b_q_gain, "b_k_gain": b_k_gain,
            "c_w_g2": c_w_g2, "c_b_g": c_b_g, "c_out_gain": c_out_gain,
            "d_conv_w": d_conv_w, "d_conv_b": d_conv_b, "d_w_a": d_w_a, "d_b_a": d_b_a,
            "d_w_x": d_w_x, "d_b_x": d_b_x, "d_lambda": d_lambda,
            "router_w": router_w, "router_b": router_b, "exp_w_up": exp_w_up, "exp_b_up": exp_b_up,
            "exp_w_down": exp_w_down, "exp_b_down": exp_b_down}

def first_block(x, c, ada_w, ada_b, norm1_g, norm2_g, w_in, w_out, a_q_gain, a_k_gain,
              a_lam_q1, a_lam_k1, a_lam_q2, a_lam_k2, a_out_gain, b_q_gain, b_k_gain,
              c_w_g2, c_b_g, c_out_gain, d_conv_w, d_conv_b, d_w_a, d_b_a, d_w_x, d_b_x, d_lambda,
              router_w, router_b, exp_w_up, exp_b_up, exp_w_down, exp_b_down):
    cond = jax.nn.silu(c)
    for l in range(DEPTH):
        mod = cond @ ada_w[l] + ada_b[l]
        sh1, sc1, g1, sh2, sc2, g2 = jnp.split(mod, 6, axis=-1)
        h = rms_norm(x, norm1_g[l]) * (1.0 + sc1[:, None, :]) + sh1[:, None, :]
        y = hybrid_mixer(h, w_in[l], w_out[l], a_q_gain[l], a_k_gain[l], a_lam_q1[l], a_lam_k1[l],
                         a_lam_q2[l], a_lam_k2[l], a_out_gain[l], b_q_gain[l], b_k_gain[l],
                         c_w_g2[l], c_b_g[l], c_out_gain[l], d_conv_w[l], d_conv_b[l],
                         d_w_a[l], d_b_a[l], d_w_x[l], d_b_x[l], d_lambda[l], l)
        x = x + g1[:, None, :] * y
        h = rms_norm(x, norm2_g[l]) * (1.0 + sc2[:, None, :]) + sh2[:, None, :]
        y = moe(h, router_w[l], router_b[l], exp_w_up[l], exp_b_up[l], exp_w_down[l], exp_b_down[l])
        x = x + g2[:, None, :] * y
    return x


DEPTH_2 = 2

SSD_EXPAND = 2
SSD_D_INNER = SSD_EXPAND * D_MODEL
SSD_HEAD_DIM = 64
SSD_N_HEADS = SSD_D_INNER // SSD_HEAD_DIM
SSD_N_GROUPS = 4
SSD_HEADS_PER_GROUP = SSD_N_HEADS // SSD_N_GROUPS
SSD_D_STATE = 128
SSD_CONV_WIDTH = 4
SSD_CHUNK = 128
SSD_CONV_DIM = SSD_D_INNER + 2 * SSD_N_GROUPS * SSD_D_STATE

S5_WIDTH = D_MODEL
S5_GROUP = 16
S5_N_GROUPS = S5_WIDTH // S5_GROUP
S5_STATE = 64
S5_MIN_STEP = 0.001
S5_MAX_STEP = 0.1
S5_MAX_REAL = -1e-4

FFN_HIDDEN = 2816

RMS_EPS = 1e-6

IN_PROJ_DIM = SSD_D_INNER + SSD_CONV_DIM + SSD_N_HEADS + S5_WIDTH + 2 * D_MODEL
SPLITS = list(np.cumsum([SSD_D_INNER, SSD_CONV_DIM, SSD_N_HEADS, S5_WIDTH, D_MODEL]))


def rmsnorm(x, g):
    xf = x.astype(jnp.float32)
    xf = xf * lax.rsqrt(jnp.mean(xf * xf, axis=-1, keepdims=True) + RMS_EPS)
    return (xf * g.astype(jnp.float32)).astype(x.dtype)

def swiglu(x, w_gate, w_up, w_down):
    return (jax.nn.silu(x @ w_gate) * (x @ w_up)) @ w_down

def causal_depthwise_conv(u, w, b):
    k, c = w.shape
    out = lax.conv_general_dilated(
        u, w[:, None, :].astype(u.dtype), window_strides=(1,), padding=[(k - 1, 0)],
        dimension_numbers=("NWC", "WIO", "NWC"), feature_group_count=c)
    return out + b.astype(u.dtype)

def segsum(a):
    t = a.shape[-1]
    cs = jnp.cumsum(a, axis=-1)
    seg = cs[..., :, None] - cs[..., None, :]
    mask = jnp.tril(jnp.ones((t, t), dtype=bool))
    return jnp.where(mask, seg, -jnp.inf)

def ssd_chunked(xdt, adt, bmat, cmat):
    b, l, h, p = xdt.shape
    g, n = bmat.shape[2], bmat.shape[3]
    r = h // g
    q = SSD_CHUNK
    c = l // q
    X = xdt.reshape(b, c, q, g, r, p)
    A = adt.reshape(b, c, q, g, r).transpose(0, 3, 4, 1, 2)
    Bc = bmat.reshape(b, c, q, g, n)
    Cc = cmat.reshape(b, c, q, g, n)
    a_cum = jnp.cumsum(A, axis=-1)
    decay_in = jnp.exp(segsum(A))
    cb = jnp.einsum("bclgn,bcsgn->bcgls", Cc, Bc)
    y_diag = jnp.einsum("bcgls,bgrcls,bcsgrp->bclgrp", cb, decay_in, X)
    decay_states = jnp.exp(a_cum[..., -1:] - a_cum)
    states = jnp.einsum("bclgn,bgrcl,bclgrp->bcgrpn", Bc, decay_states, X)
    states = jnp.concatenate([jnp.zeros_like(states[:, :1]), states], axis=1)
    chunk_a = jnp.pad(a_cum[..., -1], ((0, 0), (0, 0), (0, 0), (1, 0)))
    chunk_decay = jnp.exp(segsum(chunk_a))
    new_states = jnp.einsum("bgrzc,bcgrpn->bzgrpn", chunk_decay, states)
    states = new_states[:, :-1]
    y_off = jnp.einsum("bclgn,bcgrpn,bgrcl->bclgrp", Cc, states, jnp.exp(a_cum))
    return (y_diag + y_off).reshape(b, l, h, p)

def ssd_branch(z, xbc, dt_raw, conv_w, conv_b, dt_bias, a_log, d_skip, norm_g):
    b, l, _ = z.shape
    xbc = jax.nn.silu(causal_depthwise_conv(xbc, conv_w, conv_b)).astype(jnp.float32)
    xs = xbc[..., :SSD_D_INNER].reshape(b, l, SSD_N_HEADS, SSD_HEAD_DIM)
    bm = xbc[..., SSD_D_INNER:SSD_D_INNER + SSD_N_GROUPS * SSD_D_STATE].reshape(b, l, SSD_N_GROUPS, SSD_D_STATE)
    cm = xbc[..., SSD_D_INNER + SSD_N_GROUPS * SSD_D_STATE:].reshape(b, l, SSD_N_GROUPS, SSD_D_STATE)
    dt = jax.nn.softplus(dt_raw.astype(jnp.float32) + dt_bias.astype(jnp.float32))
    a = -jnp.exp(a_log.astype(jnp.float32))
    y = ssd_chunked(xs * dt[..., None], a * dt, bm, cm) + d_skip.astype(jnp.float32)[:, None] * xs
    y = y.reshape(b, l, SSD_D_INNER)
    y = y * jax.nn.silu(z.astype(jnp.float32))
    yg = y.reshape(b, l, SSD_N_GROUPS, SSD_D_INNER // SSD_N_GROUPS)
    yg = yg * lax.rsqrt(jnp.mean(yg * yg, axis=-1, keepdims=True) + RMS_EPS)
    y = yg.reshape(b, l, SSD_D_INNER) * norm_g.astype(jnp.float32)
    return y.astype(z.dtype)

def s5_branch(u, lam_re, lam_im, b_re, b_im, c_re, c_im, log_step, d_skip, w_glu):
    b, l, _ = u.shape
    uf = u.astype(jnp.float32)
    ug = uf.reshape(b, l, S5_N_GROUPS, S5_GROUP)
    lam = lax.complex(jnp.minimum(lam_re.astype(jnp.float32), S5_MAX_REAL), lam_im.astype(jnp.float32))
    step = jnp.exp(log_step.astype(jnp.float32))[:, None]
    lam_bar = jnp.exp(lam * step)
    b_bar = ((lam_bar - 1.0) / lam)[..., None] * lax.complex(b_re.astype(jnp.float32), b_im.astype(jnp.float32))
    bu = jnp.einsum("blgc,gnc->blgn", ug.astype(jnp.complex64), b_bar)
    a_elems = jnp.broadcast_to(lam_bar, bu.shape)

    def combine(e1, e2):
        a1, s1 = e1
        a2, s2 = e2
        return a2 * a1, a2 * s1 + s2

    _, states = lax.associative_scan(combine, (a_elems, bu), axis=1)
    c = lax.complex(c_re.astype(jnp.float32), c_im.astype(jnp.float32))
    y = jnp.real(jnp.einsum("blgn,gcn->blgc", states, c)).reshape(b, l, S5_WIDTH)
    y = y + d_skip.astype(jnp.float32) * uf
    y = jax.nn.gelu(y).astype(u.dtype)
    val, gate = jnp.split(y @ w_glu, 2, axis=-1)
    return val * jax.nn.sigmoid(gate)

def mixer(u, w_in, ssd_conv_w, ssd_conv_b, ssd_dt_bias, ssd_a_log, ssd_d, ssd_norm_g, w_branch_a,
          s5_lambda_re, s5_lambda_im, s5_b_re, s5_b_im, s5_c_re, s5_c_im, s5_log_step, s5_d, s5_w_glu,
          w_branch_b, w_out):
    proj = u @ w_in
    z, xbc, dt_raw, u5, g_a, g_b = jnp.split(proj, SPLITS, axis=-1)
    y_a = ssd_branch(z, xbc, dt_raw, ssd_conv_w, ssd_conv_b, ssd_dt_bias, ssd_a_log, ssd_d, ssd_norm_g) @ w_branch_a
    y_b = s5_branch(u5, s5_lambda_re, s5_lambda_im, s5_b_re, s5_b_im, s5_c_re, s5_c_im,
                    s5_log_step, s5_d, s5_w_glu) @ w_branch_b
    merged = jax.nn.sigmoid(g_a) * y_a + jax.nn.sigmoid(g_b) * y_b
    return merged @ w_out

def second_inputs(seed: int = 0) -> dict:
    key = jax.random.key(seed)
    ks = iter(jax.random.split(key, 40))
    f32 = jnp.float32
    L = DEPTH_2

    def normal(shape, scale):
        return jax.random.normal(next(ks), shape, f32) * scale

    def gain(shape):
        return 1.0 + 0.02 * jax.random.normal(next(ks), shape, f32)

    x = jax.random.normal(next(ks), (BATCH, SEQ, D_MODEL), f32)
    d_ = D_MODEL
    dt_init = jnp.exp(jax.random.uniform(next(ks), (L, SSD_N_HEADS), f32,
                                         math.log(0.001), math.log(0.1)))
    n_idx = jnp.arange(S5_STATE, dtype=f32)
    return {
        "x": x,
        "ffn1_pre_g": gain((L, d_)),
        "ffn1_post_g": gain((L, d_)),
        "ffn1_w_gate": normal((L, d_, FFN_HIDDEN), d_ ** -0.5),
        "ffn1_w_up": normal((L, d_, FFN_HIDDEN), d_ ** -0.5),
        "ffn1_w_down": normal((L, FFN_HIDDEN, d_), FFN_HIDDEN ** -0.5),
        "mix_pre_g": gain((L, d_)),
        "mix_post_g": gain((L, d_)),
        "w_in": normal((L, d_, IN_PROJ_DIM), d_ ** -0.5),
        "ssd_conv_w": normal((L, SSD_CONV_WIDTH, SSD_CONV_DIM), SSD_CONV_WIDTH ** -0.5),
        "ssd_conv_b": normal((L, SSD_CONV_DIM), 0.02),
        "ssd_dt_bias": dt_init + jnp.log(-jnp.expm1(-dt_init)),
        "ssd_a_log": jnp.log(jax.random.uniform(next(ks), (L, SSD_N_HEADS), f32, 1.0, 16.0)),
        "ssd_d": gain((L, SSD_N_HEADS)),
        "ssd_norm_g": gain((L, SSD_D_INNER)),
        "w_branch_a": normal((L, SSD_D_INNER, d_), SSD_D_INNER ** -0.5),
        "s5_lambda_re": -0.5 + 0.01 * jax.random.normal(next(ks), (L, S5_N_GROUPS, S5_STATE), f32),
        "s5_lambda_im": math.pi * n_idx + 0.01 * jax.random.normal(next(ks), (L, S5_N_GROUPS, S5_STATE), f32),
        "s5_b_re": normal((L, S5_N_GROUPS, S5_STATE, S5_GROUP), (2 * S5_GROUP) ** -0.5),
        "s5_b_im": normal((L, S5_N_GROUPS, S5_STATE, S5_GROUP), (2 * S5_GROUP) ** -0.5),
        "s5_c_re": normal((L, S5_N_GROUPS, S5_GROUP, S5_STATE), (2 * S5_STATE) ** -0.5),
        "s5_c_im": normal((L, S5_N_GROUPS, S5_GROUP, S5_STATE), (2 * S5_STATE) ** -0.5),
        "s5_log_step": jax.random.uniform(next(ks), (L, S5_N_GROUPS), f32,
                                          math.log(S5_MIN_STEP), math.log(S5_MAX_STEP)),
        "s5_d": normal((L, S5_WIDTH), 1.0),
        "s5_w_glu": normal((L, S5_WIDTH, 2 * S5_WIDTH), S5_WIDTH ** -0.5),
        "w_branch_b": normal((L, S5_WIDTH, d_), S5_WIDTH ** -0.5),
        "w_out": normal((L, d_, d_), d_ ** -0.5),
        "ffn2_pre_g": gain((L, d_)),
        "ffn2_post_g": gain((L, d_)),
        "ffn2_w_gate": normal((L, d_, FFN_HIDDEN), d_ ** -0.5),
        "ffn2_w_up": normal((L, d_, FFN_HIDDEN), d_ ** -0.5),
        "ffn2_w_down": normal((L, FFN_HIDDEN, d_), FFN_HIDDEN ** -0.5),
    }

def second_block(x, ffn1_pre_g, ffn1_post_g, ffn1_w_gate, ffn1_w_up, ffn1_w_down,
              mix_pre_g, mix_post_g, w_in, ssd_conv_w, ssd_conv_b, ssd_dt_bias, ssd_a_log, ssd_d,
              ssd_norm_g, w_branch_a, s5_lambda_re, s5_lambda_im, s5_b_re, s5_b_im, s5_c_re, s5_c_im,
              s5_log_step, s5_d, s5_w_glu, w_branch_b, w_out,
              ffn2_pre_g, ffn2_post_g, ffn2_w_gate, ffn2_w_up, ffn2_w_down):
    h = x
    for i in range(DEPTH_2):
        f = swiglu(rmsnorm(h, ffn1_pre_g[i]), ffn1_w_gate[i], ffn1_w_up[i], ffn1_w_down[i])
        h = h + 0.5 * rmsnorm(f, ffn1_post_g[i])
        m = mixer(rmsnorm(h, mix_pre_g[i]), w_in[i], ssd_conv_w[i], ssd_conv_b[i], ssd_dt_bias[i],
                  ssd_a_log[i], ssd_d[i], ssd_norm_g[i], w_branch_a[i],
                  s5_lambda_re[i], s5_lambda_im[i], s5_b_re[i], s5_b_im[i], s5_c_re[i], s5_c_im[i],
                  s5_log_step[i], s5_d[i], s5_w_glu[i], w_branch_b[i], w_out[i])
        h = h + rmsnorm(m, mix_post_g[i])
        f = swiglu(rmsnorm(h, ffn2_pre_g[i]), ffn2_w_gate[i], ffn2_w_up[i], ffn2_w_down[i])
        h = h + 0.5 * rmsnorm(f, ffn2_post_g[i])
    return h


def setup_inputs(seed=0):
    out = dict(first_inputs(seed))
    for name, value in second_inputs(seed + 1).items():
        if name != "x":
            out[name + "_2"] = value
    return out


def reference(
    x, c, ada_w, ada_b, norm1_g, norm2_g, w_in, w_out, a_q_gain, a_k_gain, a_lam_q1, a_lam_k1,
    a_lam_q2, a_lam_k2, a_out_gain, b_q_gain, b_k_gain, c_w_g2, c_b_g, c_out_gain, d_conv_w,
    d_conv_b, d_w_a, d_b_a, d_w_x, d_b_x, d_lambda, router_w, router_b, exp_w_up, exp_b_up,
    exp_w_down, exp_b_down, ffn1_pre_g_2, ffn1_post_g_2, ffn1_w_gate_2, ffn1_w_up_2,
    ffn1_w_down_2, mix_pre_g_2, mix_post_g_2, w_in_2, ssd_conv_w_2, ssd_conv_b_2, ssd_dt_bias_2,
    ssd_a_log_2, ssd_d_2, ssd_norm_g_2, w_branch_a_2, s5_lambda_re_2, s5_lambda_im_2, s5_b_re_2,
    s5_b_im_2, s5_c_re_2, s5_c_im_2, s5_log_step_2, s5_d_2, s5_w_glu_2, w_branch_b_2, w_out_2,
    ffn2_pre_g_2, ffn2_post_g_2, ffn2_w_gate_2, ffn2_w_up_2, ffn2_w_down_2,
):
    x = first_block(
        x, c, ada_w, ada_b, norm1_g, norm2_g, w_in, w_out, a_q_gain, a_k_gain, a_lam_q1,
        a_lam_k1, a_lam_q2, a_lam_k2, a_out_gain, b_q_gain, b_k_gain, c_w_g2, c_b_g, c_out_gain,
        d_conv_w, d_conv_b, d_w_a, d_b_a, d_w_x, d_b_x, d_lambda, router_w, router_b, exp_w_up,
        exp_b_up, exp_w_down, exp_b_down,
    )
    return second_block(
        x, ffn1_pre_g_2, ffn1_post_g_2, ffn1_w_gate_2, ffn1_w_up_2, ffn1_w_down_2, mix_pre_g_2,
        mix_post_g_2, w_in_2, ssd_conv_w_2, ssd_conv_b_2, ssd_dt_bias_2, ssd_a_log_2, ssd_d_2,
        ssd_norm_g_2, w_branch_a_2, s5_lambda_re_2, s5_lambda_im_2, s5_b_re_2, s5_b_im_2,
        s5_c_re_2, s5_c_im_2, s5_log_step_2, s5_d_2, s5_w_glu_2, w_branch_b_2, w_out_2,
        ffn2_pre_g_2, ffn2_post_g_2, ffn2_w_gate_2, ffn2_w_up_2, ffn2_w_down_2,
    )


_drawn_inputs = setup_inputs


def setup_inputs(seed=0):
    import zlib

    import numpy as np

    out = dict(_drawn_inputs(seed))
    spreads = {}
    factors = {'a_q_gain': 4.051,
     'a_k_gain': 4.673,
     'a_lam_k1': 3.68,
     'a_lam_q2': 200.0,
     'a_out_gain': 3.04,
     'b_q_gain': 8.0,
     'b_k_gain': 8.0,
     'c_b_g': 3.78,
     'c_out_gain': 4.027,
     'd_conv_b': 2.675,
     'd_b_a': 30.257,
     'd_b_x': 8.0,
     'router_b': 2.974,
     'exp_b_up': 8.0,
     'exp_b_down': 8.0,
     'ffn1_post_g_2': 3.593,
     'mix_post_g_2': 2.726,
     'ssd_d_2': 4.616,
     'ssd_norm_g_2': 3.051,
     's5_lambda_re_2': 64.0,
     's5_lambda_im_2': 24.496,
     's5_b_re_2': 34.368,
     's5_b_im_2': 35.064,
     's5_c_re_2': 34.488,
     's5_c_im_2': 34.488,
     's5_log_step_2': 25.68,
     'ffn2_pre_g_2': 4.119,
     'ffn2_post_g_2': 16.505}
    for name, (base, spread) in spreads.items():
        noise = np.random.default_rng([zlib.crc32(name.encode()), seed]).standard_normal(out[name].shape)
        drawn = base * np.exp(spread * noise) if base else spread * noise
        out[name] = __import__('jax').numpy.asarray(drawn.astype(out[name].dtype))
    for name, factor in factors.items():
        out[name] = (out[name] * factor).astype(out[name].dtype)
    return out
```

```python
from contextlib import ExitStack

import concourse.bass as bass
from concourse import mybir

P = 128
D = 1024
TOK = 256
TT = TOK // P
KT = D // P
W = 256
SLOTS = 12
NE = 32
TOPK = 4
CAP = 88
PASSES = -(-TOK // CAP)
FH = 2816
LAYERS = 2
EPS = 1e-6
NEG = -1e30
NCH = FH // W
LAM0 = 0.2

F32 = mybir.dt.float32
I32 = mybir.dt.int32
ALU = mybir.AluOpType
ACT = mybir.ActivationFunctionType
AX = mybir.AxisListType.X

AQ, AK, AV, BQ, BK, BV, CQ, CV, CG, CR, DX, DG = (
    0, 256, 512, 768, 1024, 1280, 1536, 1792, 2048, 2064, 2320, 2576)
WIN1_FEATURE = (AQ, AK, BQ, BK, CQ, CR, DX, DG)
WIN1_TOKEN = (AV, BV, CV)
Z2, XBC2, DT2, U52, GA2, GB2 = 0, 2048, 5120, 5152, 6176, 7200

V1 = {}
_n = 0
for _name, _rows in (("norm1_g", 8), ("norm2_g", 8), ("sh0", 8), ("sc0", 8), ("sh1", 8), ("sc1", 8),
                     ("c", 8), ("d_conv_w", 8), ("d_conv_b", 2), ("d_b_a", 2), ("d_b_x", 2),
                     ("d_lambda", 2), ("c_b_g", 1), ("a_q_gain", 1), ("a_k_gain", 1), ("b_q_gain", 1),
                     ("b_k_gain", 1), ("a_out_gain", 1), ("c_out_gain", 1)):
    V1[_name] = _n
    _n += _rows
NV1 = _n
V2 = {}
_n = 0
for _name, _rows in (("ffn1_pre_g", 8), ("mix_pre_g", 8), ("ffn2_pre_g", 8), ("conv_b", 24), ("norm_g", 16),
                     ("s5_d", 8), ("lam_re", 32), ("conv_w", 96), ("lam_im", 32)):
    V2[_name] = _n
    _n += _rows
NV2 = _n
NV2A = V2["conv_w"]


def build(nc, a, out, upto=99):
    ctx = ExitStack()
    with ctx:
        def sb(name, shape, dt=F32):
            return ctx.enter_context(nc.sbuf_tensor(name, shape, dt))

        sems = {}

        def sem(name):
            if name not in sems:
                sems[name] = ctx.enter_context(nc.semaphore(name))
            return sems[name]

        ctx.enter_context(nc.allow_non_contiguous_dma(reason="small vectors and state matrices"))

        ring = sb("ring", [P, SLOTS, 2048])
        x = sb("x_res", [P, TT, D])
        ffn_buf = sb("ffn_buf", [P, 2048])
        hidden = ffn_buf[:, 0:1024].rearrange("p (a b c) -> p a b c", b=2, c=W)
        gated = ffn_buf[:, 1024:2048].rearrange("p (a b c) -> p a b c", b=2, c=W)
        post_gain = sb("post_gain", [P, D])
        ident = sb("ident", [P, P])
        mask_qk = sb("mask_qk", [P, P])
        tri = sb("tri", [P, 2 * P])
        mean32 = sb("mean32", [P, P])
        mean64 = sb("mean64", [P, P])
        mean512 = sb("mean512", [P, P])
        reset64 = sb("reset64", [P, TOK])
        headmask = sb("headmask", [P, 4])
        iota_t = sb("iota_t", [P, 64])
        glmask = sb("glmask", [P, 2])
        itmp = sb("itmp", [P, 66], I32)
        vec1 = sb("vec1", [P, P])
        vec2 = sb("vec2", [P, NV2])
        small = sb("small", [P, 256])
        AW = 21568
        arena = sb("arena", [P, AW])
        ps = ctx.enter_context(nc.psum_tensor("ps", [P, 8, 512], F32))

        def view(at, *shape):
            n = 1
            for s in shape:
                n *= s
            assert at + n <= AW, (at, shape)
            v = arena[:, at:at + n]
            if len(shape) == 2:
                v = v.rearrange("p (a b) -> p a b", b=shape[1])
            elif len(shape) == 3:
                v = v.rearrange("p (a b c) -> p a b c", b=shape[1], c=shape[2])
            return v

        def col(t, c):
            return t[:, c:c + 1]

        def bank(b, *shape):
            v = ps[:, b, :]
            n = 1
            for s in shape:
                n *= s
            v = v[:, 0:n]
            if len(shape) == 2:
                v = v.rearrange("p (a b) -> p a b", b=shape[1])
            elif len(shape) == 3:
                v = v.rearrange("p (a b c) -> p a b c", b=shape[1], c=shape[2])
            return v

        uT = view(0, KT, TOK)

        w_ready = [sem(f"w_ready{s}") for s in range(SLOTS)]
        w_used = sem("w_used")

        def load_tile(sp, T, rnd, src, by_rows=False):
            s = T % SLOTS
            rounds = rnd + T // SLOTS
            number = rounds * SLOTS + s
            sp.wait_ge(w_used, number + 1)
            sp.sem_inc(sem("slots_taken"), 1)
            if by_rows:
                dst = ring[:, s, :].rearrange("p (j n) -> p j n", n=D)
                src = src.rearrange("(j p) n -> p j n", p=P)
            else:
                dst = ring[:, s, :].rearrange("p (k n) -> p k n", n=W)
                src = src.rearrange("(k p) n -> p k n", p=P)
            sp.dma_start(dst, src).then_inc(w_ready[s], 16)

        def skip_tile(sp, T, rnd):
            s = T % SLOTS
            sp.wait_ge(w_used, (rnd + T // SLOTS) * SLOTS + s + 1)
            sp.sem_inc(w_ready[s], 16)

        def landed(pe, T, rnd):
            pe.wait_ge(w_ready[T % SLOTS], (rnd + T // SLOTS + 1) * 16)

        def multiplied(eng, T, rnd):
            eng.wait_ge(w_used, (rnd + T // SLOTS + 1) * SLOTS + T % SLOTS + 1)

        def wcols(T):
            return ring[:, T % SLOTS, :].rearrange("p (k n) -> p k n", n=W)

        def wrows(T):
            return ring[:, T % SLOTS, :].rearrange("p (j n) -> p j n", n=D)

        T_ADA = 0
        T_WIN1 = 24
        T_WOUT1 = T_WIN1 + len(WIN1_FEATURE) + len(WIN1_TOKEN)
        T_MOE = T_WOUT1 + 4
        T_L = T_MOE + 12 * NE
        L_FFN1 = T_L
        L_U5 = L_FFN1 + 3 * NCH
        L_Z = L_U5 + 4
        L_XBC = L_Z + 8
        L_GA = L_XBC + 12
        L_GLU = L_GA + 8
        L_BB = L_GLU + 8
        L_BA = L_BB + 4
        L_WOUT = L_BA + 8
        L_FFN2 = L_WOUT + 4
        L_PAD = L_FFN2 + 3 * NCH
        NPAD = -(L_PAD - T_L) % SLOTS
        ROUNDS = (L_PAD + NPAD - T_L) // SLOTS

        def ffn_loads(sp, T0, rnd, gate, up, down, n_chunks):
            def gu(T, c, r):
                load_tile(sp, T, r, gate(c))
                load_tile(sp, T + 1, r, up(c))
            gu(T0, 0, rnd)
            loops = (n_chunks - 1) // 4
            with sp.Fori(0, loops) as i:
                for c in range(4):
                    gu(T0 + 2 + 3 * c, i * 4 + c + 1, rnd + i)
                    load_tile(sp, T0 + 4 + 3 * c, rnd + i, down(i * 4 + c), True)
            for c in range(4 * loops, n_chunks):
                if c + 1 < n_chunks:
                    gu(T0 + 2 + 3 * c, c + 1, rnd)
                load_tile(sp, T0 + 4 + 3 * c - (2 if c + 1 == n_chunks else 0), rnd, down(c), True)

        def sp_program(sp):
            sp.sem_inc(w_used, SLOTS)
            sp.dma_start(x[:], a["x"].rearrange("a (t p) d -> p (a t) d", p=P)).then_inc(sem("x_in"), 16)
            with sp.Fori(0, 2) as i:
                for t in range(12):
                    load_tile(sp, T_ADA + t, i, a["ada_w"][0, :, bass.ds(i * 3072 + t * W, W)])
            T = T_WIN1
            for c0 in WIN1_FEATURE + WIN1_TOKEN:
                load_tile(sp, T, 0, a["w_in"][0, :, c0:c0 + W])
                T += 1
            for n in range(4):
                load_tile(sp, T, 0, a["w_out"][0, :, n * W:(n + 1) * W])
                T += 1
            if upto < 2:
                return
            up = a["exp_w_up"].rearrange("a e k n -> (a e) k n")
            dn = a["exp_w_down"].rearrange("a e k n -> (a e) k n")

            def expert_pass(w):
                with sp.Fori(0, NE // 2) as i:
                    for n in range(2):
                        e = i * 2 + n
                        for k, (part, c) in enumerate(EXPERT_TILES):
                            T, rnd = T_MOE + SLOTS * n + k, w * NE + i * 2
                            if part == "down":
                                load_tile(sp, T, rnd, dn[e, c * W:(c + 1) * W, :], True)
                            else:
                                c0 = c * W + (D if part == "up" else 0)
                                load_tile(sp, T, rnd, up[e, :, c0:c0 + W])
            expert_pass(0)
            passes = passes_of(sp)
            with sp.If(passes > 1):
                with sp.Fori(1, passes) as w:
                    expert_pass(w)
            if upto < 3:
                return
            nl = LAYERS
            with sp.Fori(0, nl) as li:
                r = li * ROUNDS + (passes - 1) * NE

                def ffn(T0, name):
                    ffn_loads(sp, T0, r,
                              lambda c: a[f"{name}_w_gate_2"][li, :, bass.ds(c * W, W)],
                              lambda c: a[f"{name}_w_up_2"][li, :, bass.ds(c * W, W)],
                              lambda c: a[f"{name}_w_down_2"][li, bass.ds(c * W, W), :], NCH)
                ffn(L_FFN1, "ffn1")
                T = L_U5
                win = a["w_in_2"][li]
                for c0 in ([U52 + n * W for n in range(4)] + [Z2 + n * W for n in range(8)]
                           + [XBC2 + n * W for n in range(12)] + [GA2 + n * W for n in range(8)]):
                    load_tile(sp, T, r, win[:, c0:c0 + W])
                    T += 1
                for n in range(4):
                    for half in range(2):
                        load_tile(sp, T, r, a["s5_w_glu_2"][li, :, half * D + n * W:half * D + (n + 1) * W])
                        T += 1
                for n in range(4):
                    load_tile(sp, T, r, a["w_branch_b_2"][li, :, n * W:(n + 1) * W])
                    T += 1
                for n in range(4):
                    for half in range(2):
                        load_tile(sp, T, r, a["w_branch_a_2"][li, half * D:(half + 1) * D, n * W:(n + 1) * W])
                        T += 1
                for n in range(4):
                    load_tile(sp, T, r, a["w_out_2"][li, :, n * W:(n + 1) * W])
                    T += 1
                ffn(L_FFN2, "ffn2")
                for n in range(NPAD):
                    skip_tile(sp, L_PAD + n, r)

        xn = view(4096, TT, D)
        ss = small[:, 0:4]
        eps = small[:, 249:250]
        one = small[:, 250:251]
        zero = small[:, 253:254]

        def pre_norm_act(act, n):
            act.wait_ge(sem("x_new"), n + 1)
            for t in range(TT):
                nc.scalar.activation(xn[:, t, :], x[:, t, :], ACT.Square, accum_out=ss[:, t:t + 1])
            act.drain()
            nc.scalar.activation(ss[:, 2:4], ss[:, 0:2], ACT.Sqrt, bias=eps, scale=1.0 / D).then_inc(
                sem("x_rms"), 1)

        def pre_norm_dve(dve, n):
            dve.wait_ge(sem("x_rms"), n + 1)
            nc.vector.reciprocal(ss[:, 2:4], ss[:, 2:4])
            dve.drain()
            for t in range(TT):
                nc.vector.tensor_scalar(xn[:, t, :], x[:, t, :], ss[:, 2 + t:3 + t], None,
                                        ALU.mult).then_inc(sem("x_normed"), 1)

        def pre_norm_pe(pe, n):
            for t in range(TT):
                pe.wait_ge(sem("x_normed"), TT * n + t + 1)
                for k in range(KT):
                    ins = nc.tensor.transpose(bank(4 + k // 2, 2, TOK)[:, k % 2, t * P:(t + 1) * P],
                                              xn[:, t, k * P:(k + 1) * P], ident[:])
            ins.then_inc(sem("x_turned"), 1)

        def pre_norm_out(dve, n, gain, shift=None):
            dve.wait_ge(sem("x_turned"), n + 1)
            for k in range(KT):
                src = bank(4 + k // 2, 2, TOK)[:, k % 2, :]
                if shift is None:
                    ins = nc.vector.tensor_scalar(uT[:, k, :], src, gain(k), None, ALU.mult)
                else:
                    ins = nc.vector.tensor_scalar(uT[:, k, :], src, gain(k), shift(k), ALU.mult, ALU.add)
            ins.then_inc(sem("u_ready"), 1)

        y_ps = ps[:, 0:4, :].rearrange("p (t h) n -> p t (h n)", t=TT)

        def post_norm_act(act, T_last, rnd):
            multiplied(act, T_last, rnd)
            for t in range(TT):
                nc.scalar.activation(xn[:, t, :], y_ps[:, t, :], ACT.Square, accum_out=ss[:, t:t + 1])
            act.drain()
            nc.scalar.activation(ss[:, 2:4], ss[:, 0:2], ACT.Sqrt, bias=eps, scale=1.0 / D).then_inc(
                sem("branch_rms"), 1)

        def post_norm_dve(dve, p, coef):
            dve.wait_ge(sem("branch_rms"), p + 1)
            nc.vector.reciprocal(ss[:, 2:4], ss[:, 2:4])
            dve.drain()
            nc.vector.tensor_scalar(ss[:, 2:4], ss[:, 2:4], coef, None, ALU.mult)
            dve.drain()
            dve.wait_ge(sem("post_gain_in"), (p + 1) * 16)
            for t in range(TT):
                nc.vector.scalar_tensor_tensor(out=xn[:, t, :], in0=y_ps[:, t, :], scalar=ss[:, 2 + t:3 + t],
                                               in1=post_gain[:], op0=ALU.mult, op1=ALU.mult)
            dve.drain()
            nc.vector.tensor_tensor(x[:], x[:], xn, ALU.add).then_inc(sem("x_new"), 1)

        def feature_tile(pe, T, rnd, b, rhs, part=None):
            landed(pe, T, rnd)
            w = wcols(T)
            for m in range(2):
                for k in range(KT):
                    ins = nc.tensor.matmul(bank(b, 2, TOK)[:, m, :], w[:, k, m * P:(m + 1) * P], rhs[:, k, :],
                                           start=(k == 0 and (part is None or (part == 0 and m == 0))),
                                           stop=(k == KT - 1 and part != 0),
                                           skip_group_check=part is not None)
            return ins.then_inc(w_used, 1)

        def token_tile(pe, T, rnd, outs, lhs):
            landed(pe, T, rnd)
            w = wcols(T)
            for t in range(TT):
                for k in range(KT):
                    ins = nc.tensor.matmul(outs[t], lhs[:, k, t * P:(t + 1) * P], w[:, k, :],
                                           start=(k == 0), stop=(k == KT - 1))
            return ins.then_inc(w_used, 1)

        def constants(pool):
            g = nc.gpsimd
            g.memset(ident[:], 0.0)
            g.memset(mask_qk[:], 0.0)
            g.memset(tri[:], 1.0)
            g.memset(mean32[:], 0.0)
            g.memset(mean64[:], 0.0)
            g.memset(mean512[:], 1.0 / 512)
            g.memset(reset64[:], 1.0)
            g.memset(headmask[:], 0.0)
            pool.drain()
            g.affine_select(out=ident[:], in_=ident[:], compare_op=ALU.not_equal, fill=1.0, base=0,
                            pattern=[[-1, P]], channel_multiplier=1)
            g.affine_select(out=mask_qk[:], in_=mask_qk[:], compare_op=ALU.is_ge, fill=NEG, base=0,
                            pattern=[[-1, P]], channel_multiplier=1)
            g.affine_select(out=tri[:, 0:P], in_=tri[:, 0:P], compare_op=ALU.is_ge, fill=0.0, base=0,
                            pattern=[[1, P]], channel_multiplier=-1)
            for i in range(4):
                r = slice(32 * i, 32 * i + 32)
                g.memset(mean32[r, r], 1.0 / 32)
                pool.drain()
                g.memset(headmask[r, i:i + 1], 1.0)
                pool.drain()
            for i in range(2):
                r = slice(64 * i, 64 * i + 64)
                g.memset(mean64[r, r], 1.0 / 64)
                pool.drain()
            g.memset(reset64[:].rearrange("p (c t) -> p c t", t=64)[:, :, 0:1], 0.0)
            g.iota(itmp[:, 0:64], pattern=[[1, 64]], base=0, channel_multiplier=0)
            g.iota(itmp[:, 64:65], pattern=[[0, 1]], base=0, channel_multiplier=1)
            pool.drain()
            g.tensor_copy(iota_t[:], itmp[:, 0:64]).then_inc(sem("consts"), 1)

        def glmask_dve(dve):
            nc.vector.tensor_scalar(itmp[:, 65:66], itmp[:, 64:65], 4, None, ALU.arith_shift_right)
            dve.drain()
            nc.vector.tensor_scalar(itmp[:, 65:66], itmp[:, 65:66], 1, None, ALU.bitwise_and)
            dve.drain()
            nc.vector.tensor_copy(glmask[:, 1:2], itmp[:, 65:66])
            dve.drain()
            nc.vector.tensor_scalar(glmask[:, 0:1], glmask[:, 1:2], -1.0, 1.0, ALU.mult, ALU.add)

        stage = view(20480, P)
        cond_b = view(8192, KT, P)
        gmod = view(18432, 2, D)
        QK = view(4096, 8, TOK)
        SQ = view(6144, 8, TOK)
        C_in = view(8192, 2, TOK)
        CR_s = view(8704, 2, TOK)
        DX_c = view(9216, 2, TOK)
        DG_g = view(9728, 2, TOK)
        V_tok = view(10240, 3, TT, W)
        WT = view(11776, 8, 384)
        S = view(14848, 4, 384)
        yT = view(16384, KT, TOK)
        hid_flat = ffn_buf[:, 0:1024]
        gat_flat = ffn_buf[:, 1024:2048]
        wg2 = hid_flat[:, 0:128]
        wcg = hid_flat[:, 128:256].rearrange("p (k n) -> p k n", n=16)
        wbd = hid_flat[:, 256:768].rearrange("p (w t n) -> p w t n", w=2, t=2)
        lamv = hid_flat[:, 768:896].rearrange("p (a b) -> p a b", b=32)
        router = gat_flat[:, 0:256].rearrange("p (k n) -> p k n", n=NE)
        routb = gat_flat[:, 256:288]
        N_SMALL1 = 0

        def small_loads_1(pool):
            dma = pool.dma_start
            s = sem("vec1_in")
            cnt = 0

            def rows(name, src, n):
                nonlocal cnt
                dma(stage[V1[name]:V1[name] + n, :], src).then_inc(s, 16)
                cnt += 16

            pool.wait_ge(sem("zeroed"), 1)
            for name in ("norm1_g", "norm2_g", "c"):
                rows(name, a[name].rearrange("a (r p) -> (a r) p", p=P), 8)
            ab = a["ada_b"].rearrange("a (s r p) -> (a s) r p", r=8, p=P)
            for n, j in (("sh0", 0), ("sc0", 1), ("sh1", 3), ("sc1", 4)):
                rows(n, ab[j], 8)
            rows("d_conv_w", a["d_conv_w"].rearrange("a k (r p) -> (a k r) p", p=P), 8)
            for name in ("d_conv_b", "d_b_a", "d_b_x", "d_lambda"):
                rows(name, a[name].rearrange("a (r p) -> (a r) p", p=P), 2)
            rows("c_b_g", a["c_b_g"], 1)
            for name, n in (("a_q_gain", 32), ("a_k_gain", 32), ("b_q_gain", 64), ("b_k_gain", 64),
                            ("a_out_gain", 64), ("c_out_gain", 64)):
                for j in range(P // n):
                    r = V1[name]
                    dma(stage[r:r + 1, j * n:(j + 1) * n], a[name]).then_inc(s, 16)
                    cnt += 16
            assert cnt == VEC1_IN
            dma(gmod[:, 0, :], bcast(a["ada_b"][0:1, 2048:3072])).then_inc(sem("gmod_in"), 16)
            dma(gmod[:, 1, :], bcast(a["ada_b"][0:1, 5120:6144])).then_inc(sem("gmod_in"), 16)
            s = sem("small1_in")
            dma(wg2[0:16, :], a["c_w_g2"][0]).then_inc(s, 16)
            dma(wcg, a["w_in"][0, :, CG:CG + 16].rearrange("(k p) n -> p k n", p=P)).then_inc(s, 16)
            for wi, name in enumerate(("d_w_a", "d_w_x")):
                for b in range(4):
                    r = slice(64 * (b % 2), 64 * (b % 2) + 64)
                    dma(wbd[r, wi, b // 2, r], a[name][0, b]).then_inc(s, 16)
            for j, name in enumerate(("a_lam_q1", "a_lam_k1", "a_lam_q2", "a_lam_k2")):
                dma(lamv[:, j, :], bcast(a[name])).then_inc(s, 16)
            dma(router, a["router_w"][0].rearrange("(k p) n -> p k n", p=P)).then_inc(s, 16)
            dma(routb, bcast(a["router_b"])).then_inc(s, 16)

        VEC1_IN = 16 * (3 + 4 + 1 + 4 + 1 + 2 * 4 + 4 * 2)
        SMALL1_IN = 16 * (1 + 1 + 8 + 4 + 2)

        def bcast(src):
            return src.to_broadcast([P, src.shape[1]])

        modc = small[:, 16:48]

        def mod_dve(dve):
            nc.vector.memset(stage, 0.0)
            nc.vector.memset(hid_flat[:, 256:768], 0.0)
            dve.drain()
            nc.vector.memset(eps, EPS).then_inc(sem("modc_done"), 1)
            nc.vector.memset(zero, 0.0).then_inc(sem("gmod_done"), 1)
            nc.vector.memset(small[:, 254:255], 0.0).then_inc(sem("stage_used"), 1)
            nc.vector.memset(one, 1.0).then_inc(sem("zeroed"), 1)
            dve.wait_ge(sem("consts"), 1)
            dve.wait_ge(sem("vec1_turned"), 1)
            nc.vector.tensor_copy(vec1[:, 0:NV1], bank(0, P)[:, 0:NV1]).then_inc(sem("vec1_ready"), 1)
            dve.wait_ge(sem("cond_ready"), 1)
            nc.vector.tensor_copy(cond_b, small[:, 8:16].unsqueeze(2).to_broadcast([P, KT, P])).then_inc(
                sem("cond_rows"), 1)
            dve.wait_ge(sem("gmod_in"), 32)
            with dve.Fori(0, 2) as i:
                multiplied(dve, T_ADA + 7, i)
                nc.vector.tensor_tensor(modc[:, bass.ds(i * 16, 16)], bank(0, 16),
                                        vec1[:, bass.ds(V1["sh0"] + i * 16, 16)], ALU.add).then_inc(
                                            sem("modc_done"), 1)
                multiplied(dve, T_ADA + 11, i)
                g = gmod[:, i, :]
                nc.vector.tensor_tensor(g, g, ps[:, 2:4, :].rearrange("p a b -> p (a b)"), ALU.add).then_inc(
                    sem("gmod_done"), 1)
            dve.drain()
            for i, name in enumerate(("norm1_g", "norm2_g")):
                c = modc[:, 16 * i + 8:16 * i + 16]
                ins = nc.vector.scalar_tensor_tensor(out=c, in0=c, scalar=1.0, in1=vec1[:, V1[name]:V1[name] + 8],
                                                     op0=ALU.add, op1=ALU.mult)
            dve.drain()

        def mod_act(act):
            act.wait_ge(sem("vec1_ready"), 1)
            nc.scalar.activation(small[:, 8:16], vec1[:, V1["c"]:V1["c"] + 8], ACT.Silu).then_inc(
                sem("cond_ready"), 1)

        def mod_pe(pe):
            pe.wait_ge(sem("consts"), 1)
            pe.wait_ge(sem("vec1_in"), VEC1_IN)
            nc.tensor.transpose(bank(0, P), stage, ident[:]).then_inc(sem("vec1_turned"), 1)
            pe.wait_ge(sem("cond_rows"), 1)
            with pe.Fori(0, 2) as i:
                pe.wait_ge(sem("modc_done"), i + 1)
                for t in range(8):
                    landed(pe, T_ADA + t, i)
                    w = wcols(T_ADA + t)
                    for m in range(2):
                        c = t * 2 + m
                        for k in range(KT):
                            ins = nc.tensor.matmul(bank(0, 16)[:, c:c + 1], w[:, k, m * P:(m + 1) * P],
                                                   small[:, 8 + k:9 + k], start=(k == 0), stop=(k == KT - 1))
                    ins.then_inc(w_used, 1)
                pe.wait_ge(sem("gmod_done"), i + 1)
                for t in range(4):
                    landed(pe, T_ADA + 8 + t, i)
                    w = wcols(T_ADA + 8 + t)
                    for k in range(KT):
                        ins = nc.tensor.matmul(bank(2 + t // 2, 2, W)[:, t % 2, :], cond_b[:, k, :], w[:, k, :],
                                               start=(k == 0), stop=(k == KT - 1))
                    ins.then_inc(w_used, 1)

        col1 = {n: vec1[:, V1[n]:V1[n] + 1] for n in V1}
        glow = view(20608, TOK)
        NF = len(WIN1_FEATURE)

        def win1_pe(pe):
            pe.wait_ge(sem("u_ready"), 1)
            for n in range(NF):
                feature_tile(pe, T_WIN1 + n, 0, n, uT)
            for n in range(3):
                pe.wait_ge(sem("qk_raw"), n + 1)
                token_tile(pe, T_WIN1 + NF + n, 0, [bank(n, 2, W)[:, t, :] for t in range(TT)], uT)
            pe.wait_ge(sem("qk_raw"), 4)
            pe.wait_ge(sem("small1_in"), SMALL1_IN)
            for k in range(KT):
                ins = nc.tensor.matmul(bank(3, TOK)[0:16, :], wcg[:, k, :], uT[:, k, :],
                                       start=(k == 0), stop=(k == KT - 1))
            ins.then_inc(sem("glow_mm"), 1)

        def win1_dve(dve):
            for n in range(4):
                multiplied(dve, T_WIN1 + n, 0)
                nc.vector.tensor_copy(QK[:, 2 * n:2 * n + 2, :], bank(n, 2, TOK)).then_inc(sem("qk_raw"), 1)
            multiplied(dve, T_WIN1 + 4, 0)
            nc.vector.tensor_copy(C_in, bank(4, 2, TOK)).then_inc(sem("c_raw"), 1)
            multiplied(dve, T_WIN1 + 6, 0)
            cw = V1["d_conv_w"]
            for t in range(2):
                nc.vector.tensor_scalar(DX_c[:, t, :], bank(6, 2, TOK)[:, t, :], col(vec1, cw + 6 + t),
                                        col(vec1, V1["d_conv_b"] + t), ALU.mult, ALU.add)
            for lag in (1, 2, 3):
                dve.drain()
                for t in range(2):
                    ins = nc.vector.scalar_tensor_tensor(
                        out=DX_c[:, t, lag:], in0=bank(6, 2, TOK)[:, t, 0:TOK - lag],
                        scalar=col(vec1, cw + 2 * (3 - lag) + t), in1=DX_c[:, t, lag:], op0=ALU.mult, op1=ALU.add)
            ins.then_inc(sem("dx_conv"), 1)
            for n in range(3):
                multiplied(dve, T_WIN1 + NF + n, 0)
                nc.vector.tensor_copy(V_tok[:, n, :, :], bank(n, 2, W)).then_inc(sem("v_tok"), 1)
            dve.wait_ge(sem("glow_mm"), 1)
            nc.vector.tensor_copy(glow[0:16, :], bank(3, TOK)[0:16, :]).then_inc(sem("glow"), 1)

        def win1_act(act):
            for n in range(4):
                act.wait_ge(sem("qk_raw"), n + 1)
                nc.scalar.activation(SQ[:, 2 * n:2 * n + 2, :], QK[:, 2 * n:2 * n + 2, :], ACT.Square).then_inc(
                    sem("qk_squares"), 1)
            multiplied(act, T_WIN1 + 5, 0)
            nc.scalar.activation(CR_s, bank(5, 2, TOK), ACT.Silu).then_inc(sem("act_gates"), 1)
            multiplied(act, T_WIN1 + 7, 0)
            nc.scalar.activation(DG_g, bank(7, 2, TOK), ACT.Gelu_apprx_tanh).then_inc(sem("act_gates"), 1)

        mx = small[:, 64:72]
        nmx = small[:, 72:80]
        sums = small[:, 80:88]
        lam = small[:, 88:92]
        ROUNDS_A = 3
        HEADS_OF = ((0, 1), (2, 3), (4, 5, 6, 7))

        def qk_norm_pe(pe):
            pe.wait_ge(sem("qk_squares"), 4)
            pe.wait_ge(sem("c_raw"), 1)
            pe.wait_ge(sem("act_gates"), 2)
            pe.wait_ge(sem("dx_conv"), 1)
            for t in range(8):
                ins = nc.tensor.matmul(bank(4 + t // 2, 2, TOK)[:, t % 2, :], mean32[:] if t < 4 else mean64[:],
                                       SQ[:, t, :], start=True, stop=True)
            ins.then_inc(sem("qk_mean"), 1)

        def qk_norm_dve(dve):
            dve.wait_ge(sem("small1_in"), SMALL1_IN)
            nc.vector.tensor_tensor(lamv[:, 0, :], lamv[:, 0, :], lamv[:, 1, :], ALU.mult)
            nc.vector.tensor_tensor(lamv[:, 2, :], lamv[:, 2, :], lamv[:, 3, :], ALU.mult)
            dve.drain()
            nc.vector.tensor_reduce(lam[:, 0:1], lamv[:, 0, :], AX, ALU.add)
            nc.vector.tensor_reduce(lam[:, 1:2], lamv[:, 2, :], AX, ALU.add).then_inc(sem("lam_sums"), 1)
            dve.wait_ge(sem("qk_rms"), 1)
            nc.vector.reciprocal(SQ, SQ)
            dve.drain()
            for n, g in enumerate(("a_q_gain", "a_k_gain", "b_q_gain", "b_k_gain")):
                t = slice(2 * n, 2 * n + 2)
                ins = nc.vector.scalar_tensor_tensor(out=QK[:, t, :], in0=QK[:, t, :], scalar=col1[g],
                                                     in1=SQ[:, t, :], op0=ALU.mult, op1=ALU.mult)
            ins.then_inc(sem("qk_ready"), 1)
            dve.wait_ge(sem("lam_exps"), 1)
            nc.vector.tensor_tensor(lam[:, 3:4], lam[:, 1:2], lam[:, 0:1], ALU.subtract)
            dve.drain()
            nc.vector.tensor_scalar(lam[:, 3:4], lam[:, 3:4], -LAM0, None, ALU.add)
            dve.drain()

        def lam_act(act):
            act.wait_ge(sem("lam_sums"), 1)
            nc.scalar.activation(lam[:, 0:2], lam[:, 0:2], ACT.Exp).then_inc(sem("lam_exps"), 1)
            act.wait_ge(sem("qk_mean"), 1)
            nc.scalar.activation(SQ.rearrange("p a b -> p (a b)"), ps[:, 4:8, :].rearrange("p a b -> p (a b)"),
                                 ACT.Sqrt, bias=eps).then_inc(sem("qk_rms"), 1)

        def attention_pe(pe):
            pe.wait_ge(sem("qk_ready"), 1)
            pe.wait_ge(sem("v_tok"), 3)
            pe.wait_ge(sem("glow"), 1)
            for r in range(3):
                if r:
                    pe.wait_ge(sem("scores_read"), r)
                for i in range(4):
                    rows, qt, kt = ((slice(32 * i, 32 * i + 32), r, 2 + r) if r < 2 else
                                    (slice(64 * (i % 2), 64 * (i % 2) + 64), 4 + i // 2, 6 + i // 2))
                    nc.tensor.matmul(bank(i, 384)[:, 0:P], QK[rows, qt, 0:P], QK[rows, kt, 0:P],
                                     start=True, stop=True)
                    ins = nc.tensor.matmul(bank(i, 384)[:, P:384], QK[rows, qt, P:TOK], QK[rows, kt, :],
                                           start=True, stop=True)
                ins.then_inc(sem("scores"), 1)
                pe.wait_ge(sem("probs"), r + 1)
                if r == 0:
                    pe.wait_ge(sem("qk_rms"), 1)
                for hh in range(len(HEADS_OF[r])):
                    m = hh * (2 if r < 2 else 1)
                    for part in range(3):
                        c = slice(P * part, P * part + P)
                        ins = nc.tensor.transpose(bank(4 + hh, 384)[:, c], S[:, m, c], ident[:])
                ins.then_inc(sem("probs_turned"), 1)
            pe.wait_ge(sem("wt_ready"), 3)
            for h in range(8):
                j, hh = h // 4, h % 4
                o = bank(j, 2, TOK)[64 * (h % 2):64 * (h % 2) + 64, hh // 2, :]
                v = slice(64 * hh, 64 * hh + 64)
                nc.tensor.matmul(o, V_tok[:, j, 0, v], WT[:, h, 0:TOK], start=True, stop=False,
                                 skip_group_check=True)
                ins = nc.tensor.matmul(o[:, P:TOK], V_tok[:, j, 1, v], WT[:, h, TOK:384], start=False,
                                       stop=True, skip_group_check=True)
            ins.then_inc(sem("attended"), 1)

        def attention_dve(dve):
            for r in range(3):
                dve.wait_ge(sem("scores"), r + 1)
                mask = mask_qk[:].unsqueeze(1).to_broadcast([P, 4, P])
                nc.vector.tensor_tensor(S[:, :, 0:P], ps[:, 0:4, 0:P], mask, ALU.add)
                nc.vector.tensor_copy(S[:, :, P:TOK], ps[:, 0:4, P:TOK])
                nc.vector.tensor_tensor(S[:, :, TOK:384], ps[:, 0:4, TOK:384], mask, ALU.add).then_inc(
                    sem("scores_read"), 1)
                dve.drain()
                nc.vector.tensor_reduce(mx[:, 0:4], S[:, :, 0:P], AX, ALU.max)
                nc.vector.tensor_reduce(mx[:, 4:8], S[:, :, P:384], AX, ALU.max)
                dve.drain()
                scale = (32 if r < 2 else 64) ** -0.5
                nc.vector.tensor_scalar(nmx, mx, -scale, None, ALU.mult).then_inc(sem("row_max"), 1)
                dve.wait_ge(sem("exps"), r + 1)
                nc.vector.reciprocal(sums, sums)
                dve.drain()
                if r < 2:
                    s2 = sums.rearrange("p (q a i) -> p q a i", q=2, i=2)[:, :, :, 1]
                    nc.vector.tensor_scalar(s2, s2, lam[:, 3:4], None, ALU.mult)
                    dve.drain()
                for q, c in ((0, slice(0, P)), (1, slice(P, 384))):
                    for i in range(4):
                        ins = nc.vector.tensor_scalar(S[:, i, c], S[:, i, c], sums[:, 4 * q + i:4 * q + i + 1],
                                                      None, ALU.mult)
                if r < 2:
                    dve.drain()
                    ins = nc.vector.tensor_tensor(S[:, 0:4:2, :], S[:, 0:4:2, :], S[:, 1:4:2, :], ALU.add)
                ins.then_inc(sem("probs"), 1)
                h0, n = HEADS_OF[r][0], len(HEADS_OF[r])
                dve.wait_ge(sem("probs_turned"), r + 1)
                nc.vector.tensor_copy(WT[:, h0:h0 + n, :], ps[:, 4:4 + n, 0:384]).then_inc(sem("wt_ready"), 1)
            dve.wait_ge(sem("attended"), 1)
            nc.vector.tensor_copy(yT[:, 2:4, :], bank(1, 2, TOK))
            nc.vector.tensor_copy(QK[:, 0:2, :], bank(0, 2, TOK)).then_inc(sem("oa_raw"), 1)
            dve.wait_ge(sem("oa_rms"), 1)
            nc.vector.reciprocal(QK[:, 4:6, :], QK[:, 4:6, :])
            nc.vector.tensor_scalar(lam[:, 0:1], col1["a_out_gain"], 1.0 - LAM0, None, ALU.mult)
            dve.drain()
            nc.vector.scalar_tensor_tensor(out=yT[:, 0:2, :], in0=QK[:, 0:2, :], scalar=lam[:, 0:1],
                                           in1=QK[:, 4:6, :], op0=ALU.mult, op1=ALU.mult)
            dve.drain()

        def attention_act(act):
            for r in range(3):
                act.wait_ge(sem("row_max"), r + 1)
                scale = (32 if r < 2 else 64) ** -0.5
                for q, c in ((0, slice(0, P)), (1, slice(P, 384))):
                    for i in range(4):
                        j = 4 * q + i
                        ins = nc.scalar.activation(S[:, i, c], S[:, i, c], ACT.Exp, bias=nmx[:, j:j + 1],
                                                   scale=scale, accum_out=sums[:, j:j + 1])
                ins.then_inc(sem("exps"), 1)
            act.wait_ge(sem("oa_raw"), 1)
            nc.scalar.activation(QK[:, 2:4, :], QK[:, 0:2, :], ACT.Square).then_inc(sem("oa_squares"), 1)
            act.wait_ge(sem("oa_mean"), 1)
            nc.scalar.activation(QK[:, 4:6, :], bank(2, 2, TOK), ACT.Sqrt, bias=eps).then_inc(sem("oa_rms"), 1)

        def oa_mean_pe(pe):
            pe.wait_ge(sem("oa_squares"), 1)
            for t in range(2):
                ins = nc.tensor.matmul(bank(2, 2, TOK)[:, t, :], mean64[:], QK[:, 2 + t, :], start=True, stop=True)
            ins.then_inc(sem("oa_mean"), 1)

        NCK = TOK // 64
        E = view(4096, 4, TOK)
        QE = view(5120, 2, TOK)
        KM = view(5632, 4, TOK)
        KD = view(6656, TOK)
        KDT = view(6912, 2, P)
        SBD = view(7168, 3, 4, 64)
        G = view(7936, TOK)
        attS = view(14848, 2, 4, P)
        St = view(16128, 3, 64)
        OC = view(11776, 2, TOK)
        OC2 = view(12288, 2, TOK)
        RG = view(12800, 2, 2, TOK)
        clam = small[:, 92:98]

        def chunks(v):
            return v.rearrange("p (c t) -> p c t", t=64)

        def gla_dve(dve):
            dve.wait_ge(sem("gate_mm"), 1)
            nc.vector.tensor_scalar(G, bank(4, TOK), col1["c_b_g"], None, ALU.add).then_inc(sem("gate_raw"), 1)
            nc.vector.memset(attS, 0.0)
            dve.wait_ge(sem("gate_log"), 1)
            nc.vector.scalar_tensor_tensor(out=G, in0=G, scalar=0.0, in1=E[:, 1, :], op0=ALU.min,
                                           op1=ALU.subtract)
            dve.drain()
            nc.vector.tensor_scalar(G, G, 1.0 / 16, None, ALU.mult)
            dve.drain()
            nc.vector.tensor_tensor_scan(E[:, 0, :], reset64[:], G, 0.0, ALU.mult, ALU.add)
            dve.drain()
            b = chunks(E[:, 0, :])
            mid = b[:, :, 31:32].to_broadcast([P, NCK, 64])
            end = b[:, :, 63:64].to_broadcast([P, NCK, 64])
            nc.vector.tensor_tensor(chunks(E[:, 1, :]), b, mid, ALU.subtract)
            nc.vector.tensor_tensor(chunks(E[:, 2, :]), mid, b, ALU.subtract)
            nc.vector.tensor_tensor(chunks(E[:, 3, :]), end, b, ALU.subtract)
            dve.drain()
            nc.vector.tensor_scalar(E[:, 1:3, :], E[:, 1:3, :], 80.0, None, ALU.min).then_inc(sem("decays"), 1)
            dve.wait_ge(sem("decay_exps"), 1)
            for j in range(2):
                nc.vector.scalar_tensor_tensor(out=QE[:, j, :], in0=C_in[:, 0, :], scalar=32.0 ** -0.5,
                                               in1=E[:, j, :], op0=ALU.mult, op1=ALU.mult)
            for h in range(4):
                ins = nc.vector.scalar_tensor_tensor(out=KM[:, h, :], in0=C_in[:, 1, :], scalar=col(headmask, h),
                                                     in1=E[:, 2, :], op0=ALU.mult, op1=ALU.mult)
            nc.vector.tensor_tensor(KD, C_in[:, 1, :], E[:, 3, :], ALU.mult).then_inc(sem("keys"), 1)
            dve.wait_ge(sem("kd_turned"), 1)
            nc.vector.tensor_copy(KDT, bank(5, 2, P)).then_inc(sem("kdt"), 1)
            dve.wait_ge(sem("att"), 1)
            for par in range(2):
                r = slice(64 * par, 64 * par + 64)
                ins = nc.vector.tensor_tensor(
                    attS[r, :, :, r].rearrange("p t h i -> p h t i"), bank(6, 4, 2, 64)[r],
                    tri[r, r].unsqueeze(1).unsqueeze(1).to_broadcast([64, 4, 2, 64]), ALU.mult)
            ins.then_inc(sem("att_masked"), 1)
            dve.wait_ge(sem("updates"), 1)
            nc.vector.tensor_copy(St[:, 0, :], bank(7, 3, 64)[:, 0, :])
            for c in (1, 2):
                dve.drain()
                nc.vector.scalar_tensor_tensor(out=St[:, c, :], in0=St[:, c - 1, :],
                                               scalar=E[:, 0, 64 * c + 63:64 * c + 64],
                                               in1=bank(4 if c == 1 else 7, 3, 64)[:, c, :],
                                               op0=ALU.mult, op1=ALU.add)
            dve.drain()
            for c in range(3):
                ins = nc.vector.tensor_tensor(SBD[:, c, :, :], St[:, c, :].unsqueeze(1).to_broadcast([P, 4, 64]),
                                              headmask[:].unsqueeze(2).to_broadcast([P, 4, 64]), ALU.mult)
            ins.then_inc(sem("states"), 1)
            dve.wait_ge(sem("gla_out"), 1)
            for j in range(2):
                ins = nc.vector.tensor_copy(OC[:, j, :], bank(j, TOK))
            ins.then_inc(sem("oc_raw"), 1)
            lamc = vec1[:, V1["d_lambda"]:V1["d_lambda"] + 2]
            nc.vector.tensor_scalar(clam[:, 4:6], lamc, 0.0, None, ALU.min)
            dve.wait_ge(sem("oc_rms"), 1)
            nc.vector.reciprocal(OC2, OC2)
            dve.drain()
            nc.vector.scalar_tensor_tensor(out=OC, in0=OC, scalar=col1["c_out_gain"], in1=OC2,
                                           op0=ALU.mult, op1=ALU.mult)
            dve.drain()
            nc.vector.tensor_tensor(yT[:, 4:6, :], OC, CR_s, ALU.mult)

        def gla_act(act):
            act.wait_ge(sem("gate_raw"), 1)
            nc.scalar.activation(E[:, 1, :], G, ACT.Abs)
            act.drain()
            nc.scalar.activation(E[:, 1, :], E[:, 1, :], ACT.Exp, scale=-1.0)
            act.drain()
            nc.scalar.activation(E[:, 1, :], E[:, 1, :], ACT.Ln, bias=one).then_inc(sem("gate_log"), 1)
            act.wait_ge(sem("decays"), 1)
            nc.scalar.activation(E, E, ACT.Exp).then_inc(sem("decay_exps"), 1)
            act.wait_ge(sem("oc_raw"), 1)
            nc.scalar.activation(OC2, OC, ACT.Square).then_inc(sem("oc_squares"), 1)
            act.wait_ge(sem("oc_mean"), 1)
            nc.scalar.activation(OC2, bank(2, 2, TOK), ACT.Sqrt, bias=eps).then_inc(sem("oc_rms"), 1)
            nc.scalar.activation(clam[:, 0:2], vec1[:, V1["d_lambda"]:V1["d_lambda"] + 2], ACT.Abs)
            act.drain()
            nc.scalar.activation(clam[:, 2:4], clam[:, 0:2], ACT.Exp, scale=-1.0)
            act.drain()
            nc.scalar.activation(clam[:, 2:4], clam[:, 2:4], ACT.Ln, bias=one).then_inc(sem("clam_log"), 1)

        def gla_pe(pe):
            nc.tensor.matmul(bank(4, TOK), wg2[0:16, :], glow[0:16, :], start=True, stop=True).then_inc(
                sem("gate_mm"), 1)
            pe.wait_ge(sem("keys"), 1)
            for t in range(2):
                ins = nc.tensor.transpose(bank(5, 2, P)[:, t, :], KD[:, t * P:(t + 1) * P], ident[:])
            ins.then_inc(sem("kd_turned"), 1)
            for h in range(4):
                for c in range(NCK):
                    cs = slice(64 * c, 64 * c + 64)
                    ins = nc.tensor.matmul(bank(6, 4, 2, 64)[64 * (c % 2):64 * (c % 2) + 64, h, c // 2, :],
                                           KM[:, h, cs], QE[:, 1, cs], start=True, stop=True)
            ins.then_inc(sem("att"), 1)
            pe.wait_ge(sem("kdt"), 1)
            for c in range(3):
                r = slice(64 * (c % 2), 64 * (c % 2) + 64)
                for h in range(4):
                    ins = nc.tensor.matmul(bank(4 if c == 1 else 7, 3, 64)[32 * h:32 * h + 32, c, :],
                                           KDT[r, c // 2, 32 * h:32 * h + 32],
                                           V_tok[r, 2, c // 2, 64 * h:64 * h + 64], start=True, stop=True)
            ins.then_inc(sem("updates"), 1)
            pe.wait_ge(sem("att_masked"), 1)
            pe.wait_ge(sem("states"), 1)
            for hp in range(2):
                for h in (2 * hp, 2 * hp + 1):
                    for t in range(2):
                        nc.tensor.matmul(bank(hp, TOK)[64 * (h % 2):64 * (h % 2) + 64, t * P:(t + 1) * P],
                                         V_tok[:, 2, t, 64 * h:64 * h + 64], attS[:, t, h, :],
                                         start=(t == 0), stop=False, skip_group_check=True)
                for c in range(1, NCK):
                    cs = slice(64 * c, 64 * c + 64)
                    ins = nc.tensor.matmul(bank(hp, TOK)[:, cs],
                                           SBD[:, c - 1, 2 * hp:2 * hp + 2, :].rearrange("p h e -> p (h e)"),
                                           QE[:, 0, cs], start=False, stop=(c == NCK - 1), skip_group_check=True)
            ins.then_inc(sem("gla_out"), 1)
            pe.wait_ge(sem("oc_squares"), 1)
            for t in range(2):
                ins = nc.tensor.matmul(bank(2, 2, TOK)[:, t, :], mean64[:], OC2[:, t, :], start=True, stop=True)
            ins.then_inc(sem("oc_mean"), 1)

        def lru_pe(pe):
            for w in range(2):
                for t in range(2):
                    ins = nc.tensor.matmul(bank(5 + w, 2, TOK)[:, t, :], wbd[:, w, t, :], DX_c[:, t, :],
                                           start=True, stop=True)
            ins.then_inc(sem("lru_gates_mm"), 1)

        def lru_act(act):
            act.wait_ge(sem("lru_gates_mm"), 1)
            for w, b in enumerate(("d_b_a", "d_b_x")):
                for t in range(2):
                    ins = nc.scalar.activation(RG[:, w, t, :], bank(5 + w, 2, TOK)[:, t, :], ACT.Sigmoid,
                                               bias=col(vec1, V1[b] + t))
            ins.then_inc(sem("lru_gates"), 1)
            act.wait_ge(sem("log_a"), 1)
            nc.scalar.activation(OC2, RG[:, 0, :, :], ACT.Tanh, scale=-1.0)
            nc.scalar.activation(OC, RG[:, 0, :, :], ACT.Exp).then_inc(sem("lru_exps"), 1)
            act.wait_ge(sem("lru_var"), 1)
            nc.scalar.activation(OC2, OC2, ACT.Sqrt).then_inc(sem("lru_root"), 1)

        def lru_dve(dve):
            dve.wait_ge(sem("clam_log"), 1)
            nc.vector.tensor_tensor(clam[:, 4:6], clam[:, 4:6], clam[:, 2:4], ALU.subtract)
            dve.drain()
            nc.vector.tensor_scalar(clam[:, 4:6], clam[:, 4:6], 8.0, None, ALU.mult)
            dve.wait_ge(sem("lru_gates"), 1)
            dve.drain()
            for t in range(2):
                nc.vector.tensor_scalar(RG[:, 0, t, :], RG[:, 0, t, :], clam[:, 4 + t:5 + t], None, ALU.mult)
            nc.vector.tensor_tensor(RG[:, 1, :, :], RG[:, 1, :, :], DX_c, ALU.mult).then_inc(sem("log_a"), 1)
            dve.wait_ge(sem("lru_exps"), 1)
            nc.vector.tensor_tensor(RG[:, 0, :, :], OC, OC, ALU.mult)
            dve.drain()
            nc.vector.scalar_tensor_tensor(out=OC2, in0=RG[:, 0, :, :], scalar=1.0, in1=OC2, op0=ALU.add,
                                           op1=ALU.mult).then_inc(sem("lru_var"), 1)
            dve.wait_ge(sem("lru_root"), 1)
            nc.vector.tensor_tensor(RG[:, 1, :, :], RG[:, 1, :, :], OC2, ALU.mult)
            dve.drain()
            for t in range(2):
                nc.vector.tensor_tensor_scan(RG[:, 0, t, :], OC[:, t, :], RG[:, 1, t, :], 0.0, ALU.mult, ALU.add)
            dve.drain()
            nc.vector.tensor_tensor(yT[:, 6:8, :], RG[:, 0, :, :], DG_g, ALU.mult).then_inc(sem("yt1_ready"), 1)

        def wout1_pe(pe):
            pe.wait_ge(sem("yt1_ready"), 1)
            for n in range(4):
                token_tile(pe, T_WOUT1 + n, 0,
                           [bank(2 * t + n // 2, 2, W)[:, n % 2, :] for t in range(TT)], yT)

        def wout1_dve(dve, half):
            nc.vector.tensor_tensor(xn, y_ps, gmod[:, half, :].unsqueeze(1).to_broadcast([P, TT, D]), ALU.mult)
            dve.drain()
            nc.vector.tensor_tensor(x[:], x[:], xn, ALU.add).then_inc(sem("x_new"), 1)

        GB = view(4096, NE, TOK)
        b_up = view(12288, NE * 16)
        b_down = view(12800, D)
        b_up_rows = view(13824, 4, P)
        L = view(14336, TT, NE)
        R = view(14400, 5, TT, NE)
        gates = view(14720, TT, NE)
        gT = view(14848, TOK)
        m8 = small[:, 100:116].rearrange("p (t n) -> p t n", t=2)
        rs = small[:, 116:124].rearrange("p (t n) -> p t n", t=2)

        def moe_small_loads(pool):
            pool.wait_ge(sem("x_new"), 2)
            pool.dma_start(b_up_rows, a["exp_b_up"][0].rearrange("(j e) (m p) -> (e m) j p", j=4, p=P)
                           ).then_inc(sem("moe_small_in"), 16)
            pool.dma_start(b_down[0:NE, :], a["exp_b_down"][0]).then_inc(sem("moe_small_in"), 16)

        def passes_of(eng):
            eng.wait_ge(sem("passes"), 1)
            return eng.value_load(itmp[0:1, 65:66], min_val=1, max_val=PASSES)

        def router_pe(pe):
            pe.wait_ge(sem("moe_small_in"), 32)
            for j in range(4):
                ins = nc.tensor.transpose(bank(0, 4, P)[:, j, :], b_up_rows[:, j, :], ident[:])
            ins.then_inc(sem("bup_turned"), 1)
            pe.wait_ge(sem("u_ready"), 2)
            for t in range(TT):
                for k in range(KT):
                    ins = nc.tensor.matmul(bank(1, TT, NE)[:, t, :], uT[:, k, t * P:(t + 1) * P], router[:, k, :],
                                           start=(k == 0), stop=(k == KT - 1))
            ins.then_inc(sem("logits"), 1)
            for t in range(TT):
                for k in range(KT):
                    ins = nc.tensor.transpose(bank(4 + 2 * t + k // 4, 4, P)[:, k % 4, :],
                                              uT[:, k, t * P:(t + 1) * P], ident[:])
            ins.then_inc(sem("h_turned"), 1)
            pe.wait_ge(sem("routed"), 1)
            m = R[:, 1, :, :]
            o = bank(3, TT + 1, NE)
            nc.tensor.matmul(o[:, 0, :], tri[:, 0:P], m[:, 0, :], start=True, stop=True)
            nc.tensor.matmul(o[:, 1, :], tri[:, P:2 * P], m[:, 0, :], start=True, stop=False)
            nc.tensor.matmul(o[:, 1, :], tri[:, 0:P], m[:, 1, :], start=False, stop=True)
            nc.tensor.matmul(o[:, 2, :], tri[:, P:2 * P], m[:, 0, :], start=True, stop=False)
            nc.tensor.matmul(o[:, 2, :], tri[:, P:2 * P], m[:, 1, :], start=False, stop=True).then_inc(
                sem("ranks_mm"), 1)
            pe.wait_ge(sem("gates"), 1)
            for t in range(TT):
                ins = nc.tensor.transpose(bank(2, TOK)[0:NE, t * P:(t + 1) * P], gates[:, t, :], ident[:])
            ins.then_inc(sem("gates_turned"), 1)
            pe.wait_ge(sem("gates_t"), 1)
            for t in range(TT):
                for h in range(2):
                    nc.tensor.matmul(ps[:, 2 * t + h, :], gT[0:NE, t * P:(t + 1) * P],
                                     b_down[0:NE, 512 * h:512 * h + 512], start=True, stop=False,
                                     skip_group_check=True)

        def router_act(act):
            act.wait_ge(sem("shifted"), 1)
            nc.scalar.activation(R[:, 0, :, :], R[:, 0, :, :], ACT.Exp).then_inc(sem("logit_exps"), 1)
            act.wait_ge(sem("h_turned"), 1)
            nc.scalar.activation(xn.rearrange("p a b -> p (a b)"), ps[:, 4:8, :].rearrange("p a b -> p (a b)"),
                                 ACT.Copy).then_inc(sem("h_rows"), 1)

        def router_dve(dve):
            dve.wait_ge(sem("bup_turned"), 1)
            nc.vector.tensor_copy(b_up, bank(0, 512))
            dve.wait_ge(sem("logits"), 1)
            nc.vector.tensor_tensor(L, bank(1, TT, NE), routb.unsqueeze(1).to_broadcast([P, TT, NE]), ALU.add)
            dve.drain()
            for t in range(TT):
                nc.vector.max(m8[:, t, :], L[:, t, :])
            dve.drain()
            fourth = m8[:, :, 3:4].to_broadcast([P, TT, NE])
            nc.vector.tensor_tensor(R[:, 0, :, :], L, m8[:, :, 0:1].to_broadcast([P, TT, NE]),
                                    ALU.subtract).then_inc(sem("shifted"), 1)
            nc.vector.tensor_tensor(R[:, 1, :, :], L, fourth, ALU.is_gt)
            nc.vector.tensor_tensor(R[:, 2, :, :], L, fourth, ALU.is_equal)
            nc.vector.memset(R[:, 4, :, :], 1.0)
            dve.drain()
            nc.vector.tensor_reduce(rs[:, :, 0:1], R[:, 1, :, :], AX, ALU.add)
            for t in range(TT):
                nc.vector.tensor_tensor_scan(R[:, 3, t, :], R[:, 4, t, :], R[:, 2, t, :], 0.0, ALU.mult, ALU.add)
            dve.drain()
            nc.vector.tensor_tensor(R[:, 3, :, :], R[:, 3, :, :], rs[:, :, 0:1].to_broadcast([P, TT, NE]), ALU.add)
            dve.drain()
            nc.vector.tensor_scalar(R[:, 3, :, :], R[:, 3, :, :], float(TOPK), None, ALU.is_le)
            dve.drain()
            nc.vector.tensor_tensor(R[:, 2, :, :], R[:, 2, :, :], R[:, 3, :, :], ALU.mult)
            dve.drain()
            nc.vector.tensor_tensor(R[:, 1, :, :], R[:, 1, :, :], R[:, 2, :, :], ALU.add).then_inc(
                sem("routed"), 1)
            dve.drain()
            dve.wait_ge(sem("logit_exps"), 1)
            nc.vector.tensor_tensor(gates, R[:, 0, :, :], R[:, 1, :, :], ALU.mult)
            dve.drain()
            nc.vector.tensor_reduce(rs[:, :, 1:2], gates, AX, ALU.add)
            dve.drain()
            nc.vector.reciprocal(rs[:, :, 2:3], rs[:, :, 1:2])
            dve.drain()
            nc.vector.tensor_tensor(gates, gates, rs[:, :, 2:3].to_broadcast([P, TT, NE]), ALU.mult).then_inc(
                sem("gates"), 1)
            dve.drain()
            dve.wait_ge(sem("ranks_mm"), 1)
            o = bank(3, TT + 1, NE)
            nc.vector.tensor_tensor(rank[:, :, 0:NE], o[:, 0:TT, :], R[:, 1, :, :], ALU.mult)
            nc.vector.tensor_reduce(rs[:, 0, 0:1], o[:, TT, :], AX, ALU.max)
            nc.vector.tensor_copy(gate[:, :, 0:NE], gates)
            nc.vector.tensor_copy(gate[:, :, NE:NE + 1], gates[:, :, 0:1])
            dve.drain()
            nc.vector.tensor_scalar(rank[:, :, 0:NE], rank[:, :, 0:NE], -1.0, None, ALU.add)
            for k in range(1, PASSES):
                nc.vector.tensor_scalar(rs[:, 0, k:k + 1], rs[:, 0, 0:1], float(k * CAP), None, ALU.is_gt)
            dve.drain()
            nc.vector.tensor_scalar(rank[:, :, NE:NE + 1], rank[:, :, 0:1], -float(CAP), None, ALU.add)
            nc.vector.tensor_reduce(rs[:, 1, 0:1], rs[:, 0, 1:PASSES], AX, ALU.add)
            dve.drain()
            nc.vector.tensor_scalar(rs[:, 1, 1:2], rs[:, 1, 0:1], 1.0, None, ALU.add)
            dve.drain()
            nc.vector.tensor_copy(itmp[:, 65:66], rs[:, 1, 1:2]).then_inc(sem("passes"), 1)
            nc.vector.memset(scatT, 0.0)
            nc.vector.memset(y_sb, 0.0).then_inc(sem("y_copied"), 1)
            dve.wait_ge(sem("gates_turned"), 1)
            nc.vector.tensor_copy(gT[0:NE, :], bank(2, TOK)[0:NE, :]).then_inc(sem("gates_t"), 1)

        def hidden_mm(pe, T, rnd, parity):
            feature_tile(pe, T, rnd, 4 + 2 * parity, uT)
            feature_tile(pe, T + 1, rnd, 5 + 2 * parity, uT)

        def down_mm(pe, T, rnd, ready, parity, start, stop):
            landed(pe, T, rnd)
            pe.wait_ge(*ready)
            w = wrows(T)
            for j in range(2):
                for t in range(TT):
                    for h in range(2):
                        ins = nc.tensor.matmul(ps[:, 2 * t + h, :], hidden[:, parity, j, t * P:(t + 1) * P],
                                               w[:, j, 512 * h:512 * h + 512], start=(start and j == 0),
                                               stop=(stop and j == 1), skip_group_check=True)
            ins.then_inc(w_used, 1)

        EXPERT_TILES = (("gate", 0), ("up", 0), ("gate", 1), ("up", 1), ("down", 0), ("down", 1),
                        ("gate", 2), ("up", 2), ("gate", 3), ("up", 3), ("down", 2), ("down", 3))
        PLACE = {x: n for n, x in enumerate(EXPERT_TILES)}
        CHUNK_BANK = (6, 7, 6, 7)
        xe = view(6144, 2, KT, CAP)
        sel = view(7552, TT, CAP)
        sel_g = view(7728, TT, CAP)
        scatT = view(7904, TOK)
        y_sb = view(8160, D)
        rank = view(9184, TT, NE + 1)
        gate = view(9250, TT, NE + 1)
        slot_no = view(9316, CAP)
        XG = view(15104, 2, 2, CAP)
        XL = view(15104 + 4 * CAP, 2, 2, CAP)
        XH = ffn_buf[:, 0:4 * CAP].rearrange("p (a b c) -> p a b c", b=2, c=CAP)
        XS = ffn_buf[:, 1024:1024 + 4 * CAP].rearrange("p (a b c) -> p a b c", b=2, c=CAP)

        def experts_pe(pe):
            def pick(n, half, b):
                for k in range(4):
                    for t in range(TT):
                        ins = nc.tensor.matmul(bank(b, 4, CAP)[:, k, :],
                                               xn[:, t, (4 * half + k) * P:(4 * half + k + 1) * P], sel[:, t, :],
                                               start=(t == 0), stop=(t == TT - 1))
                ins.then_inc(sem("picked"), 1)

            def hidden_products(T, rnd, c, n):
                for part in (0, 1):
                    tile = T + PLACE[(("gate", "up")[part], c)]
                    landed(pe, tile, rnd)
                    w = wcols(tile)
                    for j in range(2):
                        for k in range(KT):
                            ins = nc.tensor.matmul(bank(CHUNK_BANK[c], 4, CAP)[:, 2 * part + j, :],
                                                   w[:, k, j * P:(j + 1) * P], xe[:, n, k, :],
                                                   start=(k == 0), stop=(k == KT - 1))
                    ins.then_inc(w_used, 1)

            def down_products(T, rnd, c, m):
                tile = T + PLACE[("down", c)]
                landed(pe, tile, rnd)
                pe.wait_ge(sem("expert_hidden"), m * 4 + c + 1)
                w = wrows(tile)
                for j in range(2):
                    for h in range(2):
                        ins = nc.tensor.matmul(bank(4 + h, 512)[0:CAP, :], XH[:, c % 2, j, :],
                                               w[:, j, 512 * h:512 * h + 512], start=(c == 0 and j == 0),
                                               stop=(c == 3 and j == 1))
                ins.then_inc(w_used, 1)

            def put_back(stop):
                for t in range(TT):
                    for h in range(2):
                        nc.tensor.matmul(ps[:, 2 * t + h, :], scatT[0:CAP, t * P:(t + 1) * P],
                                         y_sb[0:CAP, 512 * h:512 * h + 512], start=False, stop=stop,
                                         skip_group_check=True)

            passes = passes_of(pe)
            pe.wait_ge(sem("h_rows"), 1)
            pe.wait_ge(sem("sel_ready"), 1)
            pick(0, 0, 6)
            pick(0, 1, 7)
            with pe.Fori(0, passes) as w:
                with pe.Fori(0, NE // 2) as i:
                    for n in range(2):
                        T, rnd, m = T_MOE + SLOTS * n, w * NE + i * 2, w * NE + i * 2 + n
                        pe.wait_ge(sem("picked_read"), m * 2 + 2)
                        hidden_products(T, rnd, 0, n)
                        pe.wait_ge(sem("y_copied"), m + 1)
                        put_back(False)
                        hidden_products(T, rnd, 1, n)
                        down_products(T, rnd, 0, m)
                        pe.wait_ge(sem("sel_ready"), m + 2)
                        pick(1 - n, 0, 6)
                        down_products(T, rnd, 1, m)
                        pe.wait_ge(sem("sel_g_ready"), m + 1)
                        for t in range(TT):
                            ins = nc.tensor.transpose(bank(7, TOK)[0:CAP, t * P:(t + 1) * P], sel_g[:, t, :],
                                                      ident[:])
                        ins.then_inc(sem("sel_g_turned"), 1)
                        pe.wait_ge(sem("picked_read"), m * 2 + 3)
                        hidden_products(T, rnd, 2, n)
                        pe.wait_ge(sem("scat_ready"), m + 1)
                        hidden_products(T, rnd, 3, n)
                        down_products(T, rnd, 2, m)
                        pick(1 - n, 1, 6)
                        down_products(T, rnd, 3, m)
            pe.wait_ge(sem("y_copied"), passes * NE + 1)
            put_back(True)
            nc.tensor.matmul(bank(6, P)[:, 0:1], ident[:], zero, start=True, stop=True).then_inc(
                sem("moe_out"), 1)
            return (passes - 1) * NE

        def experts_act(act):
            def copy_picked(half, n, count):
                act.wait_ge(sem("picked"), count)
                nc.scalar.activation(xe[:, n, 4 * half:4 * half + 4, :], bank(6, 4, CAP),
                                     ACT.Copy).then_inc(sem("picked_read"), 1)

            def sigmoid(c, m):
                act.wait_ge(sem("expert_gate"), m * 4 + c + 1)
                nc.scalar.activation(XS[:, c % 2, :, :], XG[:, c % 2, :, :], ACT.Sigmoid, scale=1.702).then_inc(
                    sem("expert_sigmoid"), 1)

            passes = passes_of(act)
            for half in range(2):
                act.wait_ge(sem("picked"), half + 1)
                nc.scalar.activation(xe[:, 0, 4 * half:4 * half + 4, :], bank(6 + half, 4, CAP),
                                     ACT.Copy).then_inc(sem("picked_read"), 1)
            with act.Fori(0, passes) as w:
                with act.Fori(0, NE // 2) as i:
                    for n in range(2):
                        T, rnd, m = T_MOE + SLOTS * n, w * NE + i * 2, w * NE + i * 2 + n
                        sigmoid(0, m)
                        sigmoid(1, m)
                        copy_picked(0, 1 - n, m * 2 + 3)
                        act.wait_ge(sem("sel_g_turned"), m + 1)
                        nc.scalar.activation(scatT[0:CAP, :], bank(7, TOK)[0:CAP, :], ACT.Copy).then_inc(
                            sem("scat_ready"), 1)
                        sigmoid(2, m)
                        sigmoid(3, m)
                        copy_picked(1, 1 - n, m * 2 + 4)
                        multiplied(act, T + PLACE[("down", 3)], rnd)
                        nc.scalar.activation(y_sb[0:CAP, :].rearrange("p (h n) -> p h n", n=512),
                                             ps[0:CAP, 4:6, :], ACT.Copy).then_inc(sem("y_copied"), 1)
            return (passes - 1) * NE

        def experts_dve(dve):
            v = nc.vector

            def choose(col_, count_sem, out_, with_gate):
                for t in range(TT):
                    ins = v.tensor_scalar(out_[:, t, :], slot_no, rank[:, t, col_],
                                          gate[:, t, col_] if with_gate else None, ALU.is_equal,
                                          ALU.mult if with_gate else ALU.bypass)
                ins.then_inc(sem(count_sem), 1)

            passes = passes_of(dve)
            v.tensor_copy(slot_no[:, 0:64], iota_t[:])
            v.tensor_scalar(slot_no[:, 64:CAP], iota_t[:, 0:CAP - 64], 64.0, None, ALU.add)
            dve.drain()
            choose(bass.ds(0, 1), "sel_ready", sel, False)
            with dve.Fori(0, passes) as w:
                with dve.Fori(0, NE // 2) as i:
                    for n in range(2):
                        T, rnd, m = T_MOE + SLOTS * n, w * NE + i * 2, w * NE + i * 2 + n
                        e = i * 2 + n
                        dve.wait_ge(sem("picked_read"), m * 2 + 2)
                        choose(bass.ds(e + 1, 1), "sel_ready", sel, False)
                        choose(bass.ds(e, 1), "sel_g_ready", sel_g, True)
                        for c in range(4):
                            par = c % 2
                            multiplied(dve, T + PLACE[("up", c)], rnd)
                            src = bank(CHUNK_BANK[c], 4, CAP)
                            g, l = XG[:, par, :, :], XL[:, par, :, :]
                            for j in range(2):
                                ins = v.tensor_scalar(g[:, j, :], src[:, j, :],
                                                      b_up[:, bass.ds(e * 16 + 2 * c + j, 1)], 7.0,
                                                      ALU.add, ALU.min)
                            ins.then_inc(sem("expert_gate"), 1)
                            for j in range(2):
                                v.tensor_scalar(l[:, j, :], src[:, 2 + j, :],
                                                b_up[:, bass.ds(e * 16 + 8 + 2 * c + j, 1)], 7.0,
                                                ALU.add, ALU.min)
                            dve.drain()
                            v.tensor_scalar(l, l, -7.0, 1.0, ALU.max, ALU.add)
                            dve.drain()
                            v.tensor_tensor(l, l, g, ALU.mult)
                            dve.drain()
                            dve.wait_ge(sem("expert_sigmoid"), m * 4 + c + 1)
                            v.tensor_tensor(XH[:, par, :, :], l, XS[:, par, :, :], ALU.mult).then_inc(
                                sem("expert_hidden"), 1)
                dve.drain()
                v.tensor_scalar(rank, rank, -float(CAP), None, ALU.add)
                dve.drain()
            return (passes - 1) * NE

        u5 = view(2048, KT, TOK)
        Xtok = view(0, TT, 2 * D)
        z = view(4096, 16, TOK)
        xbc = view(8192, 24, TOK)
        ga = view(14336, KT, TOK)
        gb = view(16384, KT, TOK)
        y5 = view(18432, KT, TOK)
        stage_a = view(20480, P)
        stage_b = view(20608, P)
        stage_c = view(20736, 160)
        lay = view(20896, 96)
        w_dt = view(20992, KT, 32)
        dt_bias, a_neg = lay[:, 0:32], lay[:, 32:64]
        skip_d = small[:, 128:144]
        step = small[:, 144:176]
        dts = view(21248, 5, TT, 32)
        C_nat = [view(8192, 8, 2, 64), view(9216, 8, 2, 64)]
        B_nat = [view(10240, 32, 32), view(11264, 32, 32)]
        C_T = [view(12288, 8, P), view(13312, 8, P)]
        B_T = [view(4096, 8, P), view(5120, 8, P)]
        cos_t, sin_t = view(6144, 4, 2, 64), view(6656, 4, 2, 64)
        phase = view(7168, 4, 2, 64)
        work = [view(14336 + 512 * k, 4, 2, 64) for k in range(8)]
        cols = view(7680, 16, 32)

        def layer_loads(pool, li):
            dma = pool.dma_start
            s = sem("stage_in")
            pool.wait_ge(sem("stage_used"), li + 1)
            pool.sem_inc(sem("loads_allowed"), 1)
            for name, src, n in (("ffn1_pre_g", "ffn1_pre_g_2", 8), ("mix_pre_g", "mix_pre_g_2", 8),
                                 ("ffn2_pre_g", "ffn2_pre_g_2", 8), ("conv_b", "ssd_conv_b_2", 24),
                                 ("norm_g", "ssd_norm_g_2", 16), ("s5_d", "s5_d_2", 8)):
                dma(stage_a[V2[name]:V2[name] + n, :],
                    a[src][li, :].rearrange("(r p) -> r p", p=P)).then_inc(s, 16)
            dma(stage_a[V2["lam_re"]:V2["lam_re"] + 32, :],
                a["s5_lambda_re_2"][li].rearrange("(j g) n -> j (g n)", g=2)).then_inc(s, 16)
            dma(stage_b[0:96, :], a["ssd_conv_w_2"][li].rearrange("k (r p) -> (k r) p", p=P)).then_inc(s, 16)
            dma(stage_b[96:128, :], a["s5_lambda_im_2"][li].rearrange("(j g) n -> j (g n)", g=2)).then_inc(s, 16)
            at = 0
            for name in ("ssd_dt_bias_2", "ssd_a_log_2", "ssd_d_2", "s5_log_step_2"):
                n = a[name].shape[1]
                dma(stage_c[:, at:at + n], bcast(a[name][bass.ds(li, 1), :])).then_inc(s, 16)
                at += n
            post_gain_load(pool, li * 3, a["ffn1_post_g_2"][bass.ds(li, 1), :])
            pool.wait_ge(sem("b_zeroed"), li + 1)
            pool.sem_inc(sem("loads_allowed"), 1)
            s = sem("s5_in")
            dma(w_dt, a["w_in_2"][li, :, DT2:DT2 + 32].rearrange("(k p) n -> p k n", p=P)).then_inc(s, 16)
            for v, name in enumerate(("s5_c_re_2", "s5_c_im_2")):
                src = a[name][li].rearrange("(T q) c n -> (q c) T n", q=8)
                for half in range(2):
                    dma(C_nat[v][:, :, half, :], src).then_inc(s, 16)
            for v, name in enumerate(("s5_b_re_2", "s5_b_im_2")):
                src = a[name][li].rearrange("(j g) n c -> g n j c", g=2)
                for g in range(2):
                    dma(B_nat[v][64 * g:64 * g + 64, :, 16 * g:16 * g + 16], src[g]).then_inc(s, 16)
            post_gain_load(pool, li * 3 + 1, a["mix_post_g_2"][bass.ds(li, 1), :])
            post_gain_load(pool, li * 3 + 2, a["ffn2_post_g_2"][bass.ds(li, 1), :])

        STAGE_IN = 16 * 13
        S5_IN = 16 * 9

        def post_gain_load(pool, p, src):
            if not isinstance(p, int):
                pool.wait_ge(sem("x_new"), p + 3)
                pool.sem_inc(sem("loads_allowed"), 1)
            pool.dma_start(post_gain[:], bcast(src)).then_inc(sem("post_gain_in"), 16)

        def layer_start_pe(pe, li):
            pe.wait_ge(sem("stage_in"), (li + 1) * STAGE_IN)
            pe.wait_ge(sem("x_new"), li * 3 + 3)
            nc.tensor.transpose(bank(6, P)[:, 0:NV2A], stage_a[0:NV2A, :], ident[0:NV2A, 0:NV2A])
            nc.tensor.transpose(bank(7, P), stage_b, ident[:]).then_inc(sem("vec2_turned"), 1)

        def layer_start_dve(dve, li):
            dve.wait_ge(sem("vec2_turned"), li + 1)
            nc.vector.tensor_copy(vec2[:, 0:NV2A], bank(6, P)[:, 0:NV2A])
            nc.vector.tensor_copy(vec2[:, NV2A:NV2], bank(7, P))
            dve.wait_ge(sem("stage_in"), (li + 1) * STAGE_IN)
            nc.vector.tensor_copy(dt_bias, stage_c[:, 0:32])
            for g in range(2):
                r = slice(64 * g, 64 * g + 64)
                nc.vector.tensor_copy(skip_d[r, :], stage_c[r, 64 + g:96:2])
                nc.vector.tensor_copy(step[r, :], stage_c[r, 96 + g:160:2])
            dve.wait_ge(sem("a_exp"), li + 1)
            nc.vector.tensor_scalar(a_neg, a_neg, -1.0, None, ALU.mult)
            nc.vector.memset(B_nat[1], 0.0)
            nc.vector.memset(B_nat[0], 0.0).then_inc(sem("b_zeroed"), 1)
            nc.vector.memset(small[:, 254:255], 0.0).then_inc(sem("stage_used"), 1)

        def layer_start_act(act, li):
            act.wait_ge(sem("vec2_turned"), li + 1)
            nc.scalar.activation(a_neg, stage_c[:, 32:64], ACT.Exp).then_inc(sem("a_exp"), 1)

        FFN_LOOPS = (NCH - 1) // 4

        def ffn_pe(pe, T0, r, base):
            s = sem("ffn_hidden")
            hidden_mm(pe, T0, r, 0)
            for b in range(4):
                nc.tensor.matmul(ps[:, b, 0:1], ident[:], zero, start=True, stop=False, skip_group_check=True)
            with pe.Fori(0, FFN_LOOPS) as i:
                for c in range(4):
                    hidden_mm(pe, T0 + 2 + 3 * c, r + i, (c + 1) % 2)
                    down_mm(pe, T0 + 4 + 3 * c, r + i, (s, base + i * 4 + c + 1), c % 2, False, False)
            for c in range(4 * FFN_LOOPS, NCH):
                last = c + 1 == NCH
                if not last:
                    hidden_mm(pe, T0 + 2 + 3 * c, r, (c + 1) % 2)
                down_mm(pe, T0 + 4 + 3 * c - (2 if last else 0), r, (s, base + c + 1), c % 2, False, last)

        def ffn_chunks(eng, T0, r, base, body):
            with eng.Fori(0, FFN_LOOPS) as i:
                for c in range(4):
                    body(T0 + 3 * c + (1 if c == 0 else 0), r + i, base + i * 4 + c, c % 2)
            for c in range(4 * FFN_LOOPS, NCH):
                body(T0 + 3 * c, r, base + c, c % 2)

        def ffn_act(act, T0, r, base):
            def chunk(T, rnd, n, par):
                multiplied(act, T, rnd)
                nc.scalar.activation(gated[:, par, :, :], bank(4 + 2 * par, 2, W), ACT.Silu).then_inc(
                    sem("ffn_silu"), 1)
            ffn_chunks(act, T0, r, base, chunk)

        def ffn_dve(dve, T0, r, base):
            def chunk(T, rnd, n, par):
                dve.wait_ge(sem("ffn_silu"), n + 1)
                nc.vector.tensor_tensor(hidden[:, par, :, :], gated[:, par, :, :], bank(5 + 2 * par, 2, W),
                                        ALU.mult).then_inc(sem("ffn_hidden"), 1)
            ffn_chunks(dve, T0, r, base, chunk)

        TURN = 6.283185

        def u5_pe(pe, r):
            for n in range(4):
                feature_tile(pe, L_U5 + n, r, n, uT)

        def u5_dve(dve, r):
            for n in range(4):
                multiplied(dve, L_U5 + n, r)
                nc.vector.tensor_copy(u5[:, 2 * n:2 * n + 2, :], bank(n, 2, TOK))
            dve.drain()

        (c_re, c_mag, c_th, c_half, c_sin, c_tanh, c_fr, c_fi, c_t1, c_t2, c_kr, c_ki, c_a, c_cos, c_t3,
         c_t4) = [cols[:, k, :] for k in range(16)]
        lam_im = vec2[:, V2["lam_im"]:V2["lam_im"] + 32]
        lam_re = vec2[:, V2["lam_re"]:V2["lam_re"] + 32]
        MAGIC = 12582912.0

        def turns(dve, out_, in_):
            nc.vector.tensor_scalar(out_, in_, MAGIC, MAGIC, ALU.add, ALU.subtract)
            dve.drain()
            nc.vector.tensor_tensor(out_, in_, out_, ALU.subtract)
            dve.drain()

        def s5_params_dve(dve, li):
            v = nc.vector
            v.tensor_scalar(c_re, lam_re, -1e-4, None, ALU.min).then_inc(sem("s5_re"), 1)
            dve.drain()
            dve.wait_ge(sem("s5_step"), li + 1)
            v.tensor_tensor(c_a, c_re, step, ALU.mult)
            v.tensor_tensor(c_th, lam_im, step, ALU.mult)
            dve.drain()
            v.tensor_scalar(c_t1, c_th, 1.0 / (2.0 * 3.141592653589793), None, ALU.mult)
            dve.drain()
            turns(dve, c_th, c_t1)
            v.tensor_scalar(c_t2, c_th, 64.0, None, ALU.mult)
            dve.drain()
            turns(dve, c_t3, c_t2)
            v.tensor_scalar(c_t1, c_t3, 0.25, None, ALU.add)
            dve.drain()
            turns(dve, c_t4, c_t1)
            v.memset(small[:, 248:249], 0.0).then_inc(sem("s5_angles"), 1)
            dve.wait_ge(sem("s5_trig"), li + 1)
            v.tensor_tensor(c_half, c_half, c_half, ALU.mult)
            v.scalar_tensor_tensor(out=c_tanh, in0=c_mag, scalar=1.0, in1=c_tanh, op0=ALU.add, op1=ALU.mult)
            dve.drain()
            v.tensor_scalar(c_cos, c_half, -2.0, 1.0, ALU.mult, ALU.add)
            dve.drain()
            v.tensor_tensor(c_fr, c_tanh, c_cos, ALU.mult)
            v.tensor_tensor(c_fi, c_mag, c_sin, ALU.mult)
            dve.drain()
            v.scalar_tensor_tensor(out=c_fr, in0=c_half, scalar=-2.0, in1=c_fr, op0=ALU.mult, op1=ALU.add)
            v.tensor_tensor(c_t1, c_re, c_re, ALU.mult)
            v.tensor_tensor(c_t2, lam_im, lam_im, ALU.mult)
            dve.drain()
            v.tensor_tensor(c_t1, c_t1, c_t2, ALU.add)
            dve.drain()
            v.reciprocal(c_t1, c_t1)
            dve.drain()
            v.tensor_tensor(c_fr, c_fr, c_t1, ALU.mult)
            v.tensor_tensor(c_fi, c_fi, c_t1, ALU.mult)
            dve.drain()
            v.tensor_tensor(c_t1, c_fr, c_re, ALU.mult)
            v.tensor_tensor(c_t2, c_fi, lam_im, ALU.mult)
            v.tensor_tensor(c_half, c_fi, c_re, ALU.mult)
            v.tensor_tensor(c_sin, c_fr, lam_im, ALU.mult)
            v.tensor_tensor(c_kr, c_mag, c_t4, ALU.mult)
            v.tensor_tensor(c_ki, c_mag, c_t3, ALU.mult)
            dve.drain()
            v.tensor_tensor(c_fr, c_t1, c_t2, ALU.add)
            v.tensor_tensor(c_fi, c_half, c_sin, ALU.subtract)
            dve.drain()
            dve.wait_ge(sem("s5_in"), (li + 1) * S5_IN)
            fr = c_fr.unsqueeze(2).to_broadcast([P, 32, 32])
            fi = c_fi.unsqueeze(2).to_broadcast([P, 32, 32])
            t = [arena[:, 14336 + 1024 * k:15360 + 1024 * k].rearrange("p (a b) -> p a b", b=32) for k in range(4)]
            v.tensor_tensor(t[0], B_nat[0], fr, ALU.mult)
            v.tensor_tensor(t[1], B_nat[1], fi, ALU.mult)
            v.tensor_tensor(t[2], B_nat[0], fi, ALU.mult)
            v.tensor_tensor(t[3], B_nat[1], fr, ALU.mult)
            for k in range(2):
                v.tensor_tensor(C_nat[k], C_nat[k], glmask[:].unsqueeze(1).unsqueeze(3).to_broadcast([P, 8, 2, 64]),
                                ALU.mult)
            dve.drain()
            v.tensor_tensor(B_nat[0], t[0], t[1], ALU.subtract)
            v.tensor_tensor(B_nat[1], t[2], t[3], ALU.add).then_inc(sem("s5_mats"), 1)
            for k in range(8):
                dve.wait_ge(sem("s5_turned"), li * 8 + k + 1)
                dst = (B_T[0], B_T[1], C_T[0], C_T[1])[k // 2][:, 4 * (k % 2):4 * (k % 2) + 4, :]
                if k < 6:
                    ins = v.tensor_copy(dst, bank(k, 4, P))
                else:
                    ins = v.tensor_scalar(dst, bank(k, 4, P), -1.0, None, ALU.mult)
            ins.then_inc(sem("s5_mats_ready"), 1)

        def s5_params_act(act, li):
            act.wait_ge(sem("s5_re"), li + 1)
            nc.scalar.activation(step, step, ACT.Exp).then_inc(sem("s5_step"), 1)
            act.wait_ge(sem("s5_angles"), li + 1)
            nc.scalar.activation(c_mag, c_a, ACT.Exp)
            nc.scalar.activation(c_tanh, c_a, ACT.Tanh, scale=0.5)
            nc.scalar.activation(c_half, c_th, ACT.Sin, scale=TURN / 2)
            nc.scalar.activation(c_sin, c_th, ACT.Sin, scale=TURN)
            nc.scalar.activation(c_t3, c_t3, ACT.Sin, scale=TURN)
            nc.scalar.activation(c_t4, c_t4, ACT.Sin, scale=TURN).then_inc(sem("s5_trig"), 1)

        def s5_turn_pe(pe, li):
            pe.wait_ge(sem("s5_mats"), li + 1)
            for k in range(8):
                for q in range(4):
                    T = 4 * (k % 2) + q
                    if k < 4:
                        src = B_nat[k // 2][:, 4 * T:4 * T + 4, :].rearrange("p a b -> p (a b)")
                    else:
                        src = C_nat[k // 2 - 2][:, T, :, :].rearrange("p a b -> p (a b)")
                    ins = nc.tensor.transpose(bank(k, 4, P)[:, q, :], src, ident[:])
                ins.then_inc(sem("s5_turned"), 1)

        def s5_in_mm(pe, li, n):
            g, c = n // 4, n % 4
            for o in range(4):
                r = slice(32 * o, 32 * o + 32)
                for v in range(2):
                    for q in range(2):
                        ins = nc.tensor.matmul(bank(o, 2, 2, 64)[:, v, q, :], B_T[v][r, 2 * g + q, :],
                                               u5[r, 2 * g + q, 64 * c:64 * c + 64], start=True, stop=True)
            ins.then_inc(sem("s5_bu"), 1)

        def s5_pe(pe, li):
            pe.wait_ge(sem("s5_mats_ready"), li + 1)
            s5_in_mm(pe, li, 0)
            for n in range(16):
                g, c = n // 4, n % 4
                if n < 15:
                    pe.wait_ge(sem("s5_bu_read"), li * 16 + n + 1)
                    s5_in_mm(pe, li, n + 1)
                pe.wait_ge(sem("s5_states"), li * 16 + n + 1)
                for q in range(2):
                    for o in range(4):
                        out_ = bank(4 + n % 2, 2, 64)[32 * o:32 * o + 32, q, :]
                        j = slice(32 * o, 32 * o + 32)
                        nc.tensor.matmul(out_, C_T[0][:, 2 * g + q, j], work[6][:, o, q, :], start=True,
                                         stop=False)
                        ins = nc.tensor.matmul(out_, C_T[1][:, 2 * g + q, j], work[7][:, o, q, :], start=False,
                                               stop=True)
                ins.then_inc(sem("s5_y"), 1)

        def tile_cols(t, g):
            return t[:, 8 * g:8 * g + 8].rearrange("p (q o) -> p o q", q=2)

        def s5_dve(dve, li):
            v = nc.vector
            atab, t0, t1, t2, br, bi, sr, si = work
            full = [P, 4, 2, 64]

            def flat(w):
                return w.rearrange("p a b c -> p (a b c)")

            def read_y(n):
                g, c = n // 4, n % 4
                dve.wait_ge(sem("s5_y"), li * 16 + n + 1)
                for q in range(2):
                    cs = slice(64 * c, 64 * c + 64)
                    v.scalar_tensor_tensor(out=y5[:, 2 * g + q, cs], in0=u5[:, 2 * g + q, cs],
                                           scalar=col(vec2, V2["s5_d"] + 2 * g + q),
                                           in1=bank(4 + n % 2, 2, 64)[:, q, :], op0=ALU.mult, op1=ALU.add)

            for g in range(4):
                th = tile_cols(c_th, g)
                for o in range(4):
                    v.tensor_tensor(t0[:, o, :, :], th[:, o, :].unsqueeze(2).to_broadcast([P, 2, 64]),
                                    iota_t[:].unsqueeze(1).to_broadcast([P, 2, 64]), ALU.mult)
                    v.tensor_copy(atab[:, o, :, :],
                                  tile_cols(c_mag, g)[:, o, :].unsqueeze(2).to_broadcast([P, 2, 64]))
                dve.drain()
                v.memset(atab[:, :, :, 0:1], 0.0)
                turns(dve, phase, t0)
                v.tensor_scalar(t0, phase, 0.25, None, ALU.add)
                dve.drain()
                turns(dve, t1, t0)
                v.memset(small[:, 248:249], 0.0).then_inc(sem("s5_phase"), 1)
                dve.wait_ge(sem("s5_tables"), li * 4 + g + 1)
                for c in range(4):
                    n = 4 * g + c
                    dve.wait_ge(sem("s5_bu"), li * 16 + n + 1)
                    bu_r = ps[:, 0:4, 0:128].rearrange("p o (q t) -> p o q t", q=2)
                    bu_i = ps[:, 0:4, 128:256].rearrange("p o (q t) -> p o q t", q=2)
                    v.tensor_tensor(br, bu_r, cos_t, ALU.mult)
                    v.tensor_tensor(t0, bu_i, sin_t, ALU.mult)
                    v.tensor_tensor(bi, bu_i, cos_t, ALU.mult)
                    v.tensor_tensor(t1, bu_r, sin_t, ALU.mult).then_inc(sem("s5_bu_read"), 1)
                    if c:
                        er, ei = t2[:, 0, :, 0:4], t2[:, 1, :, 0:4]
                        kr = tile_cols(c_kr, g).rearrange("p o q -> p q o")
                        ki = tile_cols(c_ki, g).rearrange("p o q -> p q o")
                        v.tensor_tensor(t2[:, 2, :, 0:4], kr, er, ALU.mult)
                        v.tensor_tensor(t2[:, 2, :, 4:8], ki, ei, ALU.mult)
                        v.tensor_tensor(t2[:, 3, :, 0:4], kr, ei, ALU.mult)
                        v.tensor_tensor(t2[:, 3, :, 4:8], ki, er, ALU.mult)
                    dve.drain()
                    v.tensor_tensor(br, br, t0, ALU.add)
                    v.tensor_tensor(bi, bi, t1, ALU.subtract)
                    if c:
                        v.tensor_tensor(t2[:, 2, :, 0:4], t2[:, 2, :, 0:4], t2[:, 2, :, 4:8], ALU.subtract)
                        v.tensor_tensor(t2[:, 3, :, 0:4], t2[:, 3, :, 0:4], t2[:, 3, :, 4:8], ALU.add)
                        dve.drain()
                        for w, k in ((br, 2), (bi, 3)):
                            first = w[:, :, :, 0:1].rearrange("p o q t -> p q (o t)")
                            v.tensor_tensor(first, first, t2[:, k, :, 0:4], ALU.add)
                    dve.drain()
                    v.tensor_tensor_scan(flat(t0), flat(atab), flat(br), 0.0, ALU.mult, ALU.add)
                    v.tensor_tensor_scan(flat(t1), flat(atab), flat(bi), 0.0, ALU.mult, ALU.add)
                    dve.drain()
                    if n:
                        read_y(n - 1)
                    v.tensor_tensor(sr, t0, cos_t, ALU.mult)
                    v.tensor_tensor(br, t1, sin_t, ALU.mult)
                    v.tensor_tensor(si, t0, sin_t, ALU.mult)
                    v.tensor_tensor(bi, t1, cos_t, ALU.mult)
                    if c < 3:
                        v.tensor_copy(t2[:, 0, :, 0:4], t0[:, :, :, 63:64].rearrange("p o q t -> p q (o t)"))
                        v.tensor_copy(t2[:, 1, :, 0:4], t1[:, :, :, 63:64].rearrange("p o q t -> p q (o t)"))
                    dve.drain()
                    v.tensor_tensor(sr, sr, br, ALU.subtract)
                    v.tensor_tensor(si, si, bi, ALU.add).then_inc(sem("s5_states"), 1)
                    dve.drain()
            read_y(15)
            dve.drain()
            nc.vector.memset(small[:, 248:249], 0.0).then_inc(sem("y5_raw"), 1)

        def s5_act(act, li):
            for g in range(4):
                act.wait_ge(sem("s5_phase"), li * 4 + g + 1)
                nc.scalar.activation(sin_t, phase, ACT.Sin, scale=TURN)
                nc.scalar.activation(cos_t, work[2], ACT.Sin, scale=TURN).then_inc(sem("s5_tables"), 1)
            act.wait_ge(sem("y5_raw"), li + 1)
            nc.scalar.activation(y5, y5, ACT.Gelu_apprx_tanh).then_inc(sem("y5_ready"), 1)

        def proj_pe(pe, li, r):
            pe.wait_ge(sem("y5_raw"), li + 1)
            for n in range(28):
                if 8 <= n < 16:
                    pe.wait_ge(sem("z_read"), li * 8 + n - 7)
                elif n >= 16:
                    pe.wait_ge(sem("xbc_read"), li * 12 + n - 15)
                feature_tile(pe, L_Z + n, r, n % 8, uT)
            pe.wait_ge(sem("g_read"), li * 8 + 1)
            for t in range(TT):
                for k in range(KT):
                    ins = nc.tensor.matmul(bank(4, TT, 32)[:, t, :], uT[:, k, t * P:(t + 1) * P], w_dt[:, k, :],
                                           start=(k == 0), stop=(k == KT - 1))
            ins.then_inc(sem("dt_mm"), 1)
            pe.wait_ge(sem("y5_ready"), li + 1)
            pe.wait_ge(sem("dt_raw"), li + 1)
            for n in range(4):
                if n == 0:
                    pe.wait_ge(sem("g_read"), li * 8 + 4)
                if n == 2:
                    pe.wait_ge(sem("g_read"), li * 8 + 8)
                for half in range(2):
                    feature_tile(pe, L_GLU + 2 * n + half, r, (4 + 2 * n + half) % 8, y5)
            pe.wait_ge(sem("glu_ready"), li * 4 + 4)
            for n in range(4):
                feature_tile(pe, L_BB + n, r, n, uT)

        def proj_act(act, li, r):
            for n in range(8):
                multiplied(act, L_Z + n, r)
                nc.scalar.activation(z[:, 2 * n:2 * n + 2, :], bank(n, 2, TOK), ACT.Silu).then_inc(
                    sem("z_read"), 1)
            for n in range(12):
                act.wait_ge(sem("xbc_read"), li * 12 + n + 1)
                ins = nc.scalar.activation(xbc[:, 2 * n:2 * n + 2, :], xbc[:, 2 * n:2 * n + 2, :], ACT.Silu)
            ins.then_inc(sem("xbc_ready"), 1)
            for n in range(8):
                multiplied(act, L_GA + n, r)
                t = (ga, gb)[n // 4][:, 2 * (n % 4):2 * (n % 4) + 2, :]
                nc.scalar.activation(t, bank((20 + n) % 8, 2, TOK), ACT.Sigmoid).then_inc(sem("g_read"), 1)
            for n in range(4):
                multiplied(act, L_GLU + 2 * n + 1, r)
                if n >= 2:
                    act.wait_ge(sem("glu_ready"), li * 4 + n - 1)
                nc.scalar.activation(gated[:, n % 2, :, :], bank((5 + 2 * n) % 8, 2, TOK), ACT.Sigmoid).then_inc(
                    sem("glu_gate"), 1)
            dt, ab = dts[:, 0], dts[:, 1]
            act.wait_ge(sem("dt_raw"), li + 1)
            nc.scalar.activation(ab, dt, ACT.Abs)
            act.drain()
            nc.scalar.activation(ab, ab, ACT.Exp, scale=-1.0)
            act.drain()
            nc.scalar.activation(ab, ab, ACT.Ln, bias=one).then_inc(sem("dt_log"), 1)

        def proj_dve(dve, li, r):
            cw, cb_ = V2["conv_w"], V2["conv_b"]
            for n in range(12):
                multiplied(dve, L_XBC + n, r)
                src = bank(n % 8, 2, TOK)
                for t in range(2):
                    f = 2 * n + t
                    nc.vector.tensor_scalar(xbc[:, f, :], src[:, t, :], col(vec2, cw + 72 + f),
                                            col(vec2, cb_ + f), ALU.mult, ALU.add)
                for lag in (1, 2, 3):
                    dve.drain()
                    for t in range(2):
                        f = 2 * n + t
                        ins = nc.vector.scalar_tensor_tensor(
                            out=xbc[:, f, lag:], in0=src[:, t, 0:TOK - lag], scalar=col(vec2, cw + 24 * (3 - lag) + f),
                            in1=xbc[:, f, lag:], op0=ALU.mult, op1=ALU.add)
                ins.then_inc(sem("xbc_read"), 1)
            dt, ab, adt = dts[:, 0], dts[:, 1], dts[:, 2]
            dve.wait_ge(sem("dt_mm"), li + 1)
            nc.vector.tensor_tensor(dt, bank(4, TT, 32), dt_bias.unsqueeze(1).to_broadcast([P, TT, 32]),
                                    ALU.add).then_inc(sem("dt_raw"), 1)
            for n in range(4):
                dve.wait_ge(sem("glu_gate"), li * 4 + n + 1)
                nc.vector.tensor_tensor(uT[:, 2 * n:2 * n + 2, :], bank((4 + 2 * n) % 8, 2, TOK),
                                        gated[:, n % 2, :, :], ALU.mult).then_inc(sem("glu_ready"), 1)
            for n in range(4):
                multiplied(dve, L_BB + n, r)
                t = gb[:, 2 * n:2 * n + 2, :]
                nc.vector.tensor_tensor(t, t, bank(n, 2, TOK), ALU.mult)
            dve.wait_ge(sem("dt_log"), li + 1)
            nc.vector.scalar_tensor_tensor(out=dt, in0=dt, scalar=0.0, in1=ab, op0=ALU.max, op1=ALU.add)
            dve.drain()
            nc.vector.tensor_tensor(adt, dt, a_neg.unsqueeze(1).to_broadcast([P, TT, 32]), ALU.mult).then_inc(
                sem("dt_ready"), 1)

        Ms = [arena[:, 18432:18432 + 1536].rearrange("p (h n) -> p h n", n=384),
              ffn_buf[:, 0:1536].rearrange("p (h n) -> p h n", n=384)]
        CBs = [arena[:, 19968:19968 + 384], ffn_buf[:, 1536:1920]]
        nacum = dts[:, 3]

        def ssd_pe(pe, li, r):
            adt = dts[:, 2]
            pe.wait_ge(sem("dt_ready"), li + 1)
            o = bank(5, TT, 32)
            nc.tensor.matmul(o[:, 0, :], tri[:, 0:P], adt[:, 0, :], start=True, stop=True)
            nc.tensor.matmul(o[:, 1, :], tri[:, P:2 * P], adt[:, 0, :], start=True, stop=False)
            nc.tensor.matmul(o[:, 1, :], tri[:, 0:P], adt[:, 1, :], start=False, stop=True).then_inc(
                sem("acum_mm"), 1)
            pe.wait_ge(sem("xbc_ready"), li + 1)
            for n in range(8):
                g, t = n // 2, n % 2
                if n >= 2:
                    pe.wait_ge(sem("x_turned_read"), li * 8 + n - 1)
                for q in range(4):
                    ins = nc.tensor.transpose(bank(6 + n % 2, 4, P)[:, q, :], xbc[:, 4 * g + q, t * P:(t + 1) * P],
                                              ident[:])
                ins.then_inc(sem("heads_turned"), 1)
            pe.wait_ge(sem("x_turned_read"), li * 8 + 8)
            for u in range(9):
                if u < 8:
                    g = u // 2
                    if u % 2 == 0:
                        b = 6 + g % 2
                        Bm, Cm = xbc[:, 16 + g, :], xbc[:, 20 + g, :]
                        nc.tensor.matmul(bank(b, 384)[:, 0:TOK], Bm[:, 0:P], Cm, start=True, stop=True)
                        nc.tensor.matmul(bank(b, 384)[:, TOK:384], Bm[:, P:TOK], Cm[:, P:TOK], start=True,
                                         stop=True).then_inc(sem("cb_mm"), 1)
                    for i in range(4):
                        h = 4 * u + i
                        o = bank(2 * (u % 2) + i // 2, 2, TOK)[:, i % 2, :]
                        nc.tensor.matmul(o, adt[:, 0, h:h + 1].to_broadcast([P, P]), tri[:], start=True,
                                         stop=False, skip_group_check=True)
                        ins = nc.tensor.matmul(o[:, P:TOK], adt[:, 1, h:h + 1].to_broadcast([P, P]), tri[:, 0:P],
                                               start=False, stop=True, skip_group_check=True)
                    ins.then_inc(sem("sums_mm"), 1)
                if u:
                    v = u - 1
                    pe.wait_ge(sem("m_ready"), li * 8 + v + 1)
                    for i in range(4):
                        h = 4 * v + i
                        o = bank(4 + v % 2, 2, TOK)[64 * (i % 2):64 * (i % 2) + 64, i // 2, :]
                        M = Ms[v % 2]
                        nc.tensor.matmul(o, Xtok[:, 0, 64 * h:64 * h + 64], M[:, i, 0:TOK], start=True, stop=False,
                                         skip_group_check=True)
                        ins = nc.tensor.matmul(o[:, P:TOK], Xtok[:, 1, 64 * h:64 * h + 64], M[:, i, TOK:384],
                                               start=False, stop=True, skip_group_check=True)
                    ins.then_inc(sem("ssd_y"), 1)
            pe.wait_ge(sem("ya_squares"), li + 1)
            for g in range(4):
                for q in range(4):
                    ins = nc.tensor.matmul(bank(g, TOK), mean512[:], xbc[:, 4 * g + q, :], start=(q == 0),
                                           stop=(q == 3))
            ins.then_inc(sem("ya_mean"), 1)
            pe.wait_ge(sem("ya_ready"), li + 1)
            for n in range(4):
                for half in range(2):
                    feature_tile(pe, L_BA + 2 * n + half, r, 4 + n, z[:, 8 * half:8 * half + 8, :], half)
            pe.wait_ge(sem("merged"), li + 1)
            for n in range(4):
                token_tile(pe, L_WOUT + n, r, [bank(2 * t + n // 2, 2, W)[:, n % 2, :] for t in range(TT)], ga)

        def ssd_dve(dve, li, r):
            v = nc.vector
            dt = dts[:, 0]
            dve.wait_ge(sem("acum_mm"), li + 1)
            v.tensor_scalar(nacum, bank(5, TT, 32), -1.0, None, ALU.mult)
            for n in range(8):
                g, t = n // 2, n % 2
                dve.wait_ge(sem("heads_turned"), li * 8 + n + 1)
                v.tensor_tensor(Xtok[:, t, 512 * g:512 * g + 512].rearrange("p (h e) -> p h e", e=64),
                                bank(6 + n % 2, 8, 64),
                                dt[:, t, 8 * g:8 * g + 8].unsqueeze(2).to_broadcast([P, 8, 64]),
                                ALU.mult).then_inc(sem("x_turned_read"), 1)

            def out_of(u):
                dve.wait_ge(sem("ssd_y"), li * 8 + u + 1)
                for i in range(2):
                    f = 2 * u + i
                    v.scalar_tensor_tensor(out=xbc[:, f, :], in0=xbc[:, f, :], scalar=skip_d[:, f:f + 1],
                                           in1=bank(4 + u % 2, 2, TOK)[:, i, :], op0=ALU.mult, op1=ALU.add)
                dve.drain()
                return v.tensor_tensor(z[:, 2 * u:2 * u + 2, :], z[:, 2 * u:2 * u + 2, :],
                                       xbc[:, 2 * u:2 * u + 2, :], ALU.mult)

            for u in range(8):
                g, M, CB = u // 2, Ms[u % 2], CBs[(u // 2) % 2]
                if u % 2 == 0:
                    dve.wait_ge(sem("cb_mm"), li * 4 + g + 1)
                    b = bank(6 + g % 2, 384)
                    v.tensor_tensor(CB[:, 0:P], b[:, 0:P], tri[:, 0:P], ALU.mult)
                    v.tensor_copy(CB[:, P:TOK], b[:, P:TOK])
                    v.tensor_tensor(CB[:, TOK:384], b[:, TOK:384], tri[:, 0:P], ALU.mult)
                dve.wait_ge(sem("sums_mm"), li * 8 + u + 1)
                for i in range(4):
                    h = 4 * u + i
                    s = bank(2 * (u % 2) + i // 2, 2, TOK)[:, i % 2, :]
                    v.tensor_scalar(M[:, i, 0:TOK], s, nacum[:, 0, h:h + 1], 0.0, ALU.add, ALU.min)
                    ins = v.tensor_scalar(M[:, i, TOK:384], s[:, P:TOK], nacum[:, 1, h:h + 1], 0.0, ALU.add,
                                          ALU.min)
                ins.then_inc(sem("exponents"), 1)
                if u:
                    out_of(u - 1)
                dve.wait_ge(sem("decayed"), li * 8 + u + 1)
                v.tensor_tensor(M, M, CB.unsqueeze(1).to_broadcast([P, 4, 384]), ALU.mult).then_inc(
                    sem("m_ready"), 1)
            out_of(7).then_inc(sem("ya_raw"), 1)
            rms = xbc[:, 16:20, :]
            dve.wait_ge(sem("ya_rms"), li + 1)
            v.reciprocal(rms, rms)
            dve.drain()
            for f in range(16):
                ins = v.scalar_tensor_tensor(out=z[:, f, :], in0=z[:, f, :], scalar=col(vec2, V2["norm_g"] + f),
                                             in1=rms[:, f // 4, :], op0=ALU.mult, op1=ALU.mult)
            ins.then_inc(sem("ya_ready"), 1)
            for n in range(4):
                multiplied(dve, L_BA + 2 * n + 1, r)
                t = slice(2 * n, 2 * n + 2)
                v.tensor_tensor(ga[:, t, :], ga[:, t, :], bank(4 + n, 2, TOK), ALU.mult)
                dve.drain()
                ins = v.tensor_tensor(ga[:, t, :], ga[:, t, :], gb[:, t, :], ALU.add)
            ins.then_inc(sem("merged"), 1)

        def ssd_act(act, li):
            for u in range(8):
                act.wait_ge(sem("exponents"), li * 8 + u + 1)
                nc.scalar.activation(Ms[u % 2], Ms[u % 2], ACT.Exp).then_inc(sem("decayed"), 1)
            act.wait_ge(sem("ya_raw"), li + 1)
            nc.scalar.activation(xbc[:, 0:16, :], z, ACT.Square).then_inc(sem("ya_squares"), 1)
            act.wait_ge(sem("ya_mean"), li + 1)
            nc.scalar.activation(xbc[:, 16:20, :], ps[:, 0:4, 0:TOK], ACT.Sqrt, bias=eps).then_inc(
                sem("ya_rms"), 1)

        block = ctx.enter_context(nc.Block())
        FINAL = {1: 2, 2: 3, 3: 3 + 3 * LAYERS}[min(upto, 3)]


        @block.sync
        def _(sp):
            sp_program(sp)
            sp.wait_ge(sem("x_new"), FINAL)
            sp.dma_start(out.rearrange("a (t p) d -> p (a t) d", p=P), x[:]).then_inc(sem("stored"), 16)
            sp.wait_ge(sem("stored"), 16)

        @block.gpsimd
        def _(pool):
            constants(pool)
            small_loads_1(pool)
            if upto >= 2:
                moe_small_loads(pool)
            if upto >= 3:
                with pool.Fori(0, LAYERS) as li:
                    layer_loads(pool, li)

        @block.scalar
        def _(act):
            mod_act(act)
            pre_norm_act(act, 0)
            win1_act(act)
            lam_act(act)
            attention_act(act)
            gla_act(act)
            lru_act(act)
            if upto >= 2:
                pre_norm_act(act, 1)
                router_act(act)
                extra = experts_act(act)
            if upto >= 3:
                with act.Fori(0, LAYERS) as li:
                    r = li * ROUNDS + extra
                    layer_start_act(act, li)
                    pre_norm_act(act, li * 3 + 2)
                    ffn_act(act, L_FFN1, r, li * 2 * NCH)
                    post_norm_act(act, L_U5 - 1, r)
                    pre_norm_act(act, li * 3 + 3)
                    s5_params_act(act, li)
                    s5_act(act, li)
                    proj_act(act, li, r)
                    ssd_act(act, li)
                    post_norm_act(act, L_FFN2 - 1, r)
                    pre_norm_act(act, li * 3 + 4)
                    ffn_act(act, L_FFN2, r, li * 2 * NCH + NCH)
                    post_norm_act(act, L_PAD - 1, r)

        @block.vector
        def _(dve):
            mod_dve(dve)
            glmask_dve(dve)
            dve.wait_ge(sem("x_in"), 16)
            nc.vector.memset(small[:, 252:253], 0.0).then_inc(sem("x_new"), 1)
            pre_norm_dve(dve, 0)
            pre_norm_out(dve, 0, lambda k: col(modc, 8 + k), lambda k: col(modc, k))
            win1_dve(dve)
            qk_norm_dve(dve)
            attention_dve(dve)
            gla_dve(dve)
            lru_dve(dve)
            multiplied(dve, T_WOUT1 + 3, 0)
            wout1_dve(dve, 0)
            if upto >= 2:
                pre_norm_dve(dve, 1)
                pre_norm_out(dve, 1, lambda k: col(modc, 24 + k), lambda k: col(modc, 16 + k))
                router_dve(dve)
                extra = experts_dve(dve)
                dve.wait_ge(sem("moe_out"), 1)
                wout1_dve(dve, 1)
            if upto >= 3:
                with dve.Fori(0, LAYERS) as li:
                    r = li * ROUNDS + extra

                    def gains(name):
                        return lambda k: col(vec2, V2[name] + k)
                    layer_start_dve(dve, li)
                    pre_norm_dve(dve, li * 3 + 2)
                    pre_norm_out(dve, li * 3 + 2, gains("ffn1_pre_g"))
                    ffn_dve(dve, L_FFN1, r, li * 2 * NCH)
                    post_norm_dve(dve, li * 3, 0.5)
                    pre_norm_dve(dve, li * 3 + 3)
                    pre_norm_out(dve, li * 3 + 3, gains("mix_pre_g"))
                    u5_dve(dve, r)
                    s5_params_dve(dve, li)
                    s5_dve(dve, li)
                    proj_dve(dve, li, r)
                    ssd_dve(dve, li, r)
                    post_norm_dve(dve, li * 3 + 1, 1.0)
                    pre_norm_dve(dve, li * 3 + 4)
                    pre_norm_out(dve, li * 3 + 4, gains("ffn2_pre_g"))
                    ffn_dve(dve, L_FFN2, r, li * 2 * NCH + NCH)
                    post_norm_dve(dve, li * 3 + 2, 0.5)

        @block.tensor
        def _(pe):
            mod_pe(pe)
            pre_norm_pe(pe, 0)
            win1_pe(pe)
            qk_norm_pe(pe)
            attention_pe(pe)
            oa_mean_pe(pe)
            gla_pe(pe)
            lru_pe(pe)
            wout1_pe(pe)
            if upto >= 2:
                pre_norm_pe(pe, 1)
                router_pe(pe)
                extra = experts_pe(pe)
            if upto >= 3:
                with pe.Fori(0, LAYERS) as li:
                    r = li * ROUNDS + extra
                    layer_start_pe(pe, li)
                    pre_norm_pe(pe, li * 3 + 2)
                    pe.wait_ge(sem("u_ready"), li * 3 + 3)
                    ffn_pe(pe, L_FFN1, r, li * 2 * NCH)
                    pre_norm_pe(pe, li * 3 + 3)
                    pe.wait_ge(sem("u_ready"), li * 3 + 4)
                    u5_pe(pe, r)
                    s5_turn_pe(pe, li)
                    s5_pe(pe, li)
                    proj_pe(pe, li, r)
                    ssd_pe(pe, li, r)
                    pre_norm_pe(pe, li * 3 + 4)
                    pe.wait_ge(sem("u_ready"), li * 3 + 5)
                    ffn_pe(pe, L_FFN2, r, li * 2 * NCH + NCH)
                    for n in range(NPAD):
                        landed(pe, L_PAD + n, r)
                        multiplied(pe, L_PAD + n - 1, r)
                        pe.sem_inc(w_used, 1)


def kernel(**inputs):
    import numpy as np
    import concourse.bacc as bacc
    from concourse.bass_utils import run_bass_kernel_spmd

    nc = bacc.Bacc("TRN2", target_bir_lowering=False, num_devices=1)
    arrays, args = {}, {}
    for name, value in inputs.items():
        v = np.ascontiguousarray(value)
        arrays[f"in_{name}"] = v
        args[name] = nc.dram_tensor(f"in_{name}", v.shape, mybir.dt.from_np(v.dtype), kind="ExternalInput").ap()
    out = nc.dram_tensor("out_0", (1, TOK, D), F32, kind="ExternalOutput").ap()
    build(nc, args, out)
    result = run_bass_kernel_spmd(nc, [arrays], core_ids=[0])
    return result.results[0]["out_0"]
```

```python
from contextlib import ExitStack

import concourse.bass as bass
from concourse import mybir

P = 128
D = 1024
TOK = 256
TT = TOK // P
KT = D // P
W = 256
SLOTS = 6
TILES12 = 12 // SLOTS
NE = 32
TOPK = 4
CAP = 88
PASSES = -(-TOK // CAP)
TC = 128
FH = 2816
LAYERS = 2
EPS = 1e-6
NEG = -1e30
NCH = FH // W
LAM0 = 0.2

F32 = mybir.dt.float32
I32 = mybir.dt.int32
F32R = mybir.dt.float32r
ALU = mybir.AluOpType
ACT = mybir.ActivationFunctionType
AX = mybir.AxisListType.X

AQ, AK, AV, BQ, BK, BV, CQ, CV, CG, CR, DX, DG = (
    0, 256, 512, 768, 1024, 1280, 1536, 1792, 2048, 2064, 2320, 2576)
WIN1_FEATURE = (AQ, AK, BQ, BK, CQ, CR, DX, DG)
WIN1_TOKEN = (AV, BV, CV)
Z2, XBC2, DT2, U52, GA2, GB2 = 0, 2048, 5120, 5152, 6176, 7200

V1 = {}
_n = 0
for _name, _rows in (("norm1_g", 8), ("norm2_g", 8), ("sh0", 8), ("sc0", 8), ("sh1", 8), ("sc1", 8),
                     ("d_conv_w", 8), ("d_conv_b", 2), ("d_b_a", 2), ("d_b_x", 2),
                     ("d_lambda", 2), ("c_b_g", 1), ("a_q_gain", 1), ("a_k_gain", 1), ("b_q_gain", 1),
                     ("b_k_gain", 1), ("a_out_gain", 1), ("c_out_gain", 1)):
    V1[_name] = _n
    _n += _rows
NV1 = _n
V2 = {}
_n = 0
for _name, _rows in (("ffn1_pre_g", 8), ("mix_pre_g", 8), ("ffn2_pre_g", 8), ("conv_b", 24), ("norm_g", 16),
                     ("s5_d", 8), ("lam_re", 32), ("conv_w", 96), ("lam_im", 32)):
    V2[_name] = _n
    _n += _rows
NV2 = _n
NV2A = V2["conv_w"]


def build(nc, a, out, upto=99):
    ctx = ExitStack()
    with ctx:
        def sb(name, shape, dt=F32):
            return ctx.enter_context(nc.sbuf_tensor(name, shape, dt))

        sems = {}

        def sem(name):
            if name not in sems:
                sems[name] = ctx.enter_context(nc.semaphore(name))
            return sems[name]

        ctx.enter_context(nc.allow_non_contiguous_dma(reason="small vectors and state matrices"))

        ring = sb("ring", [P, SLOTS, 2048])
        x = sb("x_res", [P, TT, D])
        ffn_buf = sb("ffn_buf", [P, 2048])
        hidden = ffn_buf[:, 0:1024].rearrange("p (a b c) -> p a b c", b=2, c=W)
        gated = ffn_buf[:, 1024:2048].rearrange("p (a b c) -> p a b c", b=2, c=W)
        post_gain = sb("post_gain", [P, D])
        ident = sb("ident", [P, P])
        mask_qk = sb("mask_qk", [P, P])
        tri = sb("tri", [P, 2 * P])
        mean32 = sb("mean32", [P, P])
        mean64 = sb("mean64", [P, P])
        mean512 = sb("mean512", [P, P])
        reset64 = sb("reset64", [P, TOK])
        headmask = sb("headmask", [P, 4])
        iota_t = sb("iota_t", [P, P])
        glmask = sb("glmask", [P, 2])
        itmp = sb("itmp", [P, P + 2], I32)
        vec1 = sb("vec1", [P, P])
        vec2 = sb("vec2", [P, NV2])
        small = sb("small", [P, 256])
        AW = 21568 + 12288 - 128
        with nc.sbuf_tensor("arena", [P, AW], F32) as arena:
            pass
        sb("arena_0", [P, 2048])
        u_upper = sb("u_upper", [P, 2048], F32R)
        sb("arena_4096", [P, 8192])
        w_upper = sb("w_upper", [P, 6144], F32R)
        sb("arena_18432", [P, 3136])
        w_lower = sb("w_lower", [P, 6144], F32R)
        u_lower = sb("u_lower", [P, 2048], F32R)
        hidden_parts = sb("hidden_parts", [P, 2048], F32R)
        sb("arena_31808", [P, AW - 31808])
        ps = ctx.enter_context(nc.psum_tensor("ps", [P, 8, 512], F32))

        def view(at, *shape, of=arena):
            n = 1
            for s in shape:
                n *= s
            assert at + n <= of.shape[1], (at, shape)
            v = of[:, at:at + n]
            if len(shape) == 2:
                v = v.rearrange("p (a b) -> p a b", b=shape[1])
            elif len(shape) == 3:
                v = v.rearrange("p (a b c) -> p a b c", b=shape[1], c=shape[2])
            return v

        def col(t, c):
            return t[:, c:c + 1]

        def bank(b, *shape):
            v = ps[:, b, :]
            n = 1
            for s in shape:
                n *= s
            v = v[:, 0:n]
            if len(shape) == 2:
                v = v.rearrange("p (a b) -> p a b", b=shape[1])
            elif len(shape) == 3:
                v = v.rearrange("p (a b c) -> p a b c", b=shape[1], c=shape[2])
            return v

        uT = view(0, KT, TOK)

        w_ready = [sem(f"w_ready{s}") for s in range(SLOTS)]
        w_used = sem("w_used")

        def load_tile(sp, T, rnd, src, by_rows=False):
            s = T % SLOTS
            rounds = rnd + T // SLOTS
            number = rounds * SLOTS + s
            sp.wait_ge(w_used, number + 1)
            sp.sem_inc(sem("slots_taken"), 1)
            if by_rows:
                dst = ring[:, s, :].rearrange("p (j n) -> p j n", n=D)
                src = src.rearrange("(j p) n -> p j n", p=P)
            else:
                dst = ring[:, s, :].rearrange("p (k n) -> p k n", n=W)
                src = src.rearrange("(k p) n -> p k n", p=P)
            sp.dma_start(dst, src).then_inc(w_ready[s], 16)

        def skip_tile(sp, T, rnd):
            s = T % SLOTS
            sp.wait_ge(w_used, (rnd + T // SLOTS) * SLOTS + s + 1)
            sp.sem_inc(w_ready[s], 16)

        def landed(pe, T, rnd):
            pe.wait_ge(w_ready[T % SLOTS], (rnd + T // SLOTS + 1) * 16)

        def multiplied(eng, T, rnd):
            eng.wait_ge(w_used, (rnd + T // SLOTS + 1) * SLOTS + T % SLOTS + 1)

        def wcols(T):
            return ring[:, T % SLOTS, :].rearrange("p (k n) -> p k n", n=W)

        def wrows(T):
            return ring[:, T % SLOTS, :].rearrange("p (j n) -> p j n", n=D)

        T_ADA = 0
        T_WIN1 = 24
        T_WOUT1 = T_WIN1 + len(WIN1_FEATURE) + len(WIN1_TOKEN)
        T_MOE = T_WOUT1 + 4
        T_L = T_MOE + 12 * NE
        L_FFN1 = T_L
        L_U5 = L_FFN1 + 3 * NCH
        L_Z = L_U5 + 4
        L_GA = L_Z + 8
        L_XBC = L_GA + 8
        L_GLU = L_XBC + 12
        L_BB = L_GLU + 8
        L_BA = L_BB + 4
        L_WOUT = L_BA + 8
        L_FFN2 = L_WOUT + 4
        L_PAD = L_FFN2 + 3 * NCH
        NPAD = -(L_PAD - T_L) % SLOTS
        ROUNDS = (L_PAD + NPAD - T_L) // SLOTS

        def ffn_loads(sp, T0, rnd, gate, up, down, n_chunks):
            def gu(T, c, r):
                load_tile(sp, T, r, gate(c))
                load_tile(sp, T + 1, r, up(c))
            gu(T0, 0, rnd)
            loops = (n_chunks - 1) // 4
            with sp.Fori(0, loops) as i:
                for c in range(4):
                    gu(T0 + 2 + 3 * c, i * 4 + c + 1, rnd + i * TILES12)
                    load_tile(sp, T0 + 4 + 3 * c, rnd + i * TILES12, down(i * 4 + c), True)
            for c in range(4 * loops, n_chunks):
                if c + 1 < n_chunks:
                    gu(T0 + 2 + 3 * c, c + 1, rnd)
                load_tile(sp, T0 + 4 + 3 * c - (2 if c + 1 == n_chunks else 0), rnd, down(c), True)

        c_col = small[:, 176:184]

        def sp_program(sp):
            sp.sem_inc(w_used, SLOTS)
            sp.dma_start(c_col, a["c"].rearrange("a (k p) -> p (a k)", p=P)).then_inc(sem("c_in"), 16)
            sp.dma_start(x[:], a["x"].rearrange("a (t p) d -> p (a t) d", p=P)).then_inc(sem("x_in"), 16)
            with sp.Fori(0, 2) as i:
                for t in range(12):
                    load_tile(sp, T_ADA + t, i * TILES12, a["ada_w"][0, :, bass.ds(i * 3072 + t * W, W)])
            T = T_WIN1
            for c0 in WIN1_FEATURE + WIN1_TOKEN:
                load_tile(sp, T, 0, a["w_in"][0, :, c0:c0 + W])
                T += 1
            for n in range(4):
                load_tile(sp, T, 0, a["w_out"][0, :, n * W:(n + 1) * W])
                T += 1
            if upto < 2:
                return
            up = a["exp_w_up"].rearrange("a e k n -> (a e) k n")
            dn = a["exp_w_down"].rearrange("a e k n -> (a e) k n")

            def expert_pass(w):
                with sp.Fori(0, NE // 2) as i:
                    for n in range(2):
                        e = i * 2 + n
                        for k, (part, c) in enumerate(EXPERT_TILES):
                            T, rnd = T_MOE + 12 * n + k, (w * NE + i * 2) * TILES12
                            if part == "down":
                                load_tile(sp, T, rnd, dn[e, c * W:(c + 1) * W, :], True)
                            else:
                                c0 = c * W + (D if part == "up" else 0)
                                load_tile(sp, T, rnd, up[e, :, c0:c0 + W])
            expert_pass(0)
            passes = passes_of(sp)
            with sp.If(passes > 1):
                with sp.Fori(1, passes) as w:
                    expert_pass(w)
            if upto < 3:
                return
            nl = LAYERS
            with sp.Fori(0, nl) as li:
                r = li * ROUNDS + (passes - 1) * NE * TILES12

                def ffn(T0, name):
                    ffn_loads(sp, T0, r,
                              lambda c: a[f"{name}_w_gate_2"][li, :, bass.ds(c * W, W)],
                              lambda c: a[f"{name}_w_up_2"][li, :, bass.ds(c * W, W)],
                              lambda c: a[f"{name}_w_down_2"][li, bass.ds(c * W, W), :], NCH)
                ffn(L_FFN1, "ffn1")
                T = L_U5
                win = a["w_in_2"][li]
                for c0 in ([U52 + n * W for n in range(4)] + [Z2 + n * W for n in range(8)]
                           + [GA2 + n * W for n in range(8)] + [XBC2 + n * W for n in range(12)]):
                    load_tile(sp, T, r, win[:, c0:c0 + W])
                    T += 1
                for n in range(4):
                    for half in range(2):
                        load_tile(sp, T, r, a["s5_w_glu_2"][li, :, half * D + n * W:half * D + (n + 1) * W])
                        T += 1
                for n in range(4):
                    load_tile(sp, T, r, a["w_branch_b_2"][li, :, n * W:(n + 1) * W])
                    T += 1
                for n in range(4):
                    for half in range(2):
                        load_tile(sp, T, r, a["w_branch_a_2"][li, half * D:(half + 1) * D, n * W:(n + 1) * W])
                        T += 1
                for n in range(4):
                    load_tile(sp, T, r, a["w_out_2"][li, :, n * W:(n + 1) * W])
                    T += 1
                ffn(L_FFN2, "ffn2")
                for n in range(NPAD):
                    skip_tile(sp, L_PAD + n, r)

        xn = view(4096, TT, D)
        ss = small[:, 0:4]
        eps = small[:, 249:250]
        one = small[:, 250:251]
        zero = small[:, 253:254]

        def pre_norm_act(act, n):
            act.wait_ge(sem("x_new"), n + 1)
            for t in range(TT):
                nc.scalar.activation(xn[:, t, :], x[:, t, :], ACT.Square, accum_out=ss[:, t:t + 1])
            act.drain()
            nc.scalar.activation(ss[:, 2:4], ss[:, 0:2], ACT.Sqrt, bias=eps, scale=1.0 / D).then_inc(
                sem("x_rms"), 1)

        def pre_norm_dve(dve, n):
            dve.wait_ge(sem("x_rms"), n + 1)
            nc.vector.reciprocal(ss[:, 2:4], ss[:, 2:4])
            dve.drain()
            for t in range(TT):
                nc.vector.tensor_scalar(xn[:, t, :], x[:, t, :], ss[:, 2 + t:3 + t], None,
                                        ALU.mult).then_inc(sem("x_normed"), 1)

        def pre_norm_pe(pe, n):
            for t in range(TT):
                pe.wait_ge(sem("x_normed"), TT * n + t + 1)
                for k in range(KT):
                    ins = nc.tensor.transpose(bank(4 + k // 2, 2, TOK)[:, k % 2, t * P:(t + 1) * P],
                                              xn[:, t, k * P:(k + 1) * P], ident[:])
            ins.then_inc(sem("x_turned"), 1)

        def pre_norm_out(dve, n, gain, shift=None, done="u_ready"):
            dve.wait_ge(sem("x_turned"), n + 1)
            for k in range(KT):
                src = bank(4 + k // 2, 2, TOK)[:, k % 2, :]
                if shift is None:
                    ins = nc.vector.tensor_scalar(uT[:, k, :], src, gain(k), None, ALU.mult)
                else:
                    ins = nc.vector.tensor_scalar(uT[:, k, :], src, gain(k), shift(k), ALU.mult, ALU.add)
            ins.then_inc(sem(done), 1)
            dve.drain()

        y_ps = ps[:, 0:4, :].rearrange("p (t h) n -> p t (h n)", t=TT)

        def post_norm_act(act):
            for t in range(TT):
                nc.scalar.activation(xn[:, t, :], y_ps[:, t, :], ACT.Square, accum_out=ss[:, t:t + 1])
            act.drain()
            nc.scalar.activation(ss[:, 2:4], ss[:, 0:2], ACT.Sqrt, bias=eps, scale=1.0 / D).then_inc(
                sem("branch_rms"), 1)

        def post_norm_dve(dve, p, coef):
            dve.wait_ge(sem("branch_rms"), p + 1)
            nc.vector.reciprocal(ss[:, 2:4], ss[:, 2:4])
            dve.drain()
            nc.vector.tensor_scalar(ss[:, 2:4], ss[:, 2:4], coef, None, ALU.mult)
            dve.drain()
            dve.wait_ge(sem("post_gain_in"), (p + 1) * 16)
            for t in range(TT):
                nc.vector.scalar_tensor_tensor(out=xn[:, t, :], in0=y_ps[:, t, :], scalar=ss[:, 2 + t:3 + t],
                                               in1=post_gain[:], op0=ALU.mult, op1=ALU.mult)
            dve.drain()
            nc.vector.tensor_tensor(x[:], x[:], xn, ALU.add).then_inc(sem("x_new"), 1)

        def feature_tile(pe, T, rnd, b, rhs, part=None):
            landed(pe, T, rnd)
            w = wcols(T)
            for m in range(2):
                for k in range(KT):
                    ins = nc.tensor.matmul(bank(b, 2, TOK)[:, m, :], w[:, k, m * P:(m + 1) * P], rhs[:, k, :],
                                           start=(k == 0 and (part is None or (part == 0 and m == 0))),
                                           stop=(k == KT - 1 and part != 0),
                                           skip_group_check=part is not None)
            return ins.then_inc(w_used, 1)

        def token_tile(pe, T, rnd, outs, lhs):
            landed(pe, T, rnd)
            w = wcols(T)
            for t in range(TT):
                for k in range(KT):
                    ins = nc.tensor.matmul(outs[t], lhs[:, k, t * P:(t + 1) * P], w[:, k, :],
                                           start=(k == 0), stop=(k == KT - 1))
            return ins.then_inc(w_used, 1)

        def constants(pool):
            g = nc.gpsimd
            g.memset(ident[:], 0.0)
            g.memset(mask_qk[:], 0.0)
            g.memset(tri[:], 1.0)
            g.memset(mean32[:], 0.0)
            g.memset(mean64[:], 0.0)
            g.memset(mean512[:], 1.0 / 512)
            g.memset(reset64[:], 1.0)
            g.memset(headmask[:], 0.0)
            pool.drain()
            g.affine_select(out=ident[:], in_=ident[:], compare_op=ALU.not_equal, fill=1.0, base=0,
                            pattern=[[-1, P]], channel_multiplier=1)
            g.affine_select(out=mask_qk[:], in_=mask_qk[:], compare_op=ALU.is_ge, fill=NEG, base=0,
                            pattern=[[-1, P]], channel_multiplier=1)
            g.affine_select(out=tri[:, 0:P], in_=tri[:, 0:P], compare_op=ALU.is_ge, fill=0.0, base=0,
                            pattern=[[1, P]], channel_multiplier=-1)
            for i in range(4):
                r = slice(32 * i, 32 * i + 32)
                g.memset(mean32[r, r], 1.0 / 32)
                pool.drain()
                g.memset(headmask[r, i:i + 1], 1.0)
                pool.drain()
            for i in range(2):
                r = slice(64 * i, 64 * i + 64)
                g.memset(mean64[r, r], 1.0 / 64)
                pool.drain()
            g.memset(reset64[:].rearrange("p (c t) -> p c t", t=64)[:, :, 0:1], 0.0)
            g.iota(itmp[:, 0:P], pattern=[[1, P]], base=0, channel_multiplier=0)
            g.iota(itmp[:, P:P + 1], pattern=[[0, 1]], base=0, channel_multiplier=1)
            pool.drain()
            g.tensor_copy(iota_t[:], itmp[:, 0:P]).then_inc(sem("consts"), 1)

        def glmask_dve(dve):
            nc.vector.tensor_scalar(itmp[:, P + 1:P + 2], itmp[:, P:P + 1], 4, None, ALU.arith_shift_right)
            dve.drain()
            nc.vector.tensor_scalar(itmp[:, P + 1:P + 2], itmp[:, P + 1:P + 2], 1, None, ALU.bitwise_and)
            dve.drain()
            nc.vector.tensor_copy(glmask[:, 1:2], itmp[:, P + 1:P + 2])
            dve.drain()
            nc.vector.tensor_scalar(glmask[:, 0:1], glmask[:, 1:2], -1.0, 1.0, ALU.mult, ALU.add)

        stage = view(20480, P)
        cond_b = view(8192, KT, P)
        gmod = view(18432, 2, D)
        QK = view(4096, 8, TOK)
        SQ = view(6144, 8, TOK)
        C_in = view(8192, 2, TOK)
        CR_s = view(8704, 2, TOK)
        DX_c = view(9216, 2, TOK)
        DG_g = view(9728, 2, TOK)
        V_tok = view(10240, 3, TT, W)
        WT = view(11776, 8, 384)
        S = view(14848, 4, 384)
        yT = view(16384, KT, TOK)
        hid_flat = ffn_buf[:, 0:1024]
        gat_flat = ffn_buf[:, 1024:2048]
        wg2 = hid_flat[:, 0:128]
        wcg = hid_flat[:, 128:256].rearrange("p (k n) -> p k n", n=16)
        wbd = hid_flat[:, 256:768].rearrange("p (w t n) -> p w t n", w=2, t=2)
        lamv = hid_flat[:, 768:896].rearrange("p (a b) -> p a b", b=32)
        router = gat_flat[:, 0:256].rearrange("p (k n) -> p k n", n=NE)
        routb = gat_flat[:, 256:288]

        def small_loads_1(pool):
            dma = pool.dma_start
            s = sem("vec1_in")
            cnt = 0

            def rows(name, src, n):
                nonlocal cnt
                dma(stage[V1[name]:V1[name] + n, :], src).then_inc(s, 16)
                cnt += 16

            pool.wait_ge(sem("zeroed"), 1)
            for name in ("norm1_g", "norm2_g"):
                rows(name, a[name].rearrange("a (r p) -> (a r) p", p=P), 8)
            ab = a["ada_b"].rearrange("a (s r p) -> (a s) r p", r=8, p=P)
            for n, j in (("sh0", 0), ("sc0", 1), ("sh1", 3), ("sc1", 4)):
                rows(n, ab[j], 8)
            rows("d_conv_w", a["d_conv_w"].rearrange("a k (r p) -> (a k r) p", p=P), 8)
            for name in ("d_conv_b", "d_b_a", "d_b_x", "d_lambda"):
                rows(name, a[name].rearrange("a (r p) -> (a r) p", p=P), 2)
            rows("c_b_g", a["c_b_g"], 1)
            for name, n in (("a_q_gain", 32), ("a_k_gain", 32), ("b_q_gain", 64), ("b_k_gain", 64),
                            ("a_out_gain", 64), ("c_out_gain", 64)):
                for j in range(P // n):
                    r = V1[name]
                    dma(stage[r:r + 1, j * n:(j + 1) * n], a[name]).then_inc(s, 16)
                    cnt += 16
            assert cnt == VEC1_IN
            dma(gmod[:, 0, :], bcast(a["ada_b"][0:1, 2048:3072])).then_inc(sem("gmod_in"), 16)
            dma(gmod[:, 1, :], bcast(a["ada_b"][0:1, 5120:6144])).then_inc(sem("gmod_in"), 16)
            s = sem("small1_in")
            dma(wg2[0:16, :], a["c_w_g2"][0]).then_inc(s, 16)
            dma(wcg, a["w_in"][0, :, CG:CG + 16].rearrange("(k p) n -> p k n", p=P)).then_inc(s, 16)
            for wi, name in enumerate(("d_w_a", "d_w_x")):
                for b in range(4):
                    r = slice(64 * (b % 2), 64 * (b % 2) + 64)
                    dma(wbd[r, wi, b // 2, r], a[name][0, b]).then_inc(s, 16)
            for j, name in enumerate(("a_lam_q1", "a_lam_k1", "a_lam_q2", "a_lam_k2")):
                dma(lamv[:, j, :], bcast(a[name])).then_inc(s, 16)
            dma(router, a["router_w"][0].rearrange("(k p) n -> p k n", p=P)).then_inc(s, 16)
            dma(routb, bcast(a["router_b"])).then_inc(s, 16)

        VEC1_IN = 16 * (2 + 4 + 1 + 4 + 1 + 2 * 4 + 4 * 2)
        SMALL1_IN = 16 * (1 + 1 + 8 + 4 + 2)

        def bcast(src):
            return src.to_broadcast([P, src.shape[1]])

        modc = small[:, 16:48]
        mod_row = view(10240, 4096)

        def mod_dve(dve):
            nc.vector.memset(stage, 0.0)
            nc.vector.memset(hid_flat[:, 256:768], 0.0)
            dve.drain()
            nc.vector.memset(eps, EPS).then_inc(sem("modc_done"), 1)
            nc.vector.memset(zero, 0.0).then_inc(sem("gmod_done"), 1)
            nc.vector.memset(small[:, 254:255], 0.0).then_inc(sem("stage_used"), 1)
            nc.vector.memset(one, 1.0).then_inc(sem("zeroed"), 1)
            dve.wait_ge(sem("cond_ready"), 1)
            nc.vector.tensor_copy(cond_b, small[:, 8:16].unsqueeze(2).to_broadcast([P, KT, P])).then_inc(
                sem("cond_rows"), 1)
            dve.wait_ge(sem("gmod_in"), 32)
            with dve.Fori(0, 2) as i:
                multiplied(dve, T_ADA + 7, i * TILES12)
                nc.vector.tensor_copy(mod_row[0:1, bass.ds(i * 2048, 2048)],
                                      ps[0:1, 4:8, :].rearrange("p a b -> p (a b)")).then_inc(
                                          sem("modc_done"), 1)
                multiplied(dve, T_ADA + 11, i * TILES12)
                g = gmod[:, i, :]
                nc.vector.tensor_tensor(g, g, ps[:, 2:4, :].rearrange("p a b -> p (a b)"), ALU.add).then_inc(
                    sem("gmod_done"), 1)
            dve.wait_ge(sem("consts"), 1)
            dve.wait_ge(sem("vec1_turned"), 1)
            nc.vector.tensor_copy(vec1[:, 0:NV1], bank(1, P)[:, 0:NV1])
            dve.drain()
            nc.vector.tensor_tensor(modc, bank(0, 32), vec1[:, V1["sh0"]:V1["sh0"] + 32], ALU.add)
            dve.drain()
            for i, name in enumerate(("norm1_g", "norm2_g")):
                c = modc[:, 16 * i + 8:16 * i + 16]
                ins = nc.vector.scalar_tensor_tensor(out=c, in0=c, scalar=1.0, in1=vec1[:, V1[name]:V1[name] + 8],
                                                     op0=ALU.add, op1=ALU.mult)
            dve.drain()

        def mod_act(act):
            act.wait_ge(sem("c_in"), 16)
            nc.scalar.activation(small[:, 8:16], c_col, ACT.Silu).then_inc(
                sem("cond_ready"), 1)

        def mod_pe(pe):
            pe.sem_inc(sem("tile_mm"), 1)
            pe.wait_ge(sem("cond_rows"), 1)
            with pe.Fori(0, 2) as i:
                pe.wait_ge(sem("modc_done"), i + 1)
                for t in range(8):
                    landed(pe, T_ADA + t, i * TILES12)
                    w = wcols(T_ADA + t)
                    for k in range(KT):
                        ins = nc.tensor.matmul(bank(4 + t // 2, 2, W)[0:1, t % 2, :], small[:, 8 + k:9 + k],
                                               w[:, k, :], start=(k == 0), stop=(k == KT - 1))
                    ins.then_inc(w_used, 1)
                pe.wait_ge(sem("gmod_done"), i + 1)
                for t in range(4):
                    landed(pe, T_ADA + 8 + t, i * TILES12)
                    w = wcols(T_ADA + 8 + t)
                    for k in range(KT):
                        ins = nc.tensor.matmul(bank(2 + t // 2, 2, W)[:, t % 2, :], cond_b[:, k, :], w[:, k, :],
                                               start=(k == 0), stop=(k == KT - 1))
                    ins.then_inc(w_used, 1)
            pe.wait_ge(sem("modc_done"), 3)
            for c in range(32):
                nc.tensor.matmul(bank(0, 32)[:, c:c + 1], mod_row[0:1, c * P:(c + 1) * P], one[0:1, :],
                                 start=True, stop=True)
            pe.wait_ge(sem("consts"), 1)
            pe.wait_ge(sem("vec1_in"), VEC1_IN)
            nc.tensor.transpose(bank(1, P), stage, ident[:]).then_inc(sem("vec1_turned"), 1)

        col1 = {n: vec1[:, V1[n]:V1[n] + 1] for n in V1}
        glow = view(20608, TOK)
        NF = len(WIN1_FEATURE)

        def win1_pe(pe):
            pe.wait_ge(sem("u_ready"), 1)
            for n in range(NF):
                feature_tile(pe, T_WIN1 + n, 0, n, uT)
            for n in range(3):
                pe.wait_ge(sem("qk_raw"), n + 1)
                token_tile(pe, T_WIN1 + NF + n, 0, [bank(n, 2, W)[:, t, :] for t in range(TT)], uT)
            pe.wait_ge(sem("qk_raw"), 4)
            pe.wait_ge(sem("small1_in"), SMALL1_IN)
            for k in range(KT):
                ins = nc.tensor.matmul(bank(3, TOK)[0:16, :], wcg[:, k, :], uT[:, k, :],
                                       start=(k == 0), stop=(k == KT - 1))
            ins.then_inc(sem("glow_mm"), 1)

        def win1_dve(dve):
            for n in range(4):
                multiplied(dve, T_WIN1 + n, 0)
                nc.vector.tensor_copy(QK[:, 2 * n:2 * n + 2, :], bank(n, 2, TOK)).then_inc(sem("qk_raw"), 1)
            multiplied(dve, T_WIN1 + 4, 0)
            nc.vector.tensor_copy(C_in, bank(4, 2, TOK)).then_inc(sem("c_raw"), 1)
            multiplied(dve, T_WIN1 + 6, 0)
            cw = V1["d_conv_w"]
            for t in range(2):
                nc.vector.tensor_scalar(DX_c[:, t, :], bank(6, 2, TOK)[:, t, :], col(vec1, cw + 6 + t),
                                        col(vec1, V1["d_conv_b"] + t), ALU.mult, ALU.add)
            for lag in (1, 2, 3):
                dve.drain()
                for t in range(2):
                    ins = nc.vector.scalar_tensor_tensor(
                        out=DX_c[:, t, lag:], in0=bank(6, 2, TOK)[:, t, 0:TOK - lag],
                        scalar=col(vec1, cw + 2 * (3 - lag) + t), in1=DX_c[:, t, lag:], op0=ALU.mult, op1=ALU.add)
            ins.then_inc(sem("dx_conv"), 1)
            for n in range(3):
                multiplied(dve, T_WIN1 + NF + n, 0)
                nc.vector.tensor_copy(V_tok[:, n, :, :], bank(n, 2, W)).then_inc(sem("v_tok"), 1)
            dve.wait_ge(sem("glow_mm"), 1)
            nc.vector.tensor_copy(glow[0:16, :], bank(3, TOK)[0:16, :]).then_inc(sem("glow"), 1)

        def win1_act(act):
            for n in range(4):
                act.wait_ge(sem("qk_raw"), n + 1)
                nc.scalar.activation(SQ[:, 2 * n:2 * n + 2, :], QK[:, 2 * n:2 * n + 2, :], ACT.Square).then_inc(
                    sem("qk_squares"), 1)
            multiplied(act, T_WIN1 + 5, 0)
            nc.scalar.activation(CR_s, bank(5, 2, TOK), ACT.Silu).then_inc(sem("act_gates"), 1)
            multiplied(act, T_WIN1 + 7, 0)
            nc.scalar.activation(DG_g, bank(7, 2, TOK), ACT.Gelu_apprx_tanh).then_inc(sem("act_gates"), 1)

        mx = small[:, 64:72]
        nmx = small[:, 72:80]
        sums = small[:, 80:88]
        lam = small[:, 88:92]
        HEADS_OF = ((0, 1), (2, 3), (4, 5, 6, 7))

        def qk_norm_pe(pe):
            pe.wait_ge(sem("qk_squares"), 4)
            pe.wait_ge(sem("c_raw"), 1)
            pe.wait_ge(sem("act_gates"), 2)
            pe.wait_ge(sem("dx_conv"), 1)
            for t in range(8):
                ins = nc.tensor.matmul(bank(4 + t // 2, 2, TOK)[:, t % 2, :], mean32[:] if t < 4 else mean64[:],
                                       SQ[:, t, :], start=True, stop=True)
            ins.then_inc(sem("qk_mean"), 1)

        def qk_norm_dve(dve):
            dve.wait_ge(sem("small1_in"), SMALL1_IN)
            nc.vector.tensor_tensor(lamv[:, 0, :], lamv[:, 0, :], lamv[:, 1, :], ALU.mult)
            nc.vector.tensor_tensor(lamv[:, 2, :], lamv[:, 2, :], lamv[:, 3, :], ALU.mult)
            dve.drain()
            nc.vector.tensor_reduce(lam[:, 0:1], lamv[:, 0, :], AX, ALU.add)
            nc.vector.tensor_reduce(lam[:, 1:2], lamv[:, 2, :], AX, ALU.add).then_inc(sem("lam_sums"), 1)
            dve.wait_ge(sem("qk_rms"), 1)
            nc.vector.reciprocal(SQ, SQ)
            dve.drain()
            for n, g in enumerate(("a_q_gain", "a_k_gain", "b_q_gain", "b_k_gain")):
                t = slice(2 * n, 2 * n + 2)
                ins = nc.vector.scalar_tensor_tensor(out=QK[:, t, :], in0=QK[:, t, :], scalar=col1[g],
                                                     in1=SQ[:, t, :], op0=ALU.mult, op1=ALU.mult)
            ins.then_inc(sem("qk_ready"), 1)
            dve.wait_ge(sem("lam_exps"), 1)
            nc.vector.tensor_tensor(lam[:, 3:4], lam[:, 1:2], lam[:, 0:1], ALU.subtract)
            dve.drain()
            nc.vector.tensor_scalar(lam[:, 3:4], lam[:, 3:4], -LAM0, None, ALU.add)
            dve.drain()

        def lam_act(act):
            act.wait_ge(sem("lam_sums"), 1)
            nc.scalar.activation(lam[:, 0:2], lam[:, 0:2], ACT.Exp).then_inc(sem("lam_exps"), 1)
            act.wait_ge(sem("qk_mean"), 1)
            nc.scalar.activation(SQ.rearrange("p a b -> p (a b)"), ps[:, 4:8, :].rearrange("p a b -> p (a b)"),
                                 ACT.Sqrt, bias=eps).then_inc(sem("qk_rms"), 1)

        def attention_pe(pe):
            pe.wait_ge(sem("qk_ready"), 1)
            pe.wait_ge(sem("v_tok"), 3)
            pe.wait_ge(sem("glow"), 1)
            for r in range(3):
                if r:
                    pe.wait_ge(sem("scores_read"), r)
                for i in range(4):
                    rows, qt, kt = ((slice(32 * i, 32 * i + 32), r, 2 + r) if r < 2 else
                                    (slice(64 * (i % 2), 64 * (i % 2) + 64), 4 + i // 2, 6 + i // 2))
                    nc.tensor.matmul(bank(i, 384)[:, 0:P], QK[rows, qt, 0:P], QK[rows, kt, 0:P],
                                     start=True, stop=True)
                    ins = nc.tensor.matmul(bank(i, 384)[:, P:384], QK[rows, qt, P:TOK], QK[rows, kt, :],
                                           start=True, stop=True)
                ins.then_inc(sem("scores"), 1)
                pe.wait_ge(sem("probs"), r + 1)
                if r == 0:
                    pe.wait_ge(sem("qk_rms"), 1)
                for hh in range(len(HEADS_OF[r])):
                    m = hh * (2 if r < 2 else 1)
                    for part in range(3):
                        c = slice(P * part, P * part + P)
                        ins = nc.tensor.transpose(bank(4 + hh, 384)[:, c], S[:, m, c], ident[:])
                ins.then_inc(sem("probs_turned"), 1)
            pe.wait_ge(sem("wt_ready"), 3)
            for h in range(8):
                j, hh = h // 4, h % 4
                o = bank(j, 2, TOK)[64 * (h % 2):64 * (h % 2) + 64, hh // 2, :]
                v = slice(64 * hh, 64 * hh + 64)
                nc.tensor.matmul(o, V_tok[:, j, 0, v], WT[:, h, 0:TOK], start=True, stop=False,
                                 skip_group_check=True)
                ins = nc.tensor.matmul(o[:, P:TOK], V_tok[:, j, 1, v], WT[:, h, TOK:384], start=False,
                                       stop=True, skip_group_check=True)
            ins.then_inc(sem("attended"), 1)

        def attention_dve(dve):
            for r in range(3):
                dve.wait_ge(sem("scores"), r + 1)
                mask = mask_qk[:].unsqueeze(1).to_broadcast([P, 4, P])
                nc.vector.tensor_tensor(S[:, :, 0:P], ps[:, 0:4, 0:P], mask, ALU.add)
                nc.vector.tensor_copy(S[:, :, P:TOK], ps[:, 0:4, P:TOK])
                nc.vector.tensor_tensor(S[:, :, TOK:384], ps[:, 0:4, TOK:384], mask, ALU.add).then_inc(
                    sem("scores_read"), 1)
                dve.drain()
                nc.vector.tensor_reduce(mx[:, 0:4], S[:, :, 0:P], AX, ALU.max)
                nc.vector.tensor_reduce(mx[:, 4:8], S[:, :, P:384], AX, ALU.max)
                dve.drain()
                scale = (32 if r < 2 else 64) ** -0.5
                nc.vector.tensor_scalar(nmx, mx, -scale, None, ALU.mult).then_inc(sem("row_max"), 1)
                dve.wait_ge(sem("exps"), r + 1)
                nc.vector.reciprocal(sums, sums)
                dve.drain()
                if r < 2:
                    s2 = sums.rearrange("p (q a i) -> p q a i", q=2, i=2)[:, :, :, 1]
                    nc.vector.tensor_scalar(s2, s2, lam[:, 3:4], None, ALU.mult)
                    dve.drain()
                for q, c in ((0, slice(0, P)), (1, slice(P, 384))):
                    for i in range(4):
                        ins = nc.vector.tensor_scalar(S[:, i, c], S[:, i, c], sums[:, 4 * q + i:4 * q + i + 1],
                                                      None, ALU.mult)
                if r < 2:
                    dve.drain()
                    ins = nc.vector.tensor_tensor(S[:, 0:4:2, :], S[:, 0:4:2, :], S[:, 1:4:2, :], ALU.add)
                ins.then_inc(sem("probs"), 1)
                h0, n = HEADS_OF[r][0], len(HEADS_OF[r])
                dve.wait_ge(sem("probs_turned"), r + 1)
                nc.vector.tensor_copy(WT[:, h0:h0 + n, :], ps[:, 4:4 + n, 0:384]).then_inc(sem("wt_ready"), 1)
            dve.wait_ge(sem("attended"), 1)
            nc.vector.tensor_copy(yT[:, 2:4, :], bank(1, 2, TOK))
            nc.vector.tensor_copy(QK[:, 0:2, :], bank(0, 2, TOK)).then_inc(sem("heads_out_raw"), 1)
            dve.wait_ge(sem("heads_out_rms"), 1)
            nc.vector.reciprocal(QK[:, 4:6, :], QK[:, 4:6, :])
            nc.vector.tensor_scalar(lam[:, 0:1], col1["a_out_gain"], 1.0 - LAM0, None, ALU.mult)
            dve.drain()
            nc.vector.scalar_tensor_tensor(out=yT[:, 0:2, :], in0=QK[:, 0:2, :], scalar=lam[:, 0:1],
                                           in1=QK[:, 4:6, :], op0=ALU.mult, op1=ALU.mult)
            dve.drain()

        def attention_act(act):
            for r in range(3):
                act.wait_ge(sem("row_max"), r + 1)
                scale = (32 if r < 2 else 64) ** -0.5
                for q, c in ((0, slice(0, P)), (1, slice(P, 384))):
                    for i in range(4):
                        j = 4 * q + i
                        ins = nc.scalar.activation(S[:, i, c], S[:, i, c], ACT.Exp, bias=nmx[:, j:j + 1],
                                                   scale=scale, accum_out=sums[:, j:j + 1])
                ins.then_inc(sem("exps"), 1)
            act.wait_ge(sem("heads_out_raw"), 1)
            nc.scalar.activation(QK[:, 2:4, :], QK[:, 0:2, :], ACT.Square).then_inc(sem("heads_out_squares"), 1)
            act.wait_ge(sem("heads_out_mean"), 1)
            nc.scalar.activation(QK[:, 4:6, :], bank(2, 2, TOK), ACT.Sqrt, bias=eps).then_inc(sem("heads_out_rms"), 1)

        def oa_mean_pe(pe):
            pe.wait_ge(sem("heads_out_squares"), 1)
            for t in range(2):
                ins = nc.tensor.matmul(bank(2, 2, TOK)[:, t, :], mean64[:], QK[:, 2 + t, :], start=True, stop=True)
            ins.then_inc(sem("heads_out_mean"), 1)

        NCK = TOK // 64
        E = view(4096, 4, TOK)
        QE = view(5120, 2, TOK)
        KM = view(5632, 4, TOK)
        KD = view(6656, TOK)
        KDT = view(6912, 2, P)
        SBD = view(7168, 3, 4, 64)
        G = view(7936, TOK)
        attS = view(14848, 2, 4, P)
        St = view(16128, 3, 64)
        OC = view(11776, 2, TOK)
        OC2 = view(12288, 2, TOK)
        RG = view(12800, 2, 2, TOK)
        clam = small[:, 92:98]

        def chunks(v):
            return v.rearrange("p (c t) -> p c t", t=64)

        def gla_dve(dve):
            dve.wait_ge(sem("gate_mm"), 1)
            nc.vector.tensor_scalar(G, bank(4, TOK), col1["c_b_g"], None, ALU.add).then_inc(sem("gate_raw"), 1)
            nc.vector.memset(attS, 0.0)
            dve.wait_ge(sem("gate_log"), 1)
            nc.vector.scalar_tensor_tensor(out=G, in0=G, scalar=0.0, in1=E[:, 1, :], op0=ALU.min,
                                           op1=ALU.subtract)
            dve.drain()
            nc.vector.tensor_scalar(G, G, 1.0 / 16, None, ALU.mult)
            dve.drain()
            nc.vector.tensor_tensor_scan(E[:, 0, :], reset64[:], G, 0.0, ALU.mult, ALU.add)
            dve.drain()
            b = chunks(E[:, 0, :])
            mid = b[:, :, 31:32].to_broadcast([P, NCK, 64])
            end = b[:, :, 63:64].to_broadcast([P, NCK, 64])
            nc.vector.tensor_tensor(chunks(E[:, 1, :]), b, mid, ALU.subtract)
            nc.vector.tensor_tensor(chunks(E[:, 2, :]), mid, b, ALU.subtract)
            nc.vector.tensor_tensor(chunks(E[:, 3, :]), end, b, ALU.subtract)
            dve.drain()
            nc.vector.tensor_scalar(E[:, 1:3, :], E[:, 1:3, :], 80.0, None, ALU.min).then_inc(sem("decays"), 1)
            dve.wait_ge(sem("decay_exps"), 1)
            for j in range(2):
                nc.vector.scalar_tensor_tensor(out=QE[:, j, :], in0=C_in[:, 0, :], scalar=32.0 ** -0.5,
                                               in1=E[:, j, :], op0=ALU.mult, op1=ALU.mult)
            for h in range(4):
                ins = nc.vector.scalar_tensor_tensor(out=KM[:, h, :], in0=C_in[:, 1, :], scalar=col(headmask, h),
                                                     in1=E[:, 2, :], op0=ALU.mult, op1=ALU.mult)
            nc.vector.tensor_tensor(KD, C_in[:, 1, :], E[:, 3, :], ALU.mult).then_inc(sem("keys"), 1)
            dve.wait_ge(sem("kd_turned"), 1)
            nc.vector.tensor_copy(KDT, bank(5, 2, P)).then_inc(sem("kdt"), 1)
            dve.wait_ge(sem("att"), 1)
            for par in range(2):
                r = slice(64 * par, 64 * par + 64)
                ins = nc.vector.tensor_tensor(
                    attS[r, :, :, r].rearrange("p t h i -> p h t i"), bank(6, 4, 2, 64)[r],
                    tri[r, r].unsqueeze(1).unsqueeze(1).to_broadcast([64, 4, 2, 64]), ALU.mult)
            ins.then_inc(sem("att_masked"), 1)
            dve.wait_ge(sem("updates"), 1)
            nc.vector.tensor_copy(St[:, 0, :], bank(7, 3, 64)[:, 0, :])
            for c in (1, 2):
                dve.drain()
                nc.vector.scalar_tensor_tensor(out=St[:, c, :], in0=St[:, c - 1, :],
                                               scalar=E[:, 0, 64 * c + 63:64 * c + 64],
                                               in1=bank(4 if c == 1 else 7, 3, 64)[:, c, :],
                                               op0=ALU.mult, op1=ALU.add)
            dve.drain()
            for c in range(3):
                ins = nc.vector.tensor_tensor(SBD[:, c, :, :], St[:, c, :].unsqueeze(1).to_broadcast([P, 4, 64]),
                                              headmask[:].unsqueeze(2).to_broadcast([P, 4, 64]), ALU.mult)
            ins.then_inc(sem("states"), 1)
            dve.wait_ge(sem("gla_out"), 1)
            for j in range(2):
                ins = nc.vector.tensor_copy(OC[:, j, :], bank(j, TOK))
            ins.then_inc(sem("heads_out_raw"), 1)
            lamc = vec1[:, V1["d_lambda"]:V1["d_lambda"] + 2]
            nc.vector.tensor_scalar(clam[:, 4:6], lamc, 0.0, None, ALU.min)
            dve.wait_ge(sem("heads_out_rms"), 2)
            nc.vector.reciprocal(OC2, OC2)
            dve.drain()
            nc.vector.scalar_tensor_tensor(out=OC, in0=OC, scalar=col1["c_out_gain"], in1=OC2,
                                           op0=ALU.mult, op1=ALU.mult)
            dve.drain()
            nc.vector.tensor_tensor(yT[:, 4:6, :], OC, CR_s, ALU.mult)

        def gla_act(act):
            act.wait_ge(sem("gate_raw"), 1)
            nc.scalar.activation(E[:, 1, :], G, ACT.Abs)
            act.drain()
            nc.scalar.activation(E[:, 1, :], E[:, 1, :], ACT.Exp, scale=-1.0)
            act.drain()
            nc.scalar.activation(E[:, 1, :], E[:, 1, :], ACT.Ln, bias=one).then_inc(sem("gate_log"), 1)
            act.wait_ge(sem("decays"), 1)
            nc.scalar.activation(E, E, ACT.Exp).then_inc(sem("decay_exps"), 1)
            act.wait_ge(sem("heads_out_raw"), 2)
            nc.scalar.activation(OC2, OC, ACT.Square).then_inc(sem("heads_out_squares"), 1)
            act.wait_ge(sem("heads_out_mean"), 2)
            nc.scalar.activation(OC2, bank(2, 2, TOK), ACT.Sqrt, bias=eps).then_inc(sem("heads_out_rms"), 1)
            nc.scalar.activation(clam[:, 0:2], vec1[:, V1["d_lambda"]:V1["d_lambda"] + 2], ACT.Abs)
            act.drain()
            nc.scalar.activation(clam[:, 2:4], clam[:, 0:2], ACT.Exp, scale=-1.0)
            act.drain()
            nc.scalar.activation(clam[:, 2:4], clam[:, 2:4], ACT.Ln, bias=one).then_inc(sem("clam_log"), 1)

        def gla_pe(pe):
            nc.tensor.matmul(bank(4, TOK), wg2[0:16, :], glow[0:16, :], start=True, stop=True).then_inc(
                sem("gate_mm"), 1)
            pe.wait_ge(sem("keys"), 1)
            for t in range(2):
                ins = nc.tensor.transpose(bank(5, 2, P)[:, t, :], KD[:, t * P:(t + 1) * P], ident[:])
            ins.then_inc(sem("kd_turned"), 1)
            for h in range(4):
                for c in range(NCK):
                    cs = slice(64 * c, 64 * c + 64)
                    ins = nc.tensor.matmul(bank(6, 4, 2, 64)[64 * (c % 2):64 * (c % 2) + 64, h, c // 2, :],
                                           KM[:, h, cs], QE[:, 1, cs], start=True, stop=True)
            ins.then_inc(sem("att"), 1)
            pe.wait_ge(sem("kdt"), 1)
            for c in range(3):
                r = slice(64 * (c % 2), 64 * (c % 2) + 64)
                for h in range(4):
                    ins = nc.tensor.matmul(bank(4 if c == 1 else 7, 3, 64)[32 * h:32 * h + 32, c, :],
                                           KDT[r, c // 2, 32 * h:32 * h + 32],
                                           V_tok[r, 2, c // 2, 64 * h:64 * h + 64], start=True, stop=True)
            ins.then_inc(sem("updates"), 1)
            pe.wait_ge(sem("att_masked"), 1)
            pe.wait_ge(sem("states"), 1)
            for hp in range(2):
                for h in (2 * hp, 2 * hp + 1):
                    for t in range(2):
                        nc.tensor.matmul(bank(hp, TOK)[64 * (h % 2):64 * (h % 2) + 64, t * P:(t + 1) * P],
                                         V_tok[:, 2, t, 64 * h:64 * h + 64], attS[:, t, h, :],
                                         start=(t == 0), stop=False, skip_group_check=True)
                for c in range(1, NCK):
                    cs = slice(64 * c, 64 * c + 64)
                    ins = nc.tensor.matmul(bank(hp, TOK)[:, cs],
                                           SBD[:, c - 1, 2 * hp:2 * hp + 2, :].rearrange("p h e -> p (h e)"),
                                           QE[:, 0, cs], start=False, stop=(c == NCK - 1), skip_group_check=True)
            ins.then_inc(sem("gla_out"), 1)
            pe.wait_ge(sem("heads_out_squares"), 2)
            for t in range(2):
                ins = nc.tensor.matmul(bank(2, 2, TOK)[:, t, :], mean64[:], OC2[:, t, :], start=True, stop=True)
            ins.then_inc(sem("heads_out_mean"), 1)

        def lru_pe(pe):
            for w in range(2):
                for t in range(2):
                    ins = nc.tensor.matmul(bank(5 + w, 2, TOK)[:, t, :], wbd[:, w, t, :], DX_c[:, t, :],
                                           start=True, stop=True)
            ins.then_inc(sem("lru_gates_mm"), 1)

        def lru_act(act):
            act.wait_ge(sem("lru_gates_mm"), 1)
            for w, b in enumerate(("d_b_a", "d_b_x")):
                for t in range(2):
                    ins = nc.scalar.activation(RG[:, w, t, :], bank(5 + w, 2, TOK)[:, t, :], ACT.Sigmoid,
                                               bias=col(vec1, V1[b] + t))
            ins.then_inc(sem("lru_gates"), 1)
            act.wait_ge(sem("lru_inputs"), 1)
            nc.scalar.activation(OC2, RG[:, 0, :, :], ACT.Tanh, scale=-1.0)
            nc.scalar.activation(OC, RG[:, 0, :, :], ACT.Exp).then_inc(sem("lru_outputs"), 1)
            act.wait_ge(sem("lru_inputs"), 2)
            nc.scalar.activation(OC2, OC2, ACT.Sqrt).then_inc(sem("lru_outputs"), 1)

        def lru_dve(dve):
            dve.wait_ge(sem("clam_log"), 1)
            nc.vector.tensor_tensor(clam[:, 4:6], clam[:, 4:6], clam[:, 2:4], ALU.subtract)
            dve.drain()
            nc.vector.tensor_scalar(clam[:, 4:6], clam[:, 4:6], 8.0, None, ALU.mult)
            dve.wait_ge(sem("lru_gates"), 1)
            dve.drain()
            for t in range(2):
                nc.vector.tensor_scalar(RG[:, 0, t, :], RG[:, 0, t, :], clam[:, 4 + t:5 + t], None, ALU.mult)
            nc.vector.tensor_tensor(RG[:, 1, :, :], RG[:, 1, :, :], DX_c, ALU.mult).then_inc(sem("lru_inputs"), 1)
            dve.wait_ge(sem("lru_outputs"), 1)
            nc.vector.tensor_tensor(RG[:, 0, :, :], OC, OC, ALU.mult)
            dve.drain()
            nc.vector.scalar_tensor_tensor(out=OC2, in0=RG[:, 0, :, :], scalar=1.0, in1=OC2, op0=ALU.add,
                                           op1=ALU.mult).then_inc(sem("lru_inputs"), 1)
            dve.wait_ge(sem("lru_outputs"), 2)
            nc.vector.tensor_tensor(RG[:, 1, :, :], RG[:, 1, :, :], OC2, ALU.mult)
            dve.drain()
            for t in range(2):
                nc.vector.tensor_tensor_scan(RG[:, 0, t, :], OC[:, t, :], RG[:, 1, t, :], 0.0, ALU.mult, ALU.add)
            dve.drain()
            nc.vector.tensor_tensor(yT[:, 6:8, :], RG[:, 0, :, :], DG_g, ALU.mult).then_inc(sem("yt1_ready"), 1)

        def wout1_pe(pe):
            pe.wait_ge(sem("yt1_ready"), 1)
            for n in range(4):
                token_tile(pe, T_WOUT1 + n, 0,
                           [bank(2 * t + n // 2, 2, W)[:, n % 2, :] for t in range(TT)], yT)

        def wout1_dve(dve, half):
            nc.vector.tensor_tensor(xn, y_ps, gmod[:, half, :].unsqueeze(1).to_broadcast([P, TT, D]), ALU.mult)
            dve.drain()
            nc.vector.tensor_tensor(x[:], x[:], xn, ALU.add).then_inc(sem("x_new"), 1)

        GB = view(4096, NE, TOK)
        b_up = view(12288, NE * 16)
        b_down = view(12800, D)
        b_up_rows = view(13824, 4, P)
        L = view(14336, TT, NE)
        R = view(14400, 5, TT, NE)
        gates = view(14720, TT, NE)
        gT = view(14848, TOK)
        m8 = small[:, 100:116].rearrange("p (t n) -> p t n", t=2)
        rs = small[:, 116:124].rearrange("p (t n) -> p t n", t=2)

        def moe_small_loads(pool):
            pool.wait_ge(sem("x_new"), 2)
            pool.dma_start(b_up_rows, a["exp_b_up"][0].rearrange("(j e) (m p) -> (e m) j p", j=4, p=P)
                           ).then_inc(sem("moe_small_in"), 16)
            pool.dma_start(b_down[0:NE, :], a["exp_b_down"][0]).then_inc(sem("moe_small_in"), 16)

        def passes_of(eng):
            eng.wait_ge(sem("passes"), 1)
            return eng.value_load(itmp[0:1, P + 1:P + 2], min_val=1, max_val=PASSES)

        def router_pe(pe):
            pe.wait_ge(sem("moe_small_in"), 32)
            for j in range(4):
                ins = nc.tensor.transpose(bank(0, 4, P)[:, j, :], b_up_rows[:, j, :], ident[:])
            ins.then_inc(sem("bup_turned"), 1)
            pe.wait_ge(sem("u_ready"), 2)
            for t in range(TT):
                for k in range(KT):
                    ins = nc.tensor.matmul(bank(1, TT, NE)[:, t, :], uT[:, k, t * P:(t + 1) * P], router[:, k, :],
                                           start=(k == 0), stop=(k == KT - 1))
            ins.then_inc(sem("logits"), 1)
            for t in range(TT):
                for k in range(KT):
                    ins = nc.tensor.transpose(bank(4 + 2 * t + k // 4, 4, P)[:, k % 4, :],
                                              uT[:, k, t * P:(t + 1) * P], ident[:])
            ins.then_inc(sem("h_turned"), 1)
            pe.wait_ge(sem("routed"), 1)
            m = R[:, 1, :, :]
            o = bank(3, TT + 1, NE)
            nc.tensor.matmul(o[:, 0, :], tri[:, 0:P], m[:, 0, :], start=True, stop=True)
            nc.tensor.matmul(o[:, 1, :], tri[:, P:2 * P], m[:, 0, :], start=True, stop=False)
            nc.tensor.matmul(o[:, 1, :], tri[:, 0:P], m[:, 1, :], start=False, stop=True)
            nc.tensor.matmul(o[:, 2, :], tri[:, P:2 * P], m[:, 0, :], start=True, stop=False)
            nc.tensor.matmul(o[:, 2, :], tri[:, P:2 * P], m[:, 1, :], start=False, stop=True).then_inc(
                sem("ranks_mm"), 1)
            pe.wait_ge(sem("gates"), 1)
            for t in range(TT):
                ins = nc.tensor.transpose(bank(2, TOK)[0:NE, t * P:(t + 1) * P], gates[:, t, :], ident[:])
            ins.then_inc(sem("gates_turned"), 1)
            pe.wait_ge(sem("gates_t"), 1)
            for t in range(TT):
                for h in range(2):
                    nc.tensor.matmul(ps[:, 2 * t + h, :], gT[0:NE, t * P:(t + 1) * P],
                                     b_down[0:NE, 512 * h:512 * h + 512], start=True, stop=False,
                                     skip_group_check=True)

        def router_act(act):
            act.wait_ge(sem("shifted"), 1)
            nc.scalar.activation(R[:, 0, :, :], R[:, 0, :, :], ACT.Exp).then_inc(sem("logit_exps"), 1)
            act.wait_ge(sem("h_turned"), 1)
            nc.scalar.activation(xn.rearrange("p a b -> p (a b)"), ps[:, 4:8, :].rearrange("p a b -> p (a b)"),
                                 ACT.Copy).then_inc(sem("h_rows"), 1)

        def router_dve(dve):
            dve.wait_ge(sem("bup_turned"), 1)
            nc.vector.tensor_copy(b_up, bank(0, 512))
            dve.wait_ge(sem("logits"), 1)
            nc.vector.tensor_tensor(L, bank(1, TT, NE), routb.unsqueeze(1).to_broadcast([P, TT, NE]), ALU.add)
            dve.drain()
            for t in range(TT):
                nc.vector.max(m8[:, t, :], L[:, t, :])
            dve.drain()
            fourth = m8[:, :, 3:4].to_broadcast([P, TT, NE])
            nc.vector.tensor_tensor(R[:, 0, :, :], L, m8[:, :, 0:1].to_broadcast([P, TT, NE]),
                                    ALU.subtract).then_inc(sem("shifted"), 1)
            nc.vector.tensor_tensor(R[:, 1, :, :], L, fourth, ALU.is_gt)
            nc.vector.tensor_tensor(R[:, 2, :, :], L, fourth, ALU.is_equal)
            nc.vector.memset(R[:, 4, :, :], 1.0)
            dve.drain()
            nc.vector.tensor_reduce(rs[:, :, 0:1], R[:, 1, :, :], AX, ALU.add)
            for t in range(TT):
                nc.vector.tensor_tensor_scan(R[:, 3, t, :], R[:, 4, t, :], R[:, 2, t, :], 0.0, ALU.mult, ALU.add)
            dve.drain()
            nc.vector.tensor_tensor(R[:, 3, :, :], R[:, 3, :, :], rs[:, :, 0:1].to_broadcast([P, TT, NE]), ALU.add)
            dve.drain()
            nc.vector.tensor_scalar(R[:, 3, :, :], R[:, 3, :, :], float(TOPK), None, ALU.is_le)
            dve.drain()
            nc.vector.tensor_tensor(R[:, 2, :, :], R[:, 2, :, :], R[:, 3, :, :], ALU.mult)
            dve.drain()
            nc.vector.tensor_tensor(R[:, 1, :, :], R[:, 1, :, :], R[:, 2, :, :], ALU.add).then_inc(
                sem("routed"), 1)
            dve.drain()
            dve.wait_ge(sem("logit_exps"), 1)
            nc.vector.tensor_tensor(gates, R[:, 0, :, :], R[:, 1, :, :], ALU.mult)
            dve.drain()
            nc.vector.tensor_reduce(rs[:, :, 1:2], gates, AX, ALU.add)
            dve.drain()
            nc.vector.reciprocal(rs[:, :, 2:3], rs[:, :, 1:2])
            dve.drain()
            nc.vector.tensor_tensor(gates, gates, rs[:, :, 2:3].to_broadcast([P, TT, NE]), ALU.mult).then_inc(
                sem("gates"), 1)
            dve.drain()
            dve.wait_ge(sem("ranks_mm"), 1)
            o = bank(3, TT + 1, NE)
            nc.vector.tensor_tensor(rank[:, :, 0:NE], o[:, 0:TT, :], R[:, 1, :, :], ALU.mult)
            nc.vector.tensor_reduce(rs[:, 0, 0:1], o[:, TT, :], AX, ALU.max)
            nc.vector.tensor_copy(gate[:, :, 0:NE], gates)
            nc.vector.tensor_copy(gate[:, :, NE:NE + 1], gates[:, :, 0:1])
            dve.drain()
            nc.vector.tensor_scalar(rank[:, :, 0:NE], rank[:, :, 0:NE], -1.0, None, ALU.add)
            for k in range(1, PASSES):
                nc.vector.tensor_scalar(rs[:, 0, k:k + 1], rs[:, 0, 0:1], float(k * CAP), None, ALU.is_gt)
            dve.drain()
            nc.vector.tensor_scalar(rank[:, :, NE:NE + 1], rank[:, :, 0:1], -float(CAP), None, ALU.add)
            nc.vector.tensor_reduce(rs[:, 1, 0:1], rs[:, 0, 1:PASSES], AX, ALU.add)
            dve.drain()
            nc.vector.tensor_scalar(rs[:, 1, 1:2], rs[:, 1, 0:1], 1.0, None, ALU.add)
            dve.drain()
            nc.vector.tensor_copy(itmp[:, P + 1:P + 2], rs[:, 1, 1:2]).then_inc(sem("passes"), 1)
            nc.vector.memset(scatT, 0.0)
            nc.vector.memset(y_sb, 0.0).then_inc(sem("y_copied"), 1)
            dve.wait_ge(sem("gates_turned"), 1)
            nc.vector.tensor_copy(gT[0:NE, :], bank(2, TOK)[0:NE, :]).then_inc(sem("gates_t"), 1)

        def passes_mm(out_, wh, wl, xh, xl, w_is_lhs, start, stop, skip):
            for n, (w_, x_) in enumerate(((wh, xh), (wh, xl), (wl, xh))):
                ins = nc.tensor.matmul(out_, w_ if w_is_lhs else x_, x_ if w_is_lhs else w_,
                                       start=start and n == 0, stop=stop and n == 2, skip_group_check=skip)
            return ins

        EXPERT_TILES = (("gate", 0), ("up", 0), ("gate", 1), ("up", 1), ("down", 0), ("down", 1),
                        ("gate", 2), ("up", 2), ("gate", 3), ("up", 3), ("down", 2), ("down", 3))
        PLACE = {x: n for n, x in enumerate(EXPERT_TILES)}
        CHUNK_BANK = (6, 7, 6, 7)
        xe = view(6144, 2, KT, CAP)
        sel = view(7552, TT, CAP)
        sel_g = view(7728, TT, CAP)
        scatT = view(7904, TOK)
        y_sb = view(8160, D)
        rank = view(9184, TT, NE + 1)
        gate = view(9250, TT, NE + 1)
        slot_no = iota_t[:, 0:CAP]
        XG = view(15104, 2, 2, CAP)
        XL = view(15104 + 4 * CAP, 2, 2, CAP)
        XF = ffn_buf[:, 0:4 * CAP].rearrange("p (a b c) -> p a b c", b=2, c=CAP)
        DH = [w_lower[:, 0:2048], w_lower[:, 2048:4096]]
        DL = [w_lower[:, 4096:6144], u_lower[:]]
        XH, XHL = (view(512 * k, 2, 2, CAP, of=hidden_parts) for k in range(2))
        XS = ffn_buf[:, 1024:1024 + 4 * CAP].rearrange("p (a b c) -> p a b c", b=2, c=CAP)

        def experts_pe(pe):
            def pick(n, half, b):
                for k in range(4):
                    for t in range(TT):
                        ins = nc.tensor.matmul(bank(b, 4, CAP)[:, k, :],
                                               xn[:, t, (4 * half + k) * P:(4 * half + k + 1) * P], sel[:, t, :],
                                               start=(t == 0), stop=(t == TT - 1))
                ins.then_inc(sem("picked"), 1)

            def hidden_products(T, rnd, c, n):
                for part in (0, 1):
                    tile = T + PLACE[(("gate", "up")[part], c)]
                    landed(pe, tile, rnd)
                    w = wcols(tile)
                    for j in range(2):
                        for k in range(KT):
                            ins = nc.tensor.matmul(bank(CHUNK_BANK[c], 4, CAP)[:, 2 * part + j, :],
                                                   w[:, k, j * P:(j + 1) * P], xe[:, n, k, :],
                                                   start=(k == 0), stop=(k == KT - 1))
                    ins.then_inc(w_used, 1)

            def down_products(T, rnd, c, m):
                tile = T + PLACE[("down", c)]
                landed(pe, tile, rnd)
                pe.wait_ge(sem("expert_hidden"), m * 4 + c + 1)
                pe.wait_ge(sem("down_parts"), m * 4 + c + 1)
                wh, wl = (w[c % 2].rearrange("p (j n) -> p j n", n=D) for w in (DH, DL))
                for j in range(2):
                    for h in range(2):
                        hs = slice(512 * h, 512 * h + 512)
                        ins = passes_mm(bank(4 + h, 512)[0:CAP, :], wh[:, j, hs], wl[:, j, hs],
                                        XH[:, c % 2, j, :], XHL[:, c % 2, j, :], False, c == 0 and j == 0,
                                        c == 3 and j == 1, False)
                ins.then_inc(w_used, 1)

            def put_back(stop):
                for t in range(TT):
                    for h in range(2):
                        nc.tensor.matmul(ps[:, 2 * t + h, :], scatT[0:CAP, t * P:(t + 1) * P],
                                         y_sb[0:CAP, 512 * h:512 * h + 512], start=False, stop=stop,
                                         skip_group_check=True)

            passes = passes_of(pe)
            pe.wait_ge(sem("h_rows"), 1)
            pe.wait_ge(sem("sel_ready"), 1)
            pick(0, 0, 6)
            pick(0, 1, 7)
            with pe.Fori(0, passes) as w:
                with pe.Fori(0, NE // 2) as i:
                    for n in range(2):
                        T, rnd, m = T_MOE + 12 * n, (w * NE + i * 2) * TILES12, w * NE + i * 2 + n
                        pe.wait_ge(sem("picked_read"), m * 2 + 2)
                        hidden_products(T, rnd, 0, n)
                        pe.wait_ge(sem("y_copied"), m + 1)
                        put_back(False)
                        hidden_products(T, rnd, 1, n)
                        down_products(T, rnd, 0, m)
                        pe.wait_ge(sem("sel_ready"), m + 2)
                        pick(1 - n, 0, 6)
                        down_products(T, rnd, 1, m)
                        pe.wait_ge(sem("sel_g_ready"), m + 1)
                        for t in range(TT):
                            ins = nc.tensor.transpose(bank(7, TOK)[0:CAP, t * P:(t + 1) * P], sel_g[:, t, :],
                                                      ident[:])
                        ins.then_inc(sem("sel_g_turned"), 1)
                        pe.wait_ge(sem("picked_read"), m * 2 + 3)
                        hidden_products(T, rnd, 2, n)
                        pe.wait_ge(sem("scat_ready"), m + 1)
                        hidden_products(T, rnd, 3, n)
                        down_products(T, rnd, 2, m)
                        pick(1 - n, 1, 6)
                        down_products(T, rnd, 3, m)
            pe.wait_ge(sem("y_copied"), passes * NE + 1)
            put_back(True)
            nc.tensor.matmul(bank(6, P)[:, 0:1], ident[:], zero, start=True, stop=True).then_inc(
                sem("moe_out"), 1)
            return (passes - 1) * NE * TILES12

        def experts_act(act):
            def copy_picked(half, n, count):
                act.wait_ge(sem("picked"), count)
                nc.scalar.activation(xe[:, n, 4 * half:4 * half + 4, :], bank(6, 4, CAP),
                                     ACT.Copy).then_inc(sem("picked_read"), 1)

            def sigmoid(c, m):
                act.wait_ge(sem("expert_gate"), m * 4 + c + 1)
                nc.scalar.activation(XS[:, c % 2, :, :], XG[:, c % 2, :, :], ACT.Sigmoid, scale=1.702).then_inc(
                    sem("expert_sigmoid"), 1)

            def upper(T, rnd, c):
                landed(act, T + PLACE[("down", c)], rnd)
                multiplied(act, T + PLACE[("down", (c + 2) % 4)] - (12 if c < 2 else 0), rnd)
                nc.scalar.activation(DH[c % 2], ring[:, (T + PLACE[("down", c)]) % SLOTS, :], ACT.Copy).then_inc(
                    sem("down_upper"), 1)

            passes = passes_of(act)
            for half in range(2):
                act.wait_ge(sem("picked"), half + 1)
                nc.scalar.activation(xe[:, 0, 4 * half:4 * half + 4, :], bank(6 + half, 4, CAP),
                                     ACT.Copy).then_inc(sem("picked_read"), 1)
            with act.Fori(0, passes) as w:
                with act.Fori(0, NE // 2) as i:
                    for n in range(2):
                        T, rnd, m = T_MOE + 12 * n, (w * NE + i * 2) * TILES12, w * NE + i * 2 + n
                        sigmoid(0, m)
                        upper(T, rnd, 0)
                        upper(T, rnd, 1)
                        sigmoid(1, m)
                        copy_picked(0, 1 - n, m * 2 + 3)
                        act.wait_ge(sem("sel_g_turned"), m + 1)
                        nc.scalar.activation(scatT[0:CAP, :], bank(7, TOK)[0:CAP, :], ACT.Copy).then_inc(
                            sem("scat_ready"), 1)
                        sigmoid(2, m)
                        upper(T, rnd, 2)
                        upper(T, rnd, 3)
                        sigmoid(3, m)
                        copy_picked(1, 1 - n, m * 2 + 4)
                        multiplied(act, T + PLACE[("down", 3)], rnd)
                        nc.scalar.activation(y_sb[0:CAP, :].rearrange("p (h n) -> p h n", n=512),
                                             ps[0:CAP, 4:6, :], ACT.Copy).then_inc(sem("y_copied"), 1)
            return (passes - 1) * NE * TILES12

        def experts_dve(dve):
            v = nc.vector

            def choose(col_, count_sem, out_, with_gate):
                for t in range(TT):
                    ins = v.tensor_scalar(out_[:, t, :], slot_no, rank[:, t, col_],
                                          gate[:, t, col_] if with_gate else None, ALU.is_equal,
                                          ALU.mult if with_gate else ALU.bypass)
                ins.then_inc(sem(count_sem), 1)

            passes = passes_of(dve)
            choose(bass.ds(0, 1), "sel_ready", sel, False)
            with dve.Fori(0, passes) as w:
                with dve.Fori(0, NE // 2) as i:
                    for n in range(2):
                        T, rnd, m = T_MOE + 12 * n, (w * NE + i * 2) * TILES12, w * NE + i * 2 + n
                        e = i * 2 + n
                        dve.wait_ge(sem("picked_read"), m * 2 + 2)
                        choose(bass.ds(e + 1, 1), "sel_ready", sel, False)
                        choose(bass.ds(e, 1), "sel_g_ready", sel_g, True)
                        for c in range(4):
                            par = c % 2
                            multiplied(dve, T + PLACE[("up", c)], rnd)
                            src = bank(CHUNK_BANK[c], 4, CAP)
                            g, l = XG[:, par, :, :], XL[:, par, :, :]
                            for j in range(2):
                                ins = v.tensor_scalar(g[:, j, :], src[:, j, :],
                                                      b_up[:, bass.ds(e * 16 + 2 * c + j, 1)], 7.0,
                                                      ALU.add, ALU.min)
                            ins.then_inc(sem("expert_gate"), 1)
                            for j in range(2):
                                v.tensor_scalar(l[:, j, :], src[:, 2 + j, :],
                                                b_up[:, bass.ds(e * 16 + 8 + 2 * c + j, 1)], 7.0,
                                                ALU.add, ALU.min)
                            dve.drain()
                            v.tensor_scalar(l, l, -7.0, 1.0, ALU.max, ALU.add)
                            dve.drain()
                            v.tensor_tensor(l, l, g, ALU.mult)
                            dve.drain()
                            dve.wait_ge(sem("expert_sigmoid"), m * 4 + c + 1)
                            v.tensor_tensor(XF[:, par, :, :], l, XS[:, par, :, :], ALU.mult)
                            dve.drain()
                            v.tensor_copy(XH[:, par, :, :], XF[:, par, :, :])
                            dve.drain()
                            v.tensor_tensor(XHL[:, par, :, :], XF[:, par, :, :], XH[:, par, :, :].bitcast(F32),
                                            ALU.subtract).then_inc(sem("expert_hidden"), 1)
                            if par == 0:
                                for k in (c, c + 1):
                                    dve.wait_ge(sem("down_upper"), m * 4 + k + 1)
                                    v.tensor_tensor(DL[k % 2], ring[:, (T + PLACE[("down", k)]) % SLOTS, :],
                                                    DH[k % 2].bitcast(F32), ALU.subtract).then_inc(
                                                        sem("down_parts"), 1)
                dve.drain()
                v.tensor_scalar(rank, rank, -float(CAP), None, ALU.add)
                dve.drain()
            return (passes - 1) * NE * TILES12

        u5 = view(2048, KT, TOK)
        Xtok = view(0, TT, 2 * D)
        z = view(4096, 16, TOK)
        xbc = view(8192, 24, TOK)
        ga = view(14336, KT, TOK)
        gb = view(16384, KT, TOK)
        y5 = view(18432, KT, TOK)
        stage_a = view(20480, P)
        stage_b = view(20608, P)
        stage_c = view(20736, 160)
        lay = view(20896, 96)
        w_dt = view(20992, KT, 32)
        dt_bias, a_neg = lay[:, 0:32], lay[:, 32:64]
        skip_d = small[:, 128:144]
        step = small[:, 144:176]
        dts = view(21248, 5, TT, 32)
        C_nat = [view(8192, 8, 2, 64), view(9216, 8, 2, 64)]
        B_nat = [view(10240, 32, 32), view(11264, 32, 32)]
        C_T = [view(12288, 8, P), view(13312, 8, P)]
        work = [view(21568 + 1024 * k, 4, 2, TC) for k in range(8)]
        phase = view(29760, 4, 2, TC)
        B_T = [view(30784, 8, P), view(31808, 8, P)]
        cols = view(32832, 16, 32)
        cos_t, sin_t = view(8192, 4, 2, TC), view(9216, 4, 2, TC)

        def layer_loads(pool, li):
            dma = pool.dma_start
            s = sem("stage_in")
            pool.wait_ge(sem("stage_used"), li + 1)
            pool.sem_inc(sem("loads_allowed"), 1)
            for name, src, n in (("ffn1_pre_g", "ffn1_pre_g_2", 8), ("mix_pre_g", "mix_pre_g_2", 8),
                                 ("ffn2_pre_g", "ffn2_pre_g_2", 8), ("conv_b", "ssd_conv_b_2", 24),
                                 ("norm_g", "ssd_norm_g_2", 16), ("s5_d", "s5_d_2", 8)):
                dma(stage_a[V2[name]:V2[name] + n, :],
                    a[src][li, :].rearrange("(r p) -> r p", p=P)).then_inc(s, 16)
            dma(stage_a[V2["lam_re"]:V2["lam_re"] + 32, :],
                a["s5_lambda_re_2"][li].rearrange("(j g) n -> j (g n)", g=2)).then_inc(s, 16)
            dma(stage_b[0:96, :], a["ssd_conv_w_2"][li].rearrange("k (r p) -> (k r) p", p=P)).then_inc(s, 16)
            dma(stage_b[96:128, :], a["s5_lambda_im_2"][li].rearrange("(j g) n -> j (g n)", g=2)).then_inc(s, 16)
            at = 0
            for name in ("ssd_dt_bias_2", "ssd_a_log_2", "ssd_d_2", "s5_log_step_2"):
                n = a[name].shape[1]
                dma(stage_c[:, at:at + n], bcast(a[name][bass.ds(li, 1), :])).then_inc(s, 16)
                at += n
            post_gain_load(pool, li * 3, a["ffn1_post_g_2"][bass.ds(li, 1), :])
            pool.wait_ge(sem("b_zeroed"), li + 1)
            pool.sem_inc(sem("loads_allowed"), 1)
            s = sem("s5_in")
            dma(w_dt, a["w_in_2"][li, :, DT2:DT2 + 32].rearrange("(k p) n -> p k n", p=P)).then_inc(s, 16)
            for v, name in enumerate(("s5_c_re_2", "s5_c_im_2")):
                src = a[name][li].rearrange("(T q) c n -> (q c) T n", q=8)
                for half in range(2):
                    dma(C_nat[v][:, :, half, :], src).then_inc(s, 16)
            for v, name in enumerate(("s5_b_re_2", "s5_b_im_2")):
                src = a[name][li].rearrange("(j g) n c -> g n j c", g=2)
                for g in range(2):
                    dma(B_nat[v][64 * g:64 * g + 64, :, 16 * g:16 * g + 16], src[g]).then_inc(s, 16)
            post_gain_load(pool, li * 3 + 1, a["mix_post_g_2"][bass.ds(li, 1), :])
            post_gain_load(pool, li * 3 + 2, a["ffn2_post_g_2"][bass.ds(li, 1), :])

        STAGE_IN = 16 * 13
        S5_IN = 16 * 9

        def post_gain_load(pool, p, src):
            if not isinstance(p, int):
                pool.wait_ge(sem("x_new"), p + 3)
                pool.sem_inc(sem("loads_allowed"), 1)
            pool.dma_start(post_gain[:], bcast(src)).then_inc(sem("post_gain_in"), 16)

        def layer_start_pe(pe, li):
            pe.wait_ge(sem("stage_in"), (li + 1) * STAGE_IN)
            pe.wait_ge(sem("x_new"), li * 3 + 3)
            nc.tensor.transpose(bank(6, P)[:, 0:NV2A], stage_a[0:NV2A, :], ident[0:NV2A, 0:NV2A])
            nc.tensor.transpose(bank(7, P), stage_b, ident[:]).then_inc(sem("vec2_turned"), 1)

        def layer_start_dve(dve, li):
            dve.wait_ge(sem("vec2_turned"), li + 1)
            nc.vector.tensor_copy(vec2[:, 0:NV2A], bank(6, P)[:, 0:NV2A])
            nc.vector.tensor_copy(vec2[:, NV2A:NV2], bank(7, P))
            dve.wait_ge(sem("stage_in"), (li + 1) * STAGE_IN)
            nc.vector.tensor_copy(dt_bias, stage_c[:, 0:32])
            for g in range(2):
                r = slice(64 * g, 64 * g + 64)
                nc.vector.tensor_copy(skip_d[r, :], stage_c[r, 64 + g:96:2])
                nc.vector.tensor_copy(step[r, :], stage_c[r, 96 + g:160:2])
            dve.wait_ge(sem("a_exp"), li + 1)
            nc.vector.tensor_scalar(a_neg, a_neg, -1.0, None, ALU.mult)
            nc.vector.memset(B_nat[1], 0.0)
            nc.vector.memset(B_nat[0], 0.0).then_inc(sem("b_zeroed"), 1)
            nc.vector.memset(small[:, 254:255], 0.0).then_inc(sem("stage_used"), 1)

        def layer_start_act(act, li):
            act.wait_ge(sem("vec2_turned"), li + 1)
            nc.scalar.activation(a_neg, stage_c[:, 32:64], ACT.Exp).then_inc(sem("a_exp"), 1)

        FFN_LOOPS = (NCH - 1) // 4
        NT = 3 * NCH
        WH = [w_upper[:, 2048 * k:2048 * k + 2048] for k in range(3)]
        WL = [w_lower[:, 2048 * k:2048 * k + 2048] for k in range(3)]
        UH, UL = view(0, KT, TOK, of=u_upper), view(0, KT, TOK, of=u_lower)
        HH, HL = (view(1024 * k, 2, 2, W, of=hidden_parts) for k in range(2))

        def ffn_up_pe(pe, T, T0, rnd, b):
            multiplied(pe, T, rnd)
            k3 = (T - T0) % 3
            wh, wl = (w[k3].rearrange("p (k n) -> p k n", n=W) for w in (WH, WL))
            for m in range(2):
                c = slice(m * P, m * P + P)
                for k in range(KT):
                    ins = passes_mm(bank(b, 2, TOK)[:, m, :], wh[:, k, c], wl[:, k, c], UH[:, k, :], UL[:, k, :],
                                    True, k == 0, k == KT - 1, False)
            ins.then_inc(sem("tile_mm"), 1)

        def ffn_down_pe(pe, T, T0, rnd, count, par, last):
            multiplied(pe, T, rnd)
            pe.wait_ge(sem("hidden_parts"), count)
            k3 = (T - T0) % 3
            wh, wl = (w[k3].rearrange("p (j n) -> p j n", n=D) for w in (WH, WL))
            for j in range(2):
                for t in range(TT):
                    ts = slice(t * P, t * P + P)
                    for h in range(2):
                        hs = slice(512 * h, 512 * h + 512)
                        ins = passes_mm(ps[:, 2 * t + h, :], wh[:, j, hs], wl[:, j, hs], HH[:, par, j, ts],
                                        HL[:, par, j, ts], False, False, last and j == 1, True)
            ins.then_inc(sem("tile_mm"), 1)

        def ffn_chunks(eng, T0, r, body):
            with eng.Fori(0, FFN_LOOPS) as i:
                for c in range(4):
                    body(i * 4 + c, c, r + i * TILES12, False)
            for c in range(4 * FFN_LOOPS, NCH):
                body(c, c, r, c + 1 == NCH)

        def ffn_pe(pe, T0, r, nf):
            pe.wait_ge(sem("u_parts"), nf + 1)
            ffn_up_pe(pe, T0, T0, r, 4)
            ffn_up_pe(pe, T0 + 1, T0, r, 5)
            for b in range(4):
                nc.tensor.matmul(ps[:, b, 0:1], ident[:], zero, start=True, stop=False, skip_group_check=True)

            def chunk(c, c4, rnd, last):
                b = 4 + 2 * ((c4 + 1) % 2)
                if not last:
                    ffn_up_pe(pe, T0 + 2 + 3 * c4, T0, rnd, b)
                    ffn_up_pe(pe, T0 + 3 + 3 * c4, T0, rnd, b + 1)
                ffn_down_pe(pe, T0 + 3 * c4 + (2 if last else 4), T0, rnd, nf * NCH + c + 1, c4 % 2, last)
            ffn_chunks(pe, T0, r, chunk)

        def ffn_act(act, T0, r, nf):
            def upper(idx, c_idx, T, rnd):
                landed(act, T, rnd)
                if c_idx is not None:
                    act.wait_ge(sem("tile_mm"), nf * NT + c_idx - 1)
                nc.scalar.activation(WH[idx % 3], ring[:, T % SLOTS, :], ACT.Copy).then_inc(sem("tile_upper"), 1)

            act.wait_ge(sem("ffn_u"), nf + 1)
            nc.scalar.activation(UH, uT, ACT.Copy).then_inc(sem("u_upper"), 1)
            upper(0, None, T0, r)
            upper(1, None, T0 + 1, r)

            def chunk(c, c4, rnd, last):
                first = 3 * c + 2
                if not last:
                    upper(2, first, T0 + 2 + 3 * c4, rnd)
                act.wait_ge(sem("tile_mm"), nf * NT + 3 * c + (2 if c4 else 3))
                b = 4 + 2 * (c4 % 2)
                nc.scalar.activation(gated[:, c4 % 2, :, :], bank(b, 2, W), ACT.Silu).then_inc(sem("ffn_silu"), 1)
                if not last:
                    upper(3, first + 1, T0 + 3 + 3 * c4, rnd)
                act.wait_ge(sem("ffn_hidden"), nf * NCH + c + 1)
                nc.scalar.activation(HH[:, c4 % 2, :, :], hidden[:, c4 % 2, :, :], ACT.Copy).then_inc(
                    sem("hidden_upper"), 1)
                if last:
                    upper(2, first, T0 + 2 + 3 * c4, rnd)
                else:
                    upper(4, first + 2, T0 + 4 + 3 * c4, rnd)
            ffn_chunks(act, T0, r, chunk)

        def ffn_dve(dve, T0, r, nf):
            v = nc.vector

            def lower(idx, count, T):
                dve.wait_ge(sem("tile_upper"), nf * NT + count + 1)
                v.tensor_tensor(WL[idx % 3], ring[:, T % SLOTS, :], WH[idx % 3].bitcast(F32), ALU.subtract
                                ).then_inc(w_used, 1)

            dve.wait_ge(sem("u_upper"), nf + 1)
            v.tensor_tensor(UL, uT, UH.bitcast(F32), ALU.subtract).then_inc(sem("u_parts"), 1)
            lower(0, 0, T0)
            lower(1, 1, T0 + 1)

            def chunk(c, c4, rnd, last):
                first, par = 3 * c + 2, c4 % 2
                if not last:
                    lower(2, first, T0 + 2 + 3 * c4)
                dve.wait_ge(sem("ffn_silu"), nf * NCH + c + 1)
                v.tensor_tensor(hidden[:, par, :, :], gated[:, par, :, :], bank(5 + 2 * par, 2, W),
                                ALU.mult).then_inc(sem("ffn_hidden"), 1)
                if not last:
                    lower(3, first + 1, T0 + 3 + 3 * c4)
                dve.drain()
                dve.wait_ge(sem("hidden_upper"), nf * NCH + c + 1)
                v.tensor_tensor(HL[:, par, :, :], hidden[:, par, :, :], HH[:, par, :, :].bitcast(F32),
                                ALU.subtract).then_inc(sem("hidden_parts"), 1)
                if last:
                    lower(2, first, T0 + 2 + 3 * c4)
                else:
                    lower(4, first + 2, T0 + 4 + 3 * c4)
            ffn_chunks(dve, T0, r, chunk)

        TURN = 6.283185

        def u5_pe(pe, r):
            for n in range(4):
                feature_tile(pe, L_U5 + n, r, n, uT)

        def u5_dve(dve, r):
            for n in range(4):
                multiplied(dve, L_U5 + n, r)
                nc.vector.tensor_copy(u5[:, 2 * n:2 * n + 2, :], bank(n, 2, TOK))
            dve.drain()

        (c_re, c_mag, c_th, c_half, c_sin, c_tanh, c_fr, c_fi, c_t1, c_t2, c_kr, c_ki, c_a, c_cos, c_t3,
         c_t4) = [cols[:, k, :] for k in range(16)]
        lam_im = vec2[:, V2["lam_im"]:V2["lam_im"] + 32]
        lam_re = vec2[:, V2["lam_re"]:V2["lam_re"] + 32]
        MAGIC = 12582912.0

        def turns(dve, out_, in_):
            nc.vector.tensor_scalar(out_, in_, MAGIC, MAGIC, ALU.add, ALU.subtract)
            dve.drain()
            nc.vector.tensor_tensor(out_, in_, out_, ALU.subtract)
            dve.drain()

        def s5_params_dve(dve, li):
            v = nc.vector
            v.tensor_scalar(c_re, lam_re, -1e-4, None, ALU.min).then_inc(sem("s5_re"), 1)
            dve.drain()
            dve.wait_ge(sem("s5_step"), li + 1)
            v.tensor_tensor(c_a, c_re, step, ALU.mult)
            v.tensor_tensor(c_th, lam_im, step, ALU.mult)
            dve.drain()
            v.tensor_scalar(c_t1, c_th, 1.0 / (2.0 * 3.141592653589793), None, ALU.mult)
            dve.drain()
            turns(dve, c_th, c_t1)
            v.tensor_scalar(c_t2, c_th, float(TC), None, ALU.mult)
            dve.drain()
            turns(dve, c_t3, c_t2)
            v.tensor_scalar(c_t1, c_t3, 0.25, None, ALU.add)
            dve.drain()
            turns(dve, c_t4, c_t1)
            v.memset(small[:, 248:249], 0.0).then_inc(sem("s5_angles"), 1)
            dve.wait_ge(sem("s5_trig"), li + 1)
            v.tensor_tensor(c_half, c_half, c_half, ALU.mult)
            v.scalar_tensor_tensor(out=c_tanh, in0=c_mag, scalar=1.0, in1=c_tanh, op0=ALU.add, op1=ALU.mult)
            dve.drain()
            v.tensor_scalar(c_cos, c_half, -2.0, 1.0, ALU.mult, ALU.add)
            dve.drain()
            v.tensor_tensor(c_fr, c_tanh, c_cos, ALU.mult)
            v.tensor_tensor(c_fi, c_mag, c_sin, ALU.mult)
            dve.drain()
            v.scalar_tensor_tensor(out=c_fr, in0=c_half, scalar=-2.0, in1=c_fr, op0=ALU.mult, op1=ALU.add)
            v.tensor_tensor(c_t1, c_re, c_re, ALU.mult)
            v.tensor_tensor(c_t2, lam_im, lam_im, ALU.mult)
            dve.drain()
            v.tensor_tensor(c_t1, c_t1, c_t2, ALU.add)
            dve.drain()
            v.reciprocal(c_t1, c_t1)
            dve.drain()
            v.tensor_tensor(c_fr, c_fr, c_t1, ALU.mult)
            v.tensor_tensor(c_fi, c_fi, c_t1, ALU.mult)
            dve.drain()
            v.tensor_tensor(c_t1, c_fr, c_re, ALU.mult)
            v.tensor_tensor(c_t2, c_fi, lam_im, ALU.mult)
            v.tensor_tensor(c_half, c_fi, c_re, ALU.mult)
            v.tensor_tensor(c_sin, c_fr, lam_im, ALU.mult)
            v.tensor_tensor(c_kr, c_mag, c_t4, ALU.mult)
            v.tensor_tensor(c_ki, c_mag, c_t3, ALU.mult)
            dve.drain()
            v.tensor_tensor(c_fr, c_t1, c_t2, ALU.add)
            v.tensor_tensor(c_fi, c_half, c_sin, ALU.subtract)
            dve.drain()
            dve.wait_ge(sem("s5_in"), (li + 1) * S5_IN)
            fr = c_fr.unsqueeze(2).to_broadcast([P, 32, 32])
            fi = c_fi.unsqueeze(2).to_broadcast([P, 32, 32])
            t = [arena[:, 14336 + 1024 * k:15360 + 1024 * k].rearrange("p (a b) -> p a b", b=32) for k in range(4)]
            v.tensor_tensor(t[0], B_nat[0], fr, ALU.mult)
            v.tensor_tensor(t[1], B_nat[1], fi, ALU.mult)
            v.tensor_tensor(t[2], B_nat[0], fi, ALU.mult)
            v.tensor_tensor(t[3], B_nat[1], fr, ALU.mult)
            for k in range(2):
                v.tensor_tensor(C_nat[k], C_nat[k], glmask[:].unsqueeze(1).unsqueeze(3).to_broadcast([P, 8, 2, 64]),
                                ALU.mult)
            dve.drain()
            v.tensor_tensor(B_nat[0], t[0], t[1], ALU.subtract)
            v.tensor_tensor(B_nat[1], t[2], t[3], ALU.add).then_inc(sem("s5_mats"), 1)
            for k in range(8):
                dve.wait_ge(sem("s5_turned"), li * 8 + k + 1)
                dst = (B_T[0], B_T[1], C_T[0], C_T[1])[k // 2][:, 4 * (k % 2):4 * (k % 2) + 4, :]
                if k < 6:
                    ins = v.tensor_copy(dst, bank(k, 4, P))
                else:
                    ins = v.tensor_scalar(dst, bank(k, 4, P), -1.0, None, ALU.mult)
            ins.then_inc(sem("s5_mats_ready"), 1)

        def s5_params_act(act, li):
            act.wait_ge(sem("s5_re"), li + 1)
            nc.scalar.activation(step, step, ACT.Exp).then_inc(sem("s5_step"), 1)
            act.wait_ge(sem("s5_angles"), li + 1)
            nc.scalar.activation(c_mag, c_a, ACT.Exp)
            nc.scalar.activation(c_tanh, c_a, ACT.Tanh, scale=0.5)
            nc.scalar.activation(c_half, c_th, ACT.Sin, scale=TURN / 2)
            nc.scalar.activation(c_sin, c_th, ACT.Sin, scale=TURN)
            nc.scalar.activation(c_t3, c_t3, ACT.Sin, scale=TURN)
            nc.scalar.activation(c_t4, c_t4, ACT.Sin, scale=TURN).then_inc(sem("s5_trig"), 1)

        def s5_turn_pe(pe, li):
            pe.wait_ge(sem("s5_mats"), li + 1)
            for k in range(8):
                for q in range(4):
                    T = 4 * (k % 2) + q
                    if k < 4:
                        src = B_nat[k // 2][:, 4 * T:4 * T + 4, :].rearrange("p a b -> p (a b)")
                    else:
                        src = C_nat[k // 2 - 2][:, T, :, :].rearrange("p a b -> p (a b)")
                    ins = nc.tensor.transpose(bank(k, 4, P)[:, q, :], src, ident[:])
                ins.then_inc(sem("s5_turned"), 1)

        NTC = TOK // TC
        UNITS = 4 * NTC
        def s5_in_mm(pe, li, n):
            g, c = n // NTC, n % NTC
            for o in range(4):
                r = slice(32 * o, 32 * o + 32)
                for v in range(2):
                    for q in range(2):
                        ins = nc.tensor.matmul(bank(o, 2, 2, TC)[:, v, q, :], B_T[v][r, 2 * g + q, :],
                                               u5[r, 2 * g + q, TC * c:TC * c + TC], start=True, stop=True)
            ins.then_inc(sem("s5_bu"), 1)

        def side_tile(pe, li, r, n):
            if 2 <= n < 10:
                pe.wait_ge(sem("z_read"), li * 8 + n - 1)
            elif n >= 10:
                pe.wait_ge(sem("g_read"), li * 8 + n - 9)
            feature_tile(pe, L_Z + n, r, 6 + n % 2, uT)

        def s5_pe(pe, li, r):
            pe.wait_ge(sem("s5_mats_ready"), li + 1)
            s5_in_mm(pe, li, 0)
            for n in range(UNITS):
                g, c = n // NTC, n % NTC
                side_tile(pe, li, r, 2 * n)
                if n + 1 < UNITS:
                    pe.wait_ge(sem("s5_bu_read"), li * UNITS + n + 1)
                    s5_in_mm(pe, li, n + 1)
                side_tile(pe, li, r, 2 * n + 1)
                pe.wait_ge(sem("s5_states"), li * UNITS + n + 1)
                for q in range(2):
                    for o in range(4):
                        out_ = bank(4 + n % 2, 2, TC)[32 * o:32 * o + 32, q, :]
                        j = slice(32 * o, 32 * o + 32)
                        nc.tensor.matmul(out_, C_T[0][:, 2 * g + q, j], work[6][:, o, q, :], start=True,
                                         stop=False)
                        ins = nc.tensor.matmul(out_, C_T[1][:, 2 * g + q, j], work[7][:, o, q, :], start=False,
                                               stop=True)
                ins.then_inc(sem("s5_y"), 1)

        def tile_cols(t, g):
            return t[:, 8 * g:8 * g + 8].rearrange("p (q o) -> p o q", q=2)

        def s5_dve(dve, li):
            v = nc.vector
            atab, t0, t1, t2, br, bi, sr, si = work

            def flat(w):
                return w.rearrange("p a b c -> p (a b c)")

            def read_y(n):
                g, c = n // NTC, n % NTC
                dve.wait_ge(sem("s5_y"), li * UNITS + n + 1)
                for q in range(2):
                    cs = slice(TC * c, TC * c + TC)
                    v.scalar_tensor_tensor(out=y5[:, 2 * g + q, cs], in0=u5[:, 2 * g + q, cs],
                                           scalar=col(vec2, V2["s5_d"] + 2 * g + q),
                                           in1=bank(4 + n % 2, 2, TC)[:, q, :], op0=ALU.mult, op1=ALU.add)

            for g in range(4):
                th = tile_cols(c_th, g)
                for o in range(4):
                    v.tensor_tensor(t0[:, o, :, :], th[:, o, :].unsqueeze(2).to_broadcast([P, 2, TC]),
                                    iota_t[:, 0:TC].unsqueeze(1).to_broadcast([P, 2, TC]), ALU.mult)
                    v.tensor_copy(atab[:, o, :, :],
                                  tile_cols(c_mag, g)[:, o, :].unsqueeze(2).to_broadcast([P, 2, TC]))
                dve.drain()
                v.memset(atab[:, :, :, 0:1], 0.0)
                turns(dve, phase, t0)
                v.tensor_scalar(t0, phase, 0.25, None, ALU.add)
                dve.drain()
                turns(dve, t1, t0)
                v.memset(small[:, 248:249], 0.0).then_inc(sem("s5_phase"), 1)
                dve.wait_ge(sem("s5_tables"), li * 4 + g + 1)
                for c in range(NTC):
                    n = NTC * g + c
                    dve.wait_ge(sem("s5_bu"), li * UNITS + n + 1)
                    bu_r = ps[:, 0:4, 0:2 * TC].rearrange("p o (q t) -> p o q t", q=2)
                    bu_i = ps[:, 0:4, 2 * TC:4 * TC].rearrange("p o (q t) -> p o q t", q=2)
                    v.tensor_tensor(br, bu_r, cos_t, ALU.mult)
                    v.tensor_tensor(t0, bu_i, sin_t, ALU.mult)
                    v.tensor_tensor(bi, bu_i, cos_t, ALU.mult)
                    v.tensor_tensor(t1, bu_r, sin_t, ALU.mult).then_inc(sem("s5_bu_read"), 1)
                    if c:
                        er, ei = t2[:, 0, :, 0:4], t2[:, 1, :, 0:4]
                        kr = tile_cols(c_kr, g).rearrange("p o q -> p q o")
                        ki = tile_cols(c_ki, g).rearrange("p o q -> p q o")
                        v.tensor_tensor(t2[:, 2, :, 0:4], kr, er, ALU.mult)
                        v.tensor_tensor(t2[:, 2, :, 4:8], ki, ei, ALU.mult)
                        v.tensor_tensor(t2[:, 3, :, 0:4], kr, ei, ALU.mult)
                        v.tensor_tensor(t2[:, 3, :, 4:8], ki, er, ALU.mult)
                    dve.drain()
                    v.tensor_tensor(br, br, t0, ALU.add)
                    v.tensor_tensor(bi, bi, t1, ALU.subtract)
                    if c:
                        v.tensor_tensor(t2[:, 2, :, 0:4], t2[:, 2, :, 0:4], t2[:, 2, :, 4:8], ALU.subtract)
                        v.tensor_tensor(t2[:, 3, :, 0:4], t2[:, 3, :, 0:4], t2[:, 3, :, 4:8], ALU.add)
                        dve.drain()
                        for w, k in ((br, 2), (bi, 3)):
                            first = w[:, :, :, 0:1].rearrange("p o q t -> p q (o t)")
                            v.tensor_tensor(first, first, t2[:, k, :, 0:4], ALU.add)
                    dve.drain()
                    v.tensor_tensor_scan(flat(t0), flat(atab), flat(br), 0.0, ALU.mult, ALU.add)
                    v.tensor_tensor_scan(flat(t1), flat(atab), flat(bi), 0.0, ALU.mult, ALU.add)
                    dve.drain()
                    if n:
                        read_y(n - 1)
                    v.tensor_tensor(sr, t0, cos_t, ALU.mult)
                    v.tensor_tensor(br, t1, sin_t, ALU.mult)
                    v.tensor_tensor(si, t0, sin_t, ALU.mult)
                    v.tensor_tensor(bi, t1, cos_t, ALU.mult)
                    if c + 1 < NTC:
                        v.tensor_copy(t2[:, 0, :, 0:4], t0[:, :, :, TC - 1:TC].rearrange("p o q t -> p q (o t)"))
                        v.tensor_copy(t2[:, 1, :, 0:4], t1[:, :, :, TC - 1:TC].rearrange("p o q t -> p q (o t)"))
                    dve.drain()
                    v.tensor_tensor(sr, sr, br, ALU.subtract)
                    v.tensor_tensor(si, si, bi, ALU.add).then_inc(sem("s5_states"), 1)
                    dve.drain()
            read_y(UNITS - 1)
            dve.drain()
            nc.vector.memset(small[:, 248:249], 0.0).then_inc(sem("y5_raw"), 1)

        def s5_act(act, li, r):
            for g in range(4):
                act.wait_ge(sem("s5_phase"), li * 4 + g + 1)
                nc.scalar.activation(sin_t, phase, ACT.Sin, scale=TURN)
                nc.scalar.activation(cos_t, work[2], ACT.Sin, scale=TURN).then_inc(sem("s5_tables"), 1)
                for n in range(4 * g, 4 * g + 4):
                    multiplied(act, L_Z + n, r)
                    if n < 8:
                        nc.scalar.activation(z[:, 2 * n:2 * n + 2, :], bank(6 + n % 2, 2, TOK), ACT.Silu).then_inc(
                            sem("z_read"), 1)
                    else:
                        t = (ga, gb)[n // 4 - 2][:, 2 * (n % 4):2 * (n % 4) + 2, :]
                        nc.scalar.activation(t, bank(6 + n % 2, 2, TOK), ACT.Sigmoid).then_inc(
                            sem("g_read"), 1)
            act.wait_ge(sem("y5_raw"), li + 1)
            nc.scalar.activation(y5, y5, ACT.Gelu_apprx_tanh).then_inc(sem("y5_ready"), 1)

        def xbc_bank(n):
            return (n + 6) % 8

        def proj_pe(pe, li, r):
            for n in range(12):
                if n < 2:
                    pe.wait_ge(sem("g_read"), li * 8 + 7 + n)
                elif n == 2:
                    pe.wait_ge(sem("y5_raw"), li + 1)
                elif n >= 8:
                    pe.wait_ge(sem("xbc_read"), li * 12 + n - 7)
                feature_tile(pe, L_XBC + n, r, xbc_bank(n), uT)
            pe.wait_ge(sem("xbc_read"), li * 12 + 7)
            for t in range(TT):
                for k in range(KT):
                    ins = nc.tensor.matmul(bank(4, TT, 32)[:, t, :], uT[:, k, t * P:(t + 1) * P], w_dt[:, k, :],
                                           start=(k == 0), stop=(k == KT - 1))
            ins.then_inc(sem("dt_mm"), 1)
            pe.wait_ge(sem("y5_ready"), li + 1)
            pe.wait_ge(sem("dt_raw"), li + 1)
            pe.wait_ge(sem("xbc_read"), li * 12 + 12)
            for n in range(4):
                for half in range(2):
                    feature_tile(pe, L_GLU + 2 * n + half, r, (4 + 2 * n + half) % 8, y5)
            pe.wait_ge(sem("glu_ready"), li * 4 + 4)
            for n in range(4):
                feature_tile(pe, L_BB + n, r, n, uT)

        def proj_act(act, li, r):
            for n in range(12):
                act.wait_ge(sem("xbc_read"), li * 12 + n + 1)
                ins = nc.scalar.activation(xbc[:, 2 * n:2 * n + 2, :], xbc[:, 2 * n:2 * n + 2, :], ACT.Silu)
            ins.then_inc(sem("xbc_ready"), 1)
            for n in range(4):
                multiplied(act, L_GLU + 2 * n + 1, r)
                if n >= 2:
                    act.wait_ge(sem("glu_ready"), li * 4 + n - 1)
                nc.scalar.activation(gated[:, n % 2, :, :], bank((5 + 2 * n) % 8, 2, TOK), ACT.Sigmoid).then_inc(
                    sem("glu_gate"), 1)
            dt, ab = dts[:, 0], dts[:, 1]
            act.wait_ge(sem("dt_raw"), li + 1)
            nc.scalar.activation(ab, dt, ACT.Abs)
            act.drain()
            nc.scalar.activation(ab, ab, ACT.Exp, scale=-1.0)
            act.drain()
            nc.scalar.activation(ab, ab, ACT.Ln, bias=one).then_inc(sem("dt_log"), 1)

        def proj_dve(dve, li, r):
            cw, cb_ = V2["conv_w"], V2["conv_b"]
            for n in range(12):
                multiplied(dve, L_XBC + n, r)
                src = bank(xbc_bank(n), 2, TOK)
                for t in range(2):
                    f = 2 * n + t
                    nc.vector.tensor_scalar(xbc[:, f, :], src[:, t, :], col(vec2, cw + 72 + f),
                                            col(vec2, cb_ + f), ALU.mult, ALU.add)
                for lag in (1, 2, 3):
                    dve.drain()
                    for t in range(2):
                        f = 2 * n + t
                        ins = nc.vector.scalar_tensor_tensor(
                            out=xbc[:, f, lag:], in0=src[:, t, 0:TOK - lag], scalar=col(vec2, cw + 24 * (3 - lag) + f),
                            in1=xbc[:, f, lag:], op0=ALU.mult, op1=ALU.add)
                ins.then_inc(sem("xbc_read"), 1)
            dt, ab, adt = dts[:, 0], dts[:, 1], dts[:, 2]
            dve.wait_ge(sem("dt_mm"), li + 1)
            nc.vector.tensor_tensor(dt, bank(4, TT, 32), dt_bias.unsqueeze(1).to_broadcast([P, TT, 32]),
                                    ALU.add).then_inc(sem("dt_raw"), 1)
            for n in range(4):
                dve.wait_ge(sem("glu_gate"), li * 4 + n + 1)
                nc.vector.tensor_tensor(uT[:, 2 * n:2 * n + 2, :], bank((4 + 2 * n) % 8, 2, TOK),
                                        gated[:, n % 2, :, :], ALU.mult).then_inc(sem("glu_ready"), 1)
            for n in range(4):
                multiplied(dve, L_BB + n, r)
                t = gb[:, 2 * n:2 * n + 2, :]
                nc.vector.tensor_tensor(t, t, bank(n, 2, TOK), ALU.mult)
            dve.wait_ge(sem("dt_log"), li + 1)
            nc.vector.scalar_tensor_tensor(out=dt, in0=dt, scalar=0.0, in1=ab, op0=ALU.max, op1=ALU.add)
            dve.drain()
            nc.vector.tensor_tensor(adt, dt, a_neg.unsqueeze(1).to_broadcast([P, TT, 32]), ALU.mult).then_inc(
                sem("dt_ready"), 1)

        Ms = [arena[:, 18432:18432 + 1536].rearrange("p (h n) -> p h n", n=384),
              ffn_buf[:, 0:1536].rearrange("p (h n) -> p h n", n=384)]
        CBs = [arena[:, 19968:19968 + 384], ffn_buf[:, 1536:1920]]
        nacum = dts[:, 3]

        def ssd_pe(pe, li, r):
            adt = dts[:, 2]
            pe.wait_ge(sem("dt_ready"), li + 1)
            o = bank(5, TT, 32)
            nc.tensor.matmul(o[:, 0, :], tri[:, 0:P], adt[:, 0, :], start=True, stop=True)
            nc.tensor.matmul(o[:, 1, :], tri[:, P:2 * P], adt[:, 0, :], start=True, stop=False)
            nc.tensor.matmul(o[:, 1, :], tri[:, 0:P], adt[:, 1, :], start=False, stop=True).then_inc(
                sem("acum_mm"), 1)
            pe.wait_ge(sem("xbc_ready"), li + 1)
            for n in range(8):
                g, t = n // 2, n % 2
                if n >= 2:
                    pe.wait_ge(sem("x_turned_read"), li * 8 + n - 1)
                for q in range(4):
                    ins = nc.tensor.transpose(bank(6 + n % 2, 4, P)[:, q, :], xbc[:, 4 * g + q, t * P:(t + 1) * P],
                                              ident[:])
                ins.then_inc(sem("heads_turned"), 1)
            pe.wait_ge(sem("x_turned_read"), li * 8 + 8)
            for u in range(9):
                if u < 8:
                    g = u // 2
                    if u % 2 == 0:
                        b = 6 + g % 2
                        Bm, Cm = xbc[:, 16 + g, :], xbc[:, 20 + g, :]
                        nc.tensor.matmul(bank(b, 384)[:, 0:TOK], Bm[:, 0:P], Cm, start=True, stop=True)
                        nc.tensor.matmul(bank(b, 384)[:, TOK:384], Bm[:, P:TOK], Cm[:, P:TOK], start=True,
                                         stop=True).then_inc(sem("cb_mm"), 1)
                    for i in range(4):
                        h = 4 * u + i
                        o = bank(2 * (u % 2) + i // 2, 2, TOK)[:, i % 2, :]
                        nc.tensor.matmul(o, adt[:, 0, h:h + 1].to_broadcast([P, P]), tri[:], start=True,
                                         stop=False, skip_group_check=True)
                        ins = nc.tensor.matmul(o[:, P:TOK], adt[:, 1, h:h + 1].to_broadcast([P, P]), tri[:, 0:P],
                                               start=False, stop=True, skip_group_check=True)
                    ins.then_inc(sem("sums_mm"), 1)
                if u:
                    v = u - 1
                    pe.wait_ge(sem("m_ready"), li * 8 + v + 1)
                    for i in range(4):
                        h = 4 * v + i
                        o = bank(4 + v % 2, 2, TOK)[64 * (i % 2):64 * (i % 2) + 64, i // 2, :]
                        M = Ms[v % 2]
                        nc.tensor.matmul(o, Xtok[:, 0, 64 * h:64 * h + 64], M[:, i, 0:TOK], start=True, stop=False,
                                         skip_group_check=True)
                        ins = nc.tensor.matmul(o[:, P:TOK], Xtok[:, 1, 64 * h:64 * h + 64], M[:, i, TOK:384],
                                               start=False, stop=True, skip_group_check=True)
                    ins.then_inc(sem("ssd_y"), 1)
            pe.wait_ge(sem("ya_squares"), li + 1)
            for g in range(4):
                for q in range(4):
                    ins = nc.tensor.matmul(bank(g, TOK), mean512[:], xbc[:, 4 * g + q, :], start=(q == 0),
                                           stop=(q == 3))
            ins.then_inc(sem("ya_mean"), 1)
            pe.wait_ge(sem("ya_ready"), li + 1)
            for n in range(4):
                for half in range(2):
                    feature_tile(pe, L_BA + 2 * n + half, r, 4 + n, z[:, 8 * half:8 * half + 8, :], half)
            pe.wait_ge(sem("merged"), li + 1)
            for n in range(4):
                token_tile(pe, L_WOUT + n, r, [bank(2 * t + n // 2, 2, W)[:, n % 2, :] for t in range(TT)], ga)

        def ssd_dve(dve, li, r):
            v = nc.vector
            dt = dts[:, 0]
            dve.wait_ge(sem("acum_mm"), li + 1)
            v.tensor_scalar(nacum, bank(5, TT, 32), -1.0, None, ALU.mult)
            for n in range(8):
                g, t = n // 2, n % 2
                dve.wait_ge(sem("heads_turned"), li * 8 + n + 1)
                v.tensor_tensor(Xtok[:, t, 512 * g:512 * g + 512].rearrange("p (h e) -> p h e", e=64),
                                bank(6 + n % 2, 8, 64),
                                dt[:, t, 8 * g:8 * g + 8].unsqueeze(2).to_broadcast([P, 8, 64]),
                                ALU.mult).then_inc(sem("x_turned_read"), 1)

            def out_of(u):
                dve.wait_ge(sem("ssd_y"), li * 8 + u + 1)
                for i in range(2):
                    f = 2 * u + i
                    v.scalar_tensor_tensor(out=xbc[:, f, :], in0=xbc[:, f, :], scalar=skip_d[:, f:f + 1],
                                           in1=bank(4 + u % 2, 2, TOK)[:, i, :], op0=ALU.mult, op1=ALU.add)
                dve.drain()
                return v.tensor_tensor(z[:, 2 * u:2 * u + 2, :], z[:, 2 * u:2 * u + 2, :],
                                       xbc[:, 2 * u:2 * u + 2, :], ALU.mult)

            for u in range(8):
                g, M, CB = u // 2, Ms[u % 2], CBs[(u // 2) % 2]
                if u % 2 == 0:
                    dve.wait_ge(sem("cb_mm"), li * 4 + g + 1)
                    b = bank(6 + g % 2, 384)
                    v.tensor_tensor(CB[:, 0:P], b[:, 0:P], tri[:, 0:P], ALU.mult)
                    v.tensor_copy(CB[:, P:TOK], b[:, P:TOK])
                    v.tensor_tensor(CB[:, TOK:384], b[:, TOK:384], tri[:, 0:P], ALU.mult)
                dve.wait_ge(sem("sums_mm"), li * 8 + u + 1)
                for i in range(4):
                    h = 4 * u + i
                    s = bank(2 * (u % 2) + i // 2, 2, TOK)[:, i % 2, :]
                    v.tensor_scalar(M[:, i, 0:TOK], s, nacum[:, 0, h:h + 1], 0.0, ALU.add, ALU.min)
                    ins = v.tensor_scalar(M[:, i, TOK:384], s[:, P:TOK], nacum[:, 1, h:h + 1], 0.0, ALU.add,
                                          ALU.min)
                ins.then_inc(sem("exponents"), 1)
                if u:
                    out_of(u - 1)
                dve.wait_ge(sem("decayed"), li * 8 + u + 1)
                v.tensor_tensor(M, M, CB.unsqueeze(1).to_broadcast([P, 4, 384]), ALU.mult).then_inc(
                    sem("m_ready"), 1)
            out_of(7).then_inc(sem("ya_raw"), 1)
            rms = xbc[:, 16:20, :]
            dve.wait_ge(sem("ya_rms"), li + 1)
            v.reciprocal(rms, rms)
            dve.drain()
            for f in range(16):
                ins = v.scalar_tensor_tensor(out=z[:, f, :], in0=z[:, f, :], scalar=col(vec2, V2["norm_g"] + f),
                                             in1=rms[:, f // 4, :], op0=ALU.mult, op1=ALU.mult)
            ins.then_inc(sem("ya_ready"), 1)
            for n in range(4):
                multiplied(dve, L_BA + 2 * n + 1, r)
                t = slice(2 * n, 2 * n + 2)
                v.tensor_tensor(ga[:, t, :], ga[:, t, :], bank(4 + n, 2, TOK), ALU.mult)
                dve.drain()
                ins = v.tensor_tensor(ga[:, t, :], ga[:, t, :], gb[:, t, :], ALU.add)
            ins.then_inc(sem("merged"), 1)

        def ssd_act(act, li):
            for u in range(8):
                act.wait_ge(sem("exponents"), li * 8 + u + 1)
                nc.scalar.activation(Ms[u % 2], Ms[u % 2], ACT.Exp).then_inc(sem("decayed"), 1)
            act.wait_ge(sem("ya_raw"), li + 1)
            nc.scalar.activation(xbc[:, 0:16, :], z, ACT.Square).then_inc(sem("ya_squares"), 1)
            act.wait_ge(sem("ya_mean"), li + 1)
            nc.scalar.activation(xbc[:, 16:20, :], ps[:, 0:4, 0:TOK], ACT.Sqrt, bias=eps).then_inc(
                sem("ya_rms"), 1)

        block = ctx.enter_context(nc.Block())
        FINAL = {1: 2, 2: 3, 3: 3 + 3 * LAYERS}[min(upto, 3)]


        @block.sync
        def _(sp):
            sp_program(sp)
            sp.wait_ge(sem("x_new"), FINAL)
            sp.dma_start(out.rearrange("a (t p) d -> p (a t) d", p=P), x[:]).then_inc(sem("stored"), 16)
            sp.wait_ge(sem("stored"), 16)

        @block.gpsimd
        def _(pool):
            constants(pool)
            small_loads_1(pool)
            if upto >= 2:
                moe_small_loads(pool)
            if upto >= 3:
                with pool.Fori(0, LAYERS) as li:
                    layer_loads(pool, li)

        @block.scalar
        def _(act):
            mod_act(act)
            pre_norm_act(act, 0)
            win1_act(act)
            lam_act(act)
            attention_act(act)
            gla_act(act)
            lru_act(act)
            if upto >= 2:
                pre_norm_act(act, 1)
                router_act(act)
                extra = experts_act(act)
            if upto >= 3:
                with act.Fori(0, LAYERS) as li:
                    r = li * ROUNDS + extra
                    layer_start_act(act, li)
                    pre_norm_act(act, li * 3 + 2)
                    ffn_act(act, L_FFN1, r, li * 2)
                    act.wait_ge(sem("tile_mm"), (li * 2 + 1) * NT + 1)
                    post_norm_act(act)
                    pre_norm_act(act, li * 3 + 3)
                    s5_params_act(act, li)
                    s5_act(act, li, r)
                    proj_act(act, li, r)
                    ssd_act(act, li)
                    multiplied(act, L_FFN2 - 1, r)
                    post_norm_act(act)
                    pre_norm_act(act, li * 3 + 4)
                    ffn_act(act, L_FFN2, r, li * 2 + 1)
                    act.wait_ge(sem("tile_mm"), (li * 2 + 2) * NT + 1)
                    post_norm_act(act)

        @block.vector
        def _(dve):
            mod_dve(dve)
            glmask_dve(dve)
            dve.wait_ge(sem("x_in"), 16)
            nc.vector.memset(small[:, 252:253], 0.0).then_inc(sem("x_new"), 1)
            pre_norm_dve(dve, 0)
            pre_norm_out(dve, 0, lambda k: col(modc, 8 + k), lambda k: col(modc, k))
            win1_dve(dve)
            qk_norm_dve(dve)
            attention_dve(dve)
            gla_dve(dve)
            lru_dve(dve)
            multiplied(dve, T_WOUT1 + 3, 0)
            wout1_dve(dve, 0)
            if upto >= 2:
                pre_norm_dve(dve, 1)
                pre_norm_out(dve, 1, lambda k: col(modc, 24 + k), lambda k: col(modc, 16 + k))
                router_dve(dve)
                extra = experts_dve(dve)
                dve.wait_ge(sem("moe_out"), 1)
                wout1_dve(dve, 1)
            if upto >= 3:
                with dve.Fori(0, LAYERS) as li:
                    r = li * ROUNDS + extra

                    def gains(name):
                        return lambda k: col(vec2, V2[name] + k)
                    layer_start_dve(dve, li)
                    pre_norm_dve(dve, li * 3 + 2)
                    pre_norm_out(dve, li * 3 + 2, gains("ffn1_pre_g"), done="ffn_u")
                    ffn_dve(dve, L_FFN1, r, li * 2)
                    post_norm_dve(dve, li * 3, 0.5)
                    pre_norm_dve(dve, li * 3 + 3)
                    pre_norm_out(dve, li * 3 + 3, gains("mix_pre_g"))
                    u5_dve(dve, r)
                    s5_params_dve(dve, li)
                    s5_dve(dve, li)
                    proj_dve(dve, li, r)
                    ssd_dve(dve, li, r)
                    post_norm_dve(dve, li * 3 + 1, 1.0)
                    pre_norm_dve(dve, li * 3 + 4)
                    pre_norm_out(dve, li * 3 + 4, gains("ffn2_pre_g"), done="ffn_u")
                    ffn_dve(dve, L_FFN2, r, li * 2 + 1)
                    post_norm_dve(dve, li * 3 + 2, 0.5)

        @block.tensor
        def _(pe):
            mod_pe(pe)
            pre_norm_pe(pe, 0)
            win1_pe(pe)
            qk_norm_pe(pe)
            attention_pe(pe)
            oa_mean_pe(pe)
            gla_pe(pe)
            lru_pe(pe)
            wout1_pe(pe)
            if upto >= 2:
                pre_norm_pe(pe, 1)
                router_pe(pe)
                extra = experts_pe(pe)
            if upto >= 3:
                with pe.Fori(0, LAYERS) as li:
                    r = li * ROUNDS + extra
                    layer_start_pe(pe, li)
                    pre_norm_pe(pe, li * 3 + 2)
                    ffn_pe(pe, L_FFN1, r, li * 2)
                    pre_norm_pe(pe, li * 3 + 3)
                    pe.wait_ge(sem("u_ready"), li + 3)
                    u5_pe(pe, r)
                    s5_turn_pe(pe, li)
                    s5_pe(pe, li, r)
                    proj_pe(pe, li, r)
                    ssd_pe(pe, li, r)
                    pre_norm_pe(pe, li * 3 + 4)
                    ffn_pe(pe, L_FFN2, r, li * 2 + 1)
                    for n in range(NPAD):
                        landed(pe, L_PAD + n, r)
                        multiplied(pe, L_PAD + n - 1, r)
                        pe.sem_inc(w_used, 1)


def kernel(**inputs):
    import numpy as np
    import concourse.bacc as bacc
    from concourse.bass_utils import run_bass_kernel_spmd

    nc = bacc.Bacc("TRN2", target_bir_lowering=False, num_devices=1)
    arrays, args = {}, {}
    for name, value in inputs.items():
        v = np.ascontiguousarray(value)
        arrays[f"in_{name}"] = v
        args[name] = nc.dram_tensor(f"in_{name}", v.shape, mybir.dt.from_np(v.dtype), kind="ExternalInput").ap()
    out = nc.dram_tensor("out_0", (1, TOK, D), F32, kind="ExternalOutput").ap()
    build(nc, args, out)
    result = run_bass_kernel_spmd(nc, [arrays], core_ids=[0])
    return result.results[0]["out_0"]
```
